# Optimizing a Trainium2 kernel written in Bass

```python
import jax, jax.numpy as jnp
from jax import lax
import numpy as np
import math

D_MODEL = 1024
BATCH = 1
SEQ = 256
DEPTH = 1

SB_HEADS = 8
SB_HEAD_DIM = 64
SB_WIDTH = SB_HEADS * SB_HEAD_DIM
SB_BLOCK = 128
POOL_WINDOWS = (2, 4, 8, 16)
POOL_GROUPS = 4
POOL_GROUP_DIM = 64
POOL_WIDTH = POOL_GROUPS * POOL_GROUP_DIM
GM_GROUPS = 4
GM_GROUP_DIM = 64
GM_WIDTH = GM_GROUPS * GM_GROUP_DIM
GM_CHUNK = 128
N_BRANCH = 3
D_FF = 4 * D_MODEL
RMS_EPS = 1e-6
IN_SIZES = (SB_WIDTH, SB_WIDTH, SB_WIDTH, POOL_WIDTH, GM_WIDTH, GM_WIDTH, N_BRANCH * D_MODEL)
D_IN = sum(IN_SIZES)
IN_SPLITS = tuple(int(s) for s in np.cumsum(IN_SIZES)[:-1])


def rms_norm(x, gain):
    xf = x.astype(jnp.float32)
    y = xf * lax.rsqrt(jnp.mean(xf * xf, axis=-1, keepdims=True) + RMS_EPS)
    return (y * gain.astype(jnp.float32)).astype(x.dtype)

def stick_breaking_attention(q, k, v):
    B, S, H, Dh = q.shape
    scale = Dh ** -0.5
    outs = []
    for blk in range(S // SB_BLOCK):
        q0 = blk * SB_BLOCK
        q1 = q0 + SB_BLOCK
        qb = q[:, q0:q1]
        kb = k[:, :q1]
        vb = v[:, :q1]
        z = jnp.einsum('bthd,bshd->bhts', qb, kb).astype(jnp.float32) * scale
        t_idx = q0 + jnp.arange(SB_BLOCK)[:, None]
        s_idx = jnp.arange(q1)[None, :]
        strict = s_idx < t_idx
        log_not = jnp.where(strict, jax.nn.log_sigmoid(-z), 0.0)
        suffix = lax.cumsum(log_not, axis=3, reverse=True) - log_not
        a = jnp.where(strict, jnp.exp(jax.nn.log_sigmoid(z) + suffix), 0.0).astype(v.dtype)
        outs.append(jnp.einsum('bhts,bshd->bthd', a, vb))
    return jnp.concatenate(outs, axis=1)

def multiscale_pool(p, w_pool, pool_scale):
    B, S, _ = p.shape
    pg = p.reshape(B, S, POOL_GROUPS, POOL_GROUP_DIM)
    csum = jnp.cumsum(pg.astype(jnp.float32), axis=1)
    pos = jnp.arange(S, dtype=jnp.float32)
    pooled = []
    for g, w in enumerate(POOL_WINDOWS):
        cg = csum[:, :, g]
        shifted = jnp.pad(cg, ((0, 0), (w, 0), (0, 0)))[:, :S]
        count = jnp.minimum(pos + 1.0, float(w))[None, :, None]
        pooled.append((cg - shifted) / count - pg[:, :, g].astype(jnp.float32))
    pooled = jnp.stack(pooled, axis=2).astype(p.dtype)
    mixed = jnp.einsum('bsgc,gcd->bsgd', pooled, w_pool)
    return mixed.reshape(B, S, POOL_WIDTH) * pool_scale

def chunked_spatial_gating(u, v, gm_gain, w_spatial, b_spatial):
    B, S, _ = u.shape
    u = jax.nn.gelu(u)
    v = rms_norm(jax.nn.gelu(v), gm_gain)
    n_chunks = S // GM_CHUNK
    vc = v.reshape(B, n_chunks, GM_CHUNK, GM_GROUPS, GM_GROUP_DIM)
    causal = jnp.tril(jnp.ones((GM_CHUNK, GM_CHUNK), dtype=bool))
    ws = jnp.where(causal[None], w_spatial, 0.0).astype(v.dtype)
    mixed = jnp.einsum('gtp,bnpgc->bntgc', ws, vc) + b_spatial.T[:, :, None]
    return u * mixed.reshape(B, S, GM_WIDTH)

def first_inputs(seed: int = 0) -> dict:
    key = jax.random.key(seed)
    ks = jax.random.split(key, 18)

    def nrm(k, shape, scale):
        return jax.random.normal(k, shape, jnp.float32) * scale

    def gain(k, shape):
        return 1.0 + 0.05 * jax.random.normal(k, shape, jnp.float32)

    return {
        "x": nrm(ks[0], (BATCH, SEQ, D_MODEL), 1.0),
        "w_in": nrm(ks[1], (DEPTH, D_MODEL, D_IN), D_MODEL ** -0.5),
        "w_pool": nrm(ks[2], (DEPTH, POOL_GROUPS, POOL_GROUP_DIM, POOL_GROUP_DIM), POOL_GROUP_DIM ** -0.5),
        "pool_scale": gain(ks[3], (DEPTH, POOL_WIDTH)),
        "gm_gain": gain(ks[4], (DEPTH, GM_WIDTH)),
        "w_spatial": nrm(ks[5], (DEPTH, GM_GROUPS, GM_CHUNK, GM_CHUNK), GM_CHUNK ** -0.5),
        "b_spatial": gain(ks[6], (DEPTH, GM_GROUPS, GM_CHUNK)),
        "w_br_sb": nrm(ks[7], (DEPTH, SB_WIDTH, D_MODEL), SB_WIDTH ** -0.5),
        "w_br_pool": nrm(ks[8], (DEPTH, POOL_WIDTH, D_MODEL), POOL_WIDTH ** -0.5),
        "w_br_gm": nrm(ks[9], (DEPTH, GM_WIDTH, D_MODEL), GM_WIDTH ** -0.5),
        "w_out": nrm(ks[10], (DEPTH, D_MODEL, D_MODEL), D_MODEL ** -0.5),
        "g_mix_pre": gain(ks[11], (DEPTH, D_MODEL)),
        "g_mix_post": gain(ks[12], (DEPTH, D_MODEL)),
        "g_ff_pre": gain(ks[13], (DEPTH, D_MODEL)),
        "g_ff_post": gain(ks[14], (DEPTH, D_MODEL)),
        "w_ff_in": nrm(ks[15], (DEPTH, D_MODEL, D_FF), D_MODEL ** -0.5),
        "w_ff_out": nrm(ks[16], (DEPTH, D_FF, D_MODEL), D_FF ** -0.5),
    }

def first_block(x, w_in, w_pool, pool_scale, gm_gain, w_spatial, b_spatial, w_br_sb, w_br_pool,
              w_br_gm, w_out, g_mix_pre, g_mix_post, g_ff_pre, g_ff_post, w_ff_in, w_ff_out):
    B, S, D = x.shape
    for l in range(DEPTH):
        h = rms_norm(x, g_mix_pre[l])
        proj = h @ w_in[l]
        q, k, v, p_in, gm_u, gm_v, gate_in = jnp.split(proj, IN_SPLITS, axis=-1)
        o_sb = stick_breaking_attention(q.reshape(B, S, SB_HEADS, SB_HEAD_DIM),
                                        k.reshape(B, S, SB_HEADS, SB_HEAD_DIM),
                                        v.reshape(B, S, SB_HEADS, SB_HEAD_DIM)).reshape(B, S, SB_WIDTH)
        o_pool = multiscale_pool(p_in, w_pool[l], pool_scale[l])
        o_gm = chunked_spatial_gating(gm_u, gm_v, gm_gain[l], w_spatial[l], b_spatial[l])
        gates = jax.nn.sigmoid(gate_in.reshape(B, S, N_BRANCH, D))
        merged = (gates[:, :, 0] * (o_sb @ w_br_sb[l])
                  + gates[:, :, 1] * (o_pool @ w_br_pool[l])
                  + gates[:, :, 2] * (o_gm @ w_br_gm[l]))
        x = x + rms_norm(merged @ w_out[l], g_mix_post[l])
        h = rms_norm(x, g_ff_pre[l])
        ff = jnp.square(jax.nn.relu(h @ w_ff_in[l])) @ w_ff_out[l]
        x = x + rms_norm(ff, g_ff_post[l])
    return x


DEPTH_2 = 2

N_MIXERS = 2
N_CONV_LAYERS = (DEPTH_2 + 1) // 2
N_ATTN_LAYERS = DEPTH_2 // 2
N_HEADS = 16
HEAD_DIM = D_MODEL // N_HEADS
MOBA_BLOCK = 256
MOBA_TOP_K = 3
Q_CHUNK = 64
CONV_WIDTH = 31
D_FF_2 = 4 * D_MODEL
N_MOD = 6
EPS = 1e-6


def rms_norm_2(x, g):
    xf = x.astype(jnp.float32)
    y = xf * lax.rsqrt(jnp.mean(xf * xf, axis=-1, keepdims=True) + EPS)
    return (y * g.astype(jnp.float32)).astype(x.dtype)

def layer_norm(x, g, b):
    xf = x.astype(jnp.float32)
    mu = jnp.mean(xf, axis=-1, keepdims=True)
    xc = xf - mu
    var = jnp.mean(xc * xc, axis=-1, keepdims=True)
    y = xc * lax.rsqrt(var + EPS) * g.astype(jnp.float32) + b.astype(jnp.float32)
    return y.astype(x.dtype)

def alibi_slopes(n_heads):
    return jnp.asarray(2.0 ** (-8.0 * np.arange(1, n_heads + 1) / n_heads), dtype=jnp.float32)

def conformer_conv(h, w_in, b_in, dw, dw_b, ln_g, ln_b, w_out, b_out):
    d = h.shape[-1]
    a, g = jnp.split(h @ w_in + b_in, 2, axis=-1)
    u = a * jax.nn.sigmoid(g)
    u = lax.conv_general_dilated(
        u, dw[:, None, :].astype(u.dtype), window_strides=(1,),
        padding=((CONV_WIDTH - 1, 0),),
        dimension_numbers=('NWC', 'WIO', 'NWC'),
        feature_group_count=d) + dw_b
    u = jax.nn.silu(layer_norm(u, ln_g, ln_b))
    return u @ w_out + b_out

def moba_attention(h, w_qkv, q_norm_g, k_norm_g, w_o):
    B, S, D = h.shape
    H, DH = N_HEADS, HEAD_DIM
    q, k, v = jnp.split(h @ w_qkv, 3, axis=-1)
    to_heads = lambda z: z.reshape(B, S, H, DH).transpose(0, 2, 1, 3)
    q = rms_norm_2(to_heads(q), q_norm_g)
    k = rms_norm_2(to_heads(k), k_norm_g)
    v = to_heads(v)

    nb = -(-S // MOBA_BLOCK)
    s_pad = nb * MOBA_BLOCK
    pad = ((0, 0), (0, 0), (0, s_pad - S), (0, 0))
    q, k, v = jnp.pad(q, pad), jnp.pad(k, pad), jnp.pad(v, pad)
    k_blocks = k.reshape(B, H, nb, MOBA_BLOCK, DH)
    v_blocks = v.reshape(B, H, nb, MOBA_BLOCK, DH)
    k_mean = jnp.mean(k_blocks.astype(jnp.float32), axis=3)

    topk = min(MOBA_TOP_K, nb)
    slopes = alibi_slopes(H)
    scale = 1.0 / math.sqrt(DH)
    n_chunks = s_pad // Q_CHUNK
    q_chunks = q.reshape(B, H, n_chunks, Q_CHUNK, DH).transpose(2, 0, 1, 3, 4)
    bi = jnp.arange(B)[:, None, None, None]
    hi = jnp.arange(H)[None, :, None, None]
    blk_ids = jnp.arange(nb)
    in_block = jnp.arange(MOBA_BLOCK)

    def chunk_fn(args):
        qc, ci = args
        t = ci * Q_CHUNK + jnp.arange(Q_CHUNK)
        blk = (ci * Q_CHUNK) // MOBA_BLOCK
        gate = jnp.einsum('bhqd,bhnd->bhqn', qc.astype(jnp.float32), k_mean)
        gate = jnp.where(blk_ids < blk, gate, -jnp.inf)
        gate_val, sel = lax.top_k(gate, topk)
        sel_ok = jnp.isfinite(gate_val)
        k_sel = k_blocks[bi, hi, sel]
        v_sel = v_blocks[bi, hi, sel]
        s_sel = jnp.einsum('bhqd,bhqcsd->bhqcs', qc, k_sel).astype(jnp.float32) * scale
        pos_sel = sel[..., None] * MOBA_BLOCK + in_block
        dist_sel = t[None, None, :, None, None] - pos_sel
        s_sel = s_sel - slopes[None, :, None, None, None] * dist_sel
        s_sel = jnp.where(sel_ok[..., None], s_sel, -jnp.inf)
        k_own = lax.dynamic_slice_in_dim(k, blk * MOBA_BLOCK, MOBA_BLOCK, axis=2)
        v_own = lax.dynamic_slice_in_dim(v, blk * MOBA_BLOCK, MOBA_BLOCK, axis=2)
        s_own = jnp.einsum('bhqd,bhsd->bhqs', qc, k_own).astype(jnp.float32) * scale
        dist_own = t[:, None] - (blk * MOBA_BLOCK + in_block)[None, :]
        s_own = jnp.where(dist_own >= 0, s_own - slopes[None, :, None, None] * dist_own, -jnp.inf)
        scores = jnp.concatenate([s_sel.reshape(B, H, Q_CHUNK, topk * MOBA_BLOCK), s_own], axis=-1)
        p = jax.nn.softmax(scores, axis=-1)
        p_sel = p[..., :topk * MOBA_BLOCK].reshape(B, H, Q_CHUNK, topk, MOBA_BLOCK).astype(v.dtype)
        p_own = p[..., topk * MOBA_BLOCK:].astype(v.dtype)
        return (jnp.einsum('bhqcs,bhqcsd->bhqd', p_sel, v_sel)
                + jnp.einsum('bhqs,bhsd->bhqd', p_own, v_own))

    out = lax.map(chunk_fn, (q_chunks, jnp.arange(n_chunks)))
    out = out.transpose(1, 2, 0, 3, 4).reshape(B, H, s_pad, DH)[:, :, :S]
    out = out.transpose(0, 2, 1, 3).reshape(B, S, D)
    return out @ w_o

def second_inputs(seed: int = 0) -> dict:
    key = jax.random.key(seed)
    ks = iter(jax.random.split(key, 32))
    nrm = lambda shape, s: jax.random.normal(next(ks), shape, jnp.float32) * s
    D = D_MODEL
    return {
        "x": nrm((BATCH, SEQ, D), 1.0),
        "c": nrm((BATCH, D), 1.0),
        "ada_w": nrm((DEPTH_2, D, N_MOD * D), 0.5 * D ** -0.5),
        "ada_b": nrm((DEPTH_2, N_MOD * D), 0.02),
        "mix_norm_g": 1.0 + nrm((DEPTH_2, D), 0.1),
        "mlp_norm_g": 1.0 + nrm((DEPTH_2, D), 0.1),
        "conv_w_in": nrm((N_CONV_LAYERS, D, 2 * D), D ** -0.5),
        "conv_b_in": nrm((N_CONV_LAYERS, 2 * D), 0.02),
        "conv_dw": nrm((N_CONV_LAYERS, CONV_WIDTH, D), CONV_WIDTH ** -0.5),
        "conv_dw_b": nrm((N_CONV_LAYERS, D), 0.02),
        "conv_ln_g": 1.0 + nrm((N_CONV_LAYERS, D), 0.1),
        "conv_ln_b": nrm((N_CONV_LAYERS, D), 0.02),
        "conv_w_out": nrm((N_CONV_LAYERS, D, D), D ** -0.5),
        "conv_b_out": nrm((N_CONV_LAYERS, D), 0.02),
        "attn_w_qkv": nrm((N_ATTN_LAYERS, D, 3 * D), D ** -0.5),
        "attn_q_norm_g": 1.0 + nrm((N_ATTN_LAYERS, HEAD_DIM), 0.1),
        "attn_k_norm_g": 1.0 + nrm((N_ATTN_LAYERS, HEAD_DIM), 0.1),
        "attn_w_o": nrm((N_ATTN_LAYERS, D, D), D ** -0.5),
        "mlp_w1": nrm((DEPTH_2, D, D_FF_2), D ** -0.5),
        "mlp_w2": nrm((DEPTH_2, D_FF_2, D), D_FF_2 ** -0.5),
    }

def second_block(x, c, ada_w, ada_b, mix_norm_g, mlp_norm_g,
              conv_w_in, conv_b_in, conv_dw, conv_dw_b, conv_ln_g, conv_ln_b, conv_w_out, conv_b_out,
              attn_w_qkv, attn_q_norm_g, attn_k_norm_g, attn_w_o,
              mlp_w1, mlp_w2):
    cond = jax.nn.silu(c)
    for i in range(DEPTH_2):
        mod = cond @ ada_w[i] + ada_b[i]
        sh1, sc1, g1, sh2, sc2, g2 = [m[:, None, :] for m in jnp.split(mod, N_MOD, axis=-1)]
        h = rms_norm_2(x, mix_norm_g[i]) * (1.0 + sc1) + sh1
        j = i // N_MIXERS
        if i % N_MIXERS == 0:
            y = conformer_conv(h, conv_w_in[j], conv_b_in[j], conv_dw[j], conv_dw_b[j],
                               conv_ln_g[j], conv_ln_b[j], conv_w_out[j], conv_b_out[j])
        else:
            y = moba_attention(h, attn_w_qkv[j], attn_q_norm_g[j], attn_k_norm_g[j], attn_w_o[j])
        x = x + g1 * y
        h = rms_norm_2(x, mlp_norm_g[i]) * (1.0 + sc2) + sh2
        x = x + g2 * (jnp.square(jax.nn.relu(h @ mlp_w1[i])) @ mlp_w2[i])
    return x


def setup_inputs(seed=0):
    out = dict(first_inputs(seed))
    for name, value in second_inputs(seed + 1).items():
        if name != "x":
            out[name + "_2"] = value
    return out


def reference(
    x, w_in, w_pool, pool_scale, gm_gain, w_spatial, b_spatial, w_br_sb, w_br_pool, w_br_gm,
    w_out, g_mix_pre, g_mix_post, g_ff_pre, g_ff_post, w_ff_in, w_ff_out, c_2, ada_w_2, ada_b_2,
    mix_norm_g_2, mlp_norm_g_2, conv_w_in_2, conv_b_in_2, conv_dw_2, conv_dw_b_2, conv_ln_g_2,
    conv_ln_b_2, conv_w_out_2, conv_b_out_2, attn_w_qkv_2, attn_q_norm_g_2, attn_k_norm_g_2,
    attn_w_o_2, mlp_w1_2, mlp_w2_2,
):
    x = first_block(
        x, w_in, w_pool, pool_scale, gm_gain, w_spatial, b_spatial, w_br_sb, w_br_pool, w_br_gm,
        w_out, g_mix_pre, g_mix_post, g_ff_pre, g_ff_post, w_ff_in, w_ff_out,
    )
    return second_block(
        x, c_2, ada_w_2, ada_b_2, mix_norm_g_2, mlp_norm_g_2, conv_w_in_2, conv_b_in_2,
        conv_dw_2, conv_dw_b_2, conv_ln_g_2, conv_ln_b_2, conv_w_out_2, conv_b_out_2,
        attn_w_qkv_2, attn_q_norm_g_2, attn_k_norm_g_2, attn_w_o_2, mlp_w1_2, mlp_w2_2,
    )


_drawn_inputs = setup_inputs


def setup_inputs(seed=0):
    import zlib

    import numpy as np

    out = dict(_drawn_inputs(seed))
    spreads = {}
    factors = {'gm_gain': 4.664,
     'b_spatial': 3.01,
     'mix_norm_g_2': 3.805,
     'conv_b_in_2': 8.0,
     'conv_dw_b_2': 8.0,
     'conv_ln_g_2': 4.692,
     'conv_ln_b_2': 8.0,
     'conv_b_out_2': 8.0,
     'attn_q_norm_g_2': 8.0,
     'attn_k_norm_g_2': 8.0}
    for name, (base, spread) in spreads.items():
        noise = np.random.default_rng([zlib.crc32(name.encode()), seed]).standard_normal(out[name].shape)
        drawn = base * np.exp(spread * noise) if base else spread * noise
        out[name] = __import__('jax').numpy.asarray(drawn.astype(out[name].dtype))
    for name, factor in factors.items():
        out[name] = (out[name] * factor).astype(out[name].dtype)
    return out
```

```python
from contextlib import ExitStack

import numpy as np

import concourse.bass as bass
from concourse import mybir

ALU = mybir.AluOpType
ACT = mybir.ActivationFunctionType
AX = mybir.AxisListType
F32 = mybir.dt.float32
F32R = mybir.dt.float32r
I32 = mybir.dt.int32

P = 128
SEQ = 256
TT = SEQ // P
D = 1024
KT = D // P
UNIT = 2048
RING = 4
EPS = 1e-6
RSQRT_MAGIC = 1597463007.0
GELU_2C = 2.0 * float(np.sqrt(2.0 / np.pi))
GELU_A = 0.044715
HD = 64
SB_HEADS = 8
AT_HEADS = 16
TAPS = 31
PAD = TAPS - 1
SCALE = HD ** -0.5
NEG = -1e30
FAR = -3e37
WINDOWS = (2, 4, 8, 16)

U_Q, U_K, U_V, U_PU, U_GV, U_GATE = 0, 2, 4, 6, 8, 9
U_BR = 21
U_OUT = 25
U_MLP = (29, 73, 121)
U_CIN, U_COUT = 61, 69
U_QKV, U_WO = 105, 117
N_UNITS = 153

C_ID, C_ONE, C_TRI, C_M01, C_KEEP, C_NEG, C_DIST, C_END = 0, 128, 256, 384, 512, 640, 768, 1152

PARAMS = {}
_at = 0
for _name, _n in (("g_mix_pre", 8), ("g_ff_pre", 8), ("mix_g", 16), ("mlp_g", 16), ("conv_b_in", 16),
                  ("conv_dw_b", 8), ("conv_ln_g", 8), ("conv_ln_b", 8), ("pool_scale", 2), ("c", 8)):
    PARAMS[_name] = (_at, _n)
    _at += _n
N_MISC = _at
PARAMS["ada_b"] = (128, 96)
PARAMS["conv_dw"] = (256, TAPS * KT)
N_PCOL = 256 + TAPS * KT


def shape_constants():
    c = np.zeros((P, C_END), np.float32)
    i = np.arange(P)
    c[:, C_ID:C_ID + P] = np.eye(P)
    c[:, C_ONE:C_ONE + P] = 1.0
    c[:, C_TRI:C_TRI + P] = i[:, None] > i[None, :]
    c[:, C_M01:C_M01 + P] = i[:, None] < i[None, :]
    c[:, C_KEEP:C_KEEP + P] = i[:, None] <= i[None, :]
    c[:, C_NEG:C_NEG + P] = np.where(i[:, None] < i[None, :], 0.0, NEG)
    near = np.where(i[None, :] <= i[:, None], i[None, :] - i[:, None], FAR)
    c[:, C_DIST:C_DIST + P] = near
    c[:, C_DIST + P:C_DIST + 2 * P] = i[None, :] - i[:, None] - P
    c[:, C_DIST + 2 * P:] = near
    inv = np.zeros((P, 2, SEQ), np.float32)
    t = np.arange(SEQ) + 1.0
    for g, w in enumerate(WINDOWS):
        inv[HD * (g % 2):HD * (g % 2) + HD, g // 2] = 1.0 / np.minimum(t, float(w))
    return c, inv.reshape(P, 2 * SEQ)


def build_kernel(nc, x, w_in, w_pool, pool_scale, gm_gain, w_spatial, b_spatial, w_br_sb, w_br_pool,
                 w_br_gm, w_out, g_mix_pre, g_mix_post, g_ff_pre, g_ff_post, w_ff_in, w_ff_out,
                 c_2, ada_w_2, ada_b_2, mix_norm_g_2, mlp_norm_g_2, conv_w_in_2, conv_b_in_2,
                 conv_dw_2, conv_dw_b_2, conv_ln_g_2, conv_ln_b_2, conv_w_out_2, conv_b_out_2,
                 attn_w_qkv_2, attn_q_norm_g_2, attn_k_norm_g_2, attn_w_o_2, mlp_w1_2, mlp_w2_2,
                 consts, inv_count, out):
    ctx = ExitStack()
    with ctx:
        size = [(nc.sbuf_base + 63) // 64 * 64]

        def nbytes(shape):
            return 4 * int(np.prod(shape[1:]))

        def place(name, shape, dt=F32):
            at = size[0]
            size[0] += (nbytes(shape) + 31) // 32 * 32
            return nc.alloc_sbuf_tensor_at(name, shape, dt, offset=at)

        def area(name, n):
            start = size[0]
            size[0] += n

            def at(tile, offset, shape):
                assert offset + nbytes(shape) <= n, (name, tile)
                return nc.alloc_sbuf_tensor_at(tile, shape, F32, offset=start + offset)

            return at

        raw = place("raw", [P, RING, UNIT])
        hi = place("hi", [P, RING, UNIT], F32R)
        lo = place("lo", [P, RING, UNIT], F32R)
        X = place("X", [P, TT, D])
        hTh = place("hTh", [P, KT, SEQ], F32R)
        hTl = place("hTl", [P, KT, SEQ], F32R)
        hidh = place("hidh", [P, 8, SEQ], F32R)
        hidl = place("hidl", [P, 8, SEQ], F32R)
        cst = place("cst", [P, C_END])
        pcol = place("pcol", [P, N_PCOL])
        modT = place("modT", [P, 96])
        cond = place("cond", [P, 16])
        stat = place("stat", [P, 352])
        zero_r = place("zero_r", [P, P], F32R)
        qk_gain = place("qk_gain", [P, 2])
        ada_area = area("ada", 16384)
        row_area = area("rows", 12288)
        acc_area = area("acc", 2048)
        big = area("big", 33792)

        assert size[0] <= nc.sbuf_usable_end
        ada_raw = ada_area("ada_raw", 0, [P, 2, 4, 512])
        ada_acc = acc_area("ada_acc", 0, [P, 512])
        row_a = row_area("row_a", 0, [P, D])
        row_b = row_area("row_b", 4096, [P, D])
        row_c = row_area("row_c", 8192, [P, D])
        xn = big("xn", 0, [P, TT, D])
        junk = big("junk", 8192, [P, D])
        junk2 = big("junk2", 12288, [P, D])
        relu = big("relu", 16384, [P, 4 * SEQ])
        sqr = big("sqr", 20480, [P, 4 * SEQ])
        lo_tmp = big("lo_tmp", 24576, [P, 2, SEQ])
        prow = big("prow", 16384, [P, 4, P])
        wsrow = big("wsrow", 18432, [P, 4, P])
        gate = big("gate", 0, [P, 6, TT, 512])
        qT = big("qT", 24576, [P, 4, SEQ])
        kT = big("kT", 28672, [P, 4, SEQ])
        gm_row = big("gm_row", 20480, [P, SEQ])
        vS = ada_area("vS", 0, [P, TT, 512])
        sbt = ada_area("sbt", 4096, [P, 2, 3, 384])
        gt = ada_area("gt", 4096, [P, 3, 512])
        gv = ada_area("gv", 13312, [P, TT, SEQ])
        wpd = ada_area("wpd", 15360, [P, 2, P])
        wsT = row_area("wsT", 0, [P, 4, P])
        pp = row_area("pp", 2048, [P, 2, 16 + SEQ])
        pa = row_area("pa", 4224, [P, 2, 16 + SEQ])
        pb = row_area("pb", 6400, [P, 2, 16 + SEQ])
        gu = row_area("gu", 8576, [P, 2, SEQ])
        bsp = row_area("bsp", 10624, [P, 2, P])
        inv = acc_area("inv", 0, [P, 2, SEQ])
        u_pad = big("u_pad", 0, [P, KT, PAD + SEQ])
        cacc = big("cacc", 9152, [P, KT, SEQ])
        cxc = big("cxc", 17344, [P, KT, SEQ])
        csg = big("csg", 25536, [P, 2, 2, SEQ])
        cmr = big("cmr", 29632, [P, 2, SEQ])
        cmv = acc_area("cmv", 0, [P, 2, SEQ])
        Qs = big("Qs", 0, [P, TT, D])
        Ks = big("Ks", 8192, [P, TT, D])
        Vs = big("Vs", 16384, [P, TT, D])
        aS = big("aS", 24576, [P, 3, 384])
        aT = big("aT", 29184, [P, 3, 384])
        qT2 = ada_area("qT2", 0, [P, KT, SEQ])
        kT2 = ada_area("kT2", 8192, [P, KT, SEQ])

        ps = ctx.enter_context(nc.psum_tensor("ps", [P, 8, 512], F32))

        ident = cst[:, C_ID:C_ID + P]
        ones = cst[:, C_ONE:C_ONE + P]
        tri = cst[:, C_TRI:C_TRI + P]
        m01 = cst[:, C_M01:C_M01 + P]
        keep = cst[:, C_KEEP:C_KEEP + P]
        neg = cst[:, C_NEG:C_NEG + P]
        dist = cst[:, C_DIST:C_DIST + 3 * P]

        def par(name, j=0, n=1):
            at = PARAMS[name][0] + j
            return pcol[:, at:at + n]

        def sem(name):
            return ctx.enter_context(nc.semaphore(name))

        raw_landed = [sem(f"raw_landed{i}") for i in range(RING)]
        hi_made = sem("hi_made")
        lo_made = sem("lo_made")
        used = sem("used")
        ada_landed = [sem(f"ada_landed{i}") for i in range(2)]
        ada_step = sem("ada_step")
        ada_cols = sem("ada_cols")
        ada_kept = sem("ada_kept")
        x_in = sem("x_in")
        cst_in = sem("cst_in")
        par_in = sem("par_in")
        misc_in = sem("misc_in")
        row_a_in = sem("row_a_in")
        row_b_in = sem("row_b_in")
        row_c_in = sem("row_c_in")
        qk_gain_in = sem("qk_gain_in")
        out_sem = sem("out_sem")
        dve_chain = sem("dve_chain")
        act_chain = sem("act_chain")
        pool_chain = sem("pool_chain")
        par_tr = sem("par_tr")
        par_ok = sem("par_ok")
        cond_sig = sem("cond_sig")
        mod_ok = sem("mod_ok")
        x_ver = sem("x_ver")
        ss_act = sem("ss_act")
        rstd_ok = sem("rstd_ok")
        xn_act = sem("xn_act")
        xn_dve = sem("xn_dve")
        tr_done = sem("tr_done")
        hT_hi = sem("hT_hi")
        hT_lo = sem("hT_lo")
        relu_done = sem("relu_done")
        sq_done = sem("sq_done")
        hid_hi = sem("hid_hi")
        hid_lo = sem("hid_lo")
        row_bc = sem("row_bc")
        row_kept = sem("row_kept")
        qkv_kept = sem("qkv_kept")
        kT_kept = sem("kT_kept")
        p_kept = sem("p_kept")
        gelu_act = sem("gelu_act")
        gelu_dve = sem("gelu_dve")
        gate_kept = sem("gate_kept")
        gate_sig = sem("gate_sig")
        pool_in = sem("pool_in")
        vn_ok = sem("vn_ok")
        mix_done = sem("mix_done")
        z_done = sem("z_done")
        abs_done = sem("abs_done")
        soft_done = sem("soft_done")
        lnot_done = sem("lnot_done")
        sfx_done = sem("sfx_done")
        arg_done = sem("arg_done")
        a_done = sem("a_done")
        av_done = sem("av_done")
        o_val = sem("o_val")
        o_hi = sem("o_hi")
        o_lo = sem("o_lo")
        br_done = sem("br_done")
        merged = sem("merged")
        pad_ok = sem("pad_ok")
        glu_sig = sem("glu_sig")
        u_ok = sem("u_ok")
        conv_ok = sem("conv_ok")
        cs_sum = sem("cs_sum")
        cs_sq = sem("cs_sq")
        cs_xc = sem("cs_xc")
        cs_ln = sem("cs_ln")
        cs_sig = sem("cs_sig")
        cs_y = sem("cs_y")
        qk_kept = sem("qk_kept")
        qk_sq = sem("qk_sq")
        qk_ss = sem("qk_ss")
        qk_n = sem("qk_n")
        qk_tr = sem("qk_tr")
        qk_T = sem("qk_T")
        s_z = sem("s_z")
        s_arg = sem("s_arg")
        s_max = sem("s_max")
        s_exp = sem("s_exp")
        s_p = sem("s_p")
        s_tr = sem("s_tr")
        s_pT = sem("s_pT")
        s_o = sem("s_o")
        ss_post = sem("ss_post")
        consts_ok = sem("consts_ok")
        pool_x = sem("pool_x")


        def split_hi(act, n, slot):
            act.wait_ge(raw_landed[slot], n_landed(n, slot))
            nc.scalar.activation(hi[:, slot], raw[:, slot], ACT.Copy).then_inc(hi_made, 1)

        def n_landed(n, slot):
            return (n - slot) * (16 // RING) + 16

        def split_lo(dve, n, slot):
            dve.wait_ge(hi_made, n + 1)
            nc.vector.tensor_tensor(lo[:, slot], raw[:, slot], hi[:, slot].bitcast(F32),
                                    ALU.subtract).then_inc(lo_made, 1)

        def act_step(act, u, i=None, j=None):
            act.wait_ge(used, u + 1)
            if not isinstance(u, int) or u + RING < N_UNITS:
                split_hi(act, u + RING, slot_of(u, j))

        def dve_step(dve, u, j=None):
            if not isinstance(u, int) or u + RING < N_UNITS:
                split_lo(dve, u + RING, slot_of(u, j))

        def slot_of(u, j):
            return (u if j is None else j) % RING

        def load(sp, n, src, j=None):
            slot = slot_of(n, j)
            if not isinstance(n, int) or n >= RING:
                sp.wait_ge(lo_made, n - (RING - 1))
            dst = raw[:, slot].rearrange("p (k n) -> p k n", k=src.shape[1])
            sp.dma_start(dst, src).then_inc(raw_landed[slot], 16)

        def rows3(w):
            return w.rearrange("(k p) n -> p k n", p=P)

        def unit_w(pe, u, j, act_h, act_l, k0, bank, first, nk=4):
            slot = slot_of(u, j)
            pe.wait_ge(lo_made, u + 1)
            wh = hi[:, slot].rearrange("p (k n) -> p k n", k=nk)
            wl = lo[:, slot].rearrange("p (k n) -> p k n", k=nk)
            for ct in range(UNIT // nk // P):
                o = ps[:, bank + ct // 2, (ct % 2) * SEQ:(ct % 2 + 1) * SEQ]
                c = slice(ct * P, (ct + 1) * P)
                for k in range(nk):
                    mm(pe, o, wh[:, k, c], act_h[:, k0 + k], first and k == 0 and ct % 2 == 0)
                    mm(pe, o, wh[:, k, c], act_l[:, k0 + k])
                    last = mm(pe, o, wl[:, k, c], act_h[:, k0 + k])
            last.then_inc(used, 1)

        def mm(pe, o, lhs, rhs, start=False):
            return nc.tensor.matmul(o, lhs, rhs, start=start, stop=False, skip_group_check=True)

        def unit_x(pe, u, j, act_h, act_l, k0, outs, first, nk=4, cols=512):
            slot = slot_of(u, j)
            pe.wait_ge(lo_made, u + 1)
            wh = hi[:, slot].rearrange("p (k n) -> p k n", k=nk)
            wl = lo[:, slot].rearrange("p (k n) -> p k n", k=nk)
            parts = UNIT // nk // cols
            for tt in range(TT):
                t = slice(tt * P, (tt + 1) * P)
                for c in range(parts):
                    o = outs(tt, c)
                    n = slice(c * cols, (c + 1) * cols)
                    for k in range(nk):
                        mm(pe, o, act_h[:, k0 + k, t], wh[:, k, n], first and k == 0)
                        mm(pe, o, act_l[:, k0 + k, t], wh[:, k, n])
                        last = mm(pe, o, act_h[:, k0 + k, t], wl[:, k, n])
            last.then_inc(used, 1)

        def transposes(pe, fill, b, src, ready):
            for wait, value in ready:
                pe.wait_ge(wait, value)
            for f in range(4):
                if f >= 2:
                    pe.wait_ge(hT_lo, 8 * b + 2 * (f - 2) + 2)
                for k in (2 * f, 2 * f + 1):
                    for tt in range(TT):
                        at = (k % 2) * SEQ + tt * P
                        last = nc.tensor.transpose(ps[:, 6 + f % 2, at:at + P], src(tt, k), ident)
                last.then_inc(tr_done, 1)

        def tr_bank(k):
            return ps[:, 6 + (k // 2) % 2, (k % 2) * SEQ:(k % 2 + 1) * SEQ]

        def hT_act(act, fill, b, scale, bias):
            for k in range(KT):
                act.wait_ge(tr_done, 4 * fill + k // 2 + 1)
                nc.scalar.activation(hTh[:, k], tr_bank(k), ACT.Identity, bias=bias(k),
                                     scale=scale(k)).then_inc(hT_hi, 1)

        def hT_dve(dve, fill, b, scale, bias):
            for k in range(KT):
                if k % 2 == 0:
                    dve.wait_ge(hT_hi, 8 * b + k + 2)
                if scale is None:
                    nc.vector.tensor_tensor(hTl[:, k], tr_bank(k), hTh[:, k].bitcast(F32),
                                            ALU.subtract).then_inc(hT_lo, 1)
                elif bias is None:
                    nc.vector.scalar_tensor_tensor(out=hTl[:, k], in0=tr_bank(k), scalar=scale(k),
                                                   in1=hTh[:, k].bitcast(F32), op0=ALU.mult,
                                                   op1=ALU.subtract).then_inc(hT_lo, 1)
                else:
                    link(dve, nc.vector.tensor_scalar(lo_tmp[:, k % 2], tr_bank(k), scale(k), bias(k),
                                                      ALU.mult, ALU.add))
                    nc.vector.tensor_tensor(hTl[:, k], lo_tmp[:, k % 2], hTh[:, k].bitcast(F32),
                                            ALU.subtract).then_inc(hT_lo, 1)

        links = {"dve": 0, "act": 0, "pool": 0}

        def link(dve, ins):
            links["dve"] += 1
            ins.then_inc(dve_chain, 1)
            dve.wait_ge(dve_chain, links["dve"])

        def link_act(act, ins):
            links["act"] += 1
            ins.then_inc(act_chain, 1)
            act.wait_ge(act_chain, links["act"])

        def link_pool(pool, ins):
            links["pool"] += 1
            ins.then_inc(pool_chain, 1)
            pool.wait_ge(pool_chain, links["pool"])

        def rsqrt(dve, y, ss, v, a, n):
            link(dve, nc.vector.tensor_scalar(v, ss, 1.0 / n, EPS, ALU.mult, ALU.add))
            link(dve, nc.vector.tensor_scalar(y.bitcast(I32), v.bitcast(I32), 1, None,
                                              ALU.logical_shift_right))
            link(dve, nc.vector.tensor_scalar(y.bitcast(I32), y.bitcast(I32), -1.0, RSQRT_MAGIC,
                                              ALU.mult, ALU.add))
            for _ in range(3):
                link(dve, nc.vector.tensor_tensor(a, y, y, ALU.mult))
                link(dve, nc.vector.tensor_tensor(a, a, v, ALU.mult))
                link(dve, nc.vector.tensor_scalar(a, a, -0.5, 1.5, ALU.mult, ALU.add))
                link(dve, nc.vector.tensor_tensor(y, y, a, ALU.mult))

        N_SS, N_Y, N_A, N_V = stat[:, 0:2], stat[:, 8:10], stat[:, 16:18], stat[:, 24:26]

        def norm_act(act, norm, fill, b, free, scale, bias):
            if norm == 0:
                act.wait_ge(x_in, 16)
            else:
                act.wait_ge(x_ver, 2 * norm)
            nc.scalar.activation(junk[:], X[:, 0], ACT.Square, accum_out=stat[:, 0:1]).then_inc(ss_act, 1)
            act.wait_ge(rstd_ok, norm + 1)
            nc.scalar.activation(xn[:, 0], X[:, 0], ACT.Copy, scale=stat[:, 8:9]).then_inc(xn_act, 1)
            if free:
                act.wait_ge(used, free)
            hT_act(act, fill, b, scale, bias)

        def norm_dve(dve, norm, fill, b, scale, bias):
            if norm == 0:
                dve.wait_ge(x_in, 16)
            else:
                dve.wait_ge(x_ver, 2 * norm)
            link(dve, nc.vector.scalar_tensor_tensor(out=junk2[:], in0=X[:, 1], scalar=1.0, in1=X[:, 1],
                                                     op0=ALU.mult, op1=ALU.mult, accum_out=stat[:, 1:2]))
            dve.wait_ge(ss_act, norm + 1)
            rsqrt(dve, N_Y, N_SS, N_V, N_A, D)
            dve_inc(rstd_ok)
            nc.vector.tensor_scalar(xn[:, 1], X[:, 1], stat[:, 9:10], None, ALU.mult).then_inc(xn_dve, 1)
            hT_dve(dve, fill, b, scale, bias)

        def dve_inc(s, n=1):
            nc.vector.sem_inc(s, n)

        def norm_pe(pe, norm, fill, b):
            transposes(pe, fill, b, lambda tt, k: xn[:, tt, k * P:(k + 1) * P],
                       [(xn_act, norm + 1), (xn_dve, norm + 1)])

        def y_bank(tt, c):
            return ps[:, 2 * tt + c]

        def y_full(tt):
            return ps[:, 2 * tt:2 * tt + 2].rearrange("p b n -> p (b n)")

        y_tmp = (junk2, sqr)

        def post_act(act, which, done):
            act.wait_ge(used, done)
            for tt in range(TT):
                nc.scalar.activation((junk, junk2)[tt][:], y_full(tt), ACT.Square,
                                     accum_out=stat[:, tt:tt + 1]).then_inc(ss_post, 1)

        def post_dve(dve, which, row):
            dve.wait_ge(ss_post, 2 * which + 2)
            rsqrt(dve, N_Y, N_SS, N_V, N_A, D)
            for tt in range(TT):
                link(dve, nc.vector.scalar_tensor_tensor(out=y_tmp[tt][:], in0=y_full(tt),
                                                         scalar=stat[:, 8 + tt:9 + tt], in1=row[:],
                                                         op0=ALU.mult, op1=ALU.mult))
                add_x(dve, tt, y_tmp[tt])

        def add_x(dve, tt, y):
            ins = nc.vector.tensor_tensor(X[:, tt], X[:, tt], y[:], ALU.add)
            ins.then_inc(x_ver, 1)

        def gated_dve(dve, done, row):
            dve.wait_ge(used, done)
            for tt in range(TT):
                link(dve, nc.vector.tensor_tensor(y_tmp[tt][:], y_full(tt), row[:], ALU.mult))
                add_x(dve, tt, y_tmp[tt])

        def hid(t, c):
            return t[:, 4 * (c % 2):4 * (c % 2) + 4]

        def mlp_pe(pe, m):
            u0 = U_MLP[m]
            unit_w(pe, u0, None, hTh, hTl, 0, 4, True)
            unit_w(pe, u0 + 1, None, hTh, hTl, 4, 4, False)
            for b in range(4):
                nc.tensor.matmul(ps[:, b, 0:2], zero_r[:], zero_r[:, 0:2], start=True, stop=False,
                                 skip_group_check=True)

            def first(c, u, j, chunk):
                pe.wait_ge(relu_done, chunk)
                unit_w(pe, u, j, hTh, hTl, 0, 4, True)
                unit_w(pe, u + 1, j + 1, hTh, hTl, 4, 4, False)

            def second(par_, u, j, chunk):
                pe.wait_ge(hid_lo, chunk)
                for h in range(2):
                    unit_x(pe, u + h, j + h, hid(hidh, par_), hid(hidl, par_), 0,
                           lambda tt, c, h=h: y_bank(tt, h), False)

            def cols(chunk):
                pe.wait_ge(ada_step, chunk * 8 + 16)
                pe.wait_ge(ada_kept, chunk + 1)
                for q in range(4):
                    last = nc.tensor.matmul(ps[:, 6, q:q + 1], ada_acc[:, q * P:(q + 1) * P],
                                            ones[:, 0:1], start=True, stop=True)
                last.then_inc(ada_cols, 1)

            with nc.tensor.Fori(0, 3, 1) as i:
                n, s = 8 * i + (u0 + 2), u0 + 2
                first(1, n, s, 2 * i + (8 * m + 1))
                if m < 2:
                    cols(4 * i + 12 * m)
                second(0, n + 2, s + 2, 2 * i + (8 * m + 1))
                if m < 2:
                    cols(4 * i + (12 * m + 1))
                first(2, n + 4, s + 4, 2 * i + (8 * m + 2))
                if m < 2:
                    cols(4 * i + (12 * m + 2))
                second(1, n + 6, s + 6, 2 * i + (8 * m + 2))
                if m < 2:
                    cols(4 * i + (12 * m + 3))
            n = u0 + 26
            first(7, n, n, 8 * m + 7)
            second(0, n + 2, n + 2, 8 * m + 7)
            second(1, n + 4, n + 4, 8 * m + 8)

        def mlp_act(act, m):
            u0 = U_MLP[m]

            def relu_of(chunk):
                nc.scalar.activation(relu[:], ps[:, 4:6].rearrange("p b n -> p (b n)"),
                                     ACT.Relu).then_inc(relu_done, 1)

            def hi_of(par_, chunk):
                act.wait_ge(sq_done, chunk + 1)
                nc.scalar.activation(hid(hidh, par_).rearrange("p k n -> p (k n)"), sqr[:],
                                     ACT.Copy).then_inc(hid_hi, 1)

            act_step(act, u0)
            act.wait_ge(used, u0 + 2)
            relu_of(8 * m)
            act_step(act, u0 + 1)
            hi_of(0, 8 * m)

            def body(u, s, js, chunk):
                for j in js:
                    if j % 4 == 1 and j < len(js) - 1:
                        act.wait_ge(used, u + (j + 1))
                        relu_of(chunk + j // 4)
                    act_step(act, u + j, j=s + j)
                    if j % 4 == 1 and j < len(js) - 1:
                        hi_of(1 - j // 4, chunk + j // 4)

            with nc.scalar.Fori(0, 3, 1) as i:
                body(8 * i + (u0 + 2), u0 + 2, range(8), 2 * i + (8 * m + 1))
            body(u0 + 26, u0 + 26, range(6) if m < 2 else range(3), 8 * m + 7)

        def mlp_pool(pool, m):
            def square(chunk, free):
                pool.wait_ge(relu_done, chunk + 1)
                if free:
                    pool.wait_ge(hid_lo, chunk)
                nc.gpsimd.tensor_tensor(sqr[:], relu[:], relu[:], ALU.mult).then_inc(sq_done, 1)

            square(8 * m, m > 0)
            with nc.gpsimd.Fori(1, 8, 1) as c:
                square(c + 8 * m, True)

        def ada_unit(dve, layer, chunk, h):
            dve.wait_ge(ada_landed[h], chunk * 16 + 16)
            for k in range(4):
                step = chunk * 8 + (8 + 4 * h + k)
                w, s = ada_raw[:, h, k], cond[:, 4 * h + k:4 * h + k + 1]
                if h == 0 and k == 0:
                    ins = nc.vector.tensor_scalar(ada_acc[:], w, s, None, ALU.mult)
                else:
                    dve.wait_ge(ada_step, step)
                    ins = nc.vector.scalar_tensor_tensor(out=ada_acc[:], in0=w, scalar=s, in1=ada_acc[:],
                                                         op0=ALU.mult, op1=ALU.add)
                ins.then_inc(ada_step, 1)

        def ada_keep(dve, chunk):
            dve.wait_ge(ada_cols, chunk + 1)
            at = bass.ds(chunk * 4, 4)
            nc.vector.tensor_tensor(modT[:, at], ps[:, 6, 0:4], ada_bT[:, at], ALU.add).then_inc(ada_kept, 1)

        def mlp_dve(dve, m):
            u0 = U_MLP[m]

            def lo_of(par_, chunk):
                dve.wait_ge(hid_hi, chunk + 1)
                nc.vector.tensor_tensor(hid(hidl, par_).rearrange("p k n -> p (k n)"), sqr[:],
                                        hid(hidh, par_).rearrange("p k n -> p (k n)").bitcast(F32),
                                        ALU.subtract).then_inc(hid_lo, 1)

            dve_step(dve, u0)
            dve_step(dve, u0 + 1)
            lo_of(0, 8 * m)

            def body(u, s, js, chunk, ada):
                for j in js:
                    if ada is not None:
                        ada_unit(dve, m, ada + j // 2, j % 2)
                    dve_step(dve, u + j, j=s + j)
                    if j % 4 == 1 and j < len(js) - 1:
                        lo_of(1 - j // 4, chunk + j // 4)
                    if ada is not None and j % 2:
                        ada_keep(dve, ada + j // 2)

            with nc.vector.Fori(0, 3, 1) as i:
                body(8 * i + (u0 + 2), u0 + 2, range(8), 2 * i + (8 * m + 1),
                     4 * i + 12 * m if m < 2 else None)
            body(u0 + 26, u0 + 26, range(6) if m < 2 else range(3), 8 * m + 7, None)

        def mlp_sp(sp, m, w1, w2):
            u0 = U_MLP[m]
            v1, v2 = rows3(w1), rows3(w2)

            def first(n, j, c, h):
                load(sp, n, v1[:, 4 * h:4 * h + 4, bass.ds(c * 512, 512)], j)

            def second(n, j, c, h):
                load(sp, n, v2[:, bass.ds(c * 4, 4), h * 512:h * 512 + 512], j)

            def ada(i, j):
                chunk, h = 4 * i + j // 2, j % 2
                sp.wait_ge(ada_step, (chunk + 12 * m) * 8 + (4 * h + 4))
                src = rows3(ada_w_2[m])[:, 4 * h:4 * h + 4, bass.ds(chunk * 512, 512)]
                sp.dma_start(ada_raw[:, h], src).then_inc(ada_landed[h], 16)

            for h in range(2):
                first(u0 + h, u0 + h, 0, h)
            for h in range(2):
                first(u0 + 2 + h, u0 + 2 + h, 1, h)
            for h in range(2):
                second(u0 + 4 + h, u0 + 4 + h, 0, h)
            with nc.sync.Fori(0, 3, 1) as i:
                n, s = 8 * i + (u0 + 6), u0 + 6
                for j in range(8):
                    c = 2 * i + (2, 1, 3, 2)[j // 2]
                    (first, second)[j // 2 % 2](n + j, s + j, c, j % 2)
                    if m < 2:
                        ada(i, j)
            for h in range(2):
                second(u0 + 30 + h, u0 + 30 + h, 7, h)

        ada_bT = par("ada_b", 0, 96)
        conv_tap = sem("conv_tap")
        qsq = big("qsq", 24576, [P, TT, 512])

        def mod_shift(layer, vec, k):
            return modT[:, (layer * 6 + vec) * 8 + k:(layer * 6 + vec) * 8 + k + 1]

        def mod_scale(layer, vec, k):
            return mod_shift(layer, vec + 1, k)

        PAR_SRC = (("g_mix_pre", g_mix_pre), ("g_ff_pre", g_ff_pre), ("mix_g", mix_norm_g_2),
                   ("mlp_g", mlp_norm_g_2), ("conv_b_in", conv_b_in_2), ("conv_dw_b", conv_dw_b_2),
                   ("conv_ln_g", conv_ln_g_2), ("conv_ln_b", conv_ln_b_2), ("pool_scale", pool_scale),
                   ("c", c_2), ("ada_b", ada_b_2), ("conv_dw", conv_dw_2))
        N_PAR_DMAS = len(PAR_SRC) + 2
        N_MISC_DMAS = 10

        def conv_out_part(dve, k):
            dve.wait_ge(cs_sig, k + 1)
            nc.vector.scalar_tensor_tensor(out=cxc[:, k], in0=cxc[:, k], scalar=par("conv_ln_b", k),
                                           in1=csg[:, k % 2, 0], op0=ALU.add, op1=ALU.mult).then_inc(cs_y, 1)
            dve.wait_ge(hT_hi, 32 + k + 1)
            nc.vector.tensor_tensor(hTl[:, k], cxc[:, k], hTh[:, k].bitcast(F32),
                                    ALU.subtract).then_inc(hT_lo, 1)

        def chunk_bank(g):
            return 2 * (g % 2)

        def pair(bank):
            return ps[:, bank:bank + 2]

        def row(v, n=D):
            return v.partition_broadcast(P)

        block = ctx.enter_context(nc.Block())

        @block.sync
        def _(sp):
            sp.dma_start(X[:], x.rearrange("a (t p) d -> p (a t) d", p=P)).then_inc(x_in, 16)
            sp.dma_start(cst[:], consts).then_inc(cst_in, 16)
            win = rows3(w_in[0])
            for c in range(4):
                for h in range(2):
                    load(sp, 2 * c + h, win[:, 4 * h:4 * h + 4, 512 * c:512 * c + 512])
            load(sp, U_GV, win[:, :, 2048:2304])
            for c in range(6):
                for h in range(2):
                    n = 2304 + 512 * c
                    load(sp, U_GATE + 2 * c + h, win[:, 4 * h:4 * h + 4, n:n + 512])
            for c in range(2):
                load(sp, U_BR + c, rows3(w_br_sb[0])[:, :, 512 * c:512 * c + 512])
            load(sp, U_BR + 2, rows3(w_br_pool[0]))
            load(sp, U_BR + 3, rows3(w_br_gm[0]))

            def square(first, w):
                for c in range(2):
                    for h in range(2):
                        load(sp, first + 2 * c + h, rows3(w)[:, 4 * h:4 * h + 4, 512 * c:512 * c + 512])

            square(U_OUT, w_out[0])
            mlp_sp(sp, 0, w_ff_in[0], w_ff_out[0])
            for c in range(4):
                for h in range(2):
                    load(sp, U_CIN + 2 * c + h,
                         rows3(conv_w_in_2[0])[:, :, D * h + SEQ * c:D * h + SEQ * c + SEQ])
            square(U_COUT, conv_w_out_2[0])
            mlp_sp(sp, 1, mlp_w1_2[0], mlp_w2_2[0])
            for c in range(6):
                for h in range(2):
                    load(sp, U_QKV + 2 * c + h,
                         rows3(attn_w_qkv_2[0])[:, 4 * h:4 * h + 4, 512 * c:512 * c + 512])
            square(U_WO, attn_w_o_2[0])
            mlp_sp(sp, 2, mlp_w1_2[1], mlp_w2_2[1])
            for tt in range(TT):
                sp.wait_ge(x_ver, 2 * 5 + tt + 1)
                sp.dma_start(out[0, tt * P:(tt + 1) * P, :], X[:, tt]).then_inc(out_sem, 16)
            sp.wait_ge(out_sem, 32)

        @block.tensor
        def _(pe):
            pe.wait_ge(par_in, 16 * N_PAR_DMAS)
            pe.wait_ge(cst_in, 16)
            for g, (at, n) in enumerate(((0, N_MISC), (128, 96), (256, 124), (380, 124))):
                nc.tensor.transpose(ps[:, 0, at:at + n], prow[0:n, g], ident[0:n, 0:n])
            for g in range(4):
                last = nc.tensor.transpose(ps[:, 1, g * P:(g + 1) * P], wsrow[:, g], ident)
            last.then_inc(par_tr, 1)
            norm_pe(pe, 0, 0, 0)

            pe.wait_ge(hT_lo, 8)
            for c, bank in ((0, 0), (1, 2)):
                unit_w(pe, 2 * c, None, hTh, hTl, 0, bank, True)
                unit_w(pe, 2 * c + 1, None, hTh, hTl, 4, bank, False)
            for h in range(2):
                unit_x(pe, U_V + h, None, hTh, hTl, 4 * h, lambda tt, c: ps[:, 4 + tt], h == 0)
            pe.wait_ge(qkv_kept, 1)
            unit_w(pe, U_PU, None, hTh, hTl, 0, 0, True)
            unit_w(pe, U_PU + 1, None, hTh, hTl, 4, 0, False)
            pe.wait_ge(kT_kept, 1)
            unit_x(pe, U_GV, None, hTh, hTl, 0, lambda tt, c: ps[:, 2, tt * SEQ:(tt + 1) * SEQ],
                   True, nk=8, cols=SEQ)

            def scores(h):
                if h == 0:
                    pe.wait_ge(qkv_kept, 2)
                if h >= 2:
                    pe.wait_ge(arg_done, h - 1)
                r = slice(HD * (h % 2), HD * (h % 2) + HD)
                k = h // 2
                nc.tensor.matmul(ps[:, 4 + h % 2, 0:SEQ], kT[r, k, 0:P], qT[r, k, :], start=True,
                                 stop=False, skip_group_check=True)
                nc.tensor.matmul(ps[:, 4 + h % 2, SEQ:384], kT[r, k, P:SEQ], qT[r, k, P:SEQ],
                                 start=False, stop=False, skip_group_check=True).then_inc(z_done, 1)

            def suffix(h):
                pe.wait_ge(lnot_done, h + 1)
                if h >= 1:
                    pe.wait_ge(arg_done, h)
                t = sbt[:, h % 2, 1]
                mm(pe, ps[:, 6, 0:SEQ], tri, t[:, 0:SEQ], True)
                mm(pe, ps[:, 6, P:SEQ], ones, t[:, SEQ:384])
                mm(pe, ps[:, 6, SEQ:384], tri, t[:, SEQ:384]).then_inc(sfx_done, 1)

            def values(h):
                pe.wait_ge(a_done, h + 1)
                if h >= 2 and h % 2 == 0:
                    pe.wait_ge(o_lo, h // 2)
                a = sbt[:, h % 2, 2]
                r, at = slice(HD * (h % 2), HD * (h % 2) + HD), (h // 2 % 2) * SEQ
                v = slice(h * HD, h * HD + HD)
                mm(pe, ps[r, 7, at:at + SEQ], vS[:, 0, v], a[:, 0:SEQ], True)
                mm(pe, ps[r, 7, at + P:at + SEQ], vS[:, 1, v], a[:, SEQ:384]).then_inc(av_done, 1)

            for s in range(12):
                g = s // 2
                bank = chunk_bank(g)
                if s == 0:
                    pe.wait_ge(p_kept, 1)
                    pe.wait_ge(gelu_dve, 2)
                elif s == 2:
                    pe.wait_ge(gelu_dve, 4)
                elif s % 2 == 0:
                    pe.wait_ge(gate_kept, g - 1)
                unit_x(pe, U_GATE + s, None, hTh, hTl, 4 * (s % 2), lambda tt, c: ps[:, bank + tt],
                       s % 2 == 0)
                if s < SB_HEADS:
                    scores(s)
                if 1 <= s < SB_HEADS + 1:
                    suffix(s - 1)
                if 2 <= s < SB_HEADS + 2:
                    values(s - 2)
                if s == 9:
                    pe.wait_ge(pool_in, 1)
                    pe.wait_ge(misc_in, 16 * N_MISC_DMAS)
                    pe.wait_ge(arg_done, SB_HEADS)
                    for i in range(2):
                        last = mm(pe, ps[:, 5, i * SEQ:(i + 1) * SEQ], wpd[:, i], pp[:, i, 16:16 + SEQ], True)
                    last.then_inc(mix_done, 1)
                    pe.wait_ge(vn_ok, 1)
                    for g4 in range(4):
                        r = slice(HD * (g4 % 2), HD * (g4 % 2) + HD)
                        for tt in range(TT):
                            at = (g4 // 2) * SEQ + tt * P
                            last = mm(pe, ps[r, 6, at:at + P], gv[:, tt, g4 * HD:(g4 + 1) * HD],
                                      wsT[:, g4], True)
                    last.then_inc(mix_done, 1)

            pe.wait_ge(gate_kept, 6)
            pe.wait_ge(o_lo, 6)
            for c in range(2):
                unit_x(pe, U_BR + c, None, hidh, hidl, 0, lambda tt, _, c=c: ps[:, 2 * c + tt], True)
            pe.wait_ge(o_lo, 8)
            unit_x(pe, U_BR + 2, None, hidh, hidl, 4, lambda tt, c: ps[:, 4 + 2 * c + tt], True, nk=2)
            pe.wait_ge(br_done, 2)
            unit_x(pe, U_BR + 3, None, hidh, hidl, 6, lambda tt, c: ps[:, 2 * c + tt], True, nk=2)
            transposes(pe, 1, 1, lambda tt, k: gate[:, k // 4, tt, (k % 4) * P:(k % 4 + 1) * P],
                       [(merged, 2)])

            def square(first, b):
                pe.wait_ge(hT_lo, 8 * b + 8)
                for c in range(2):
                    for h in range(2):
                        unit_x(pe, first + 2 * c + h, None, hTh, hTl, 4 * h,
                               lambda tt, _, c=c: y_bank(tt, c), h == 0)

            square(U_OUT, 1)
            norm_pe(pe, 1, 2, 2)
            pe.wait_ge(hT_lo, 24)
            mlp_pe(pe, 0)

            def gate_rows(layer):
                for i, vec in enumerate((2, 5)):
                    if i or layer:
                        pe.wait_ge(row_kept, 2 * layer + i)
                    else:
                        pe.wait_ge(relu_done, 8)
                    pe.wait_ge(ada_kept, 12 * layer + 13)
                    for k in range(KT):
                        m = layer * 48 + vec * 8 + k
                        last = nc.tensor.matmul(ps[:, 4 + k // 4, (k % 4) * P:(k % 4 + 1) * P],
                                                modT[:, m:m + 1].broadcast_to([P, P]), ident,
                                                start=True, stop=True)
                    last.then_inc(row_bc, 1)

            gate_rows(0)
            norm_pe(pe, 2, 3, 3)
            pe.wait_ge(hT_lo, 32)
            for c in range(4):
                if c >= 2:
                    pe.wait_ge(u_ok, 2 * (c - 1))
                for h in range(2):
                    unit_w(pe, U_CIN + 2 * c + h, None, hTh, hTl, 0, chunk_bank(c) + h, True, nk=8)
            pe.wait_ge(conv_ok, 1)
            pe.wait_ge(row_kept, 2)
            for k in range(KT):
                last = mm(pe, ps[:, 4, 0:SEQ], ones, cacc[:, k], k == 0)
            last.then_inc(cs_sum, 1)
            pe.wait_ge(cs_sq, 1)
            for k in range(KT):
                last = mm(pe, ps[:, 5, 0:SEQ], ones, cacc[:, k], k == 0)
            last.then_inc(cs_sum, 1)
            square(U_COUT, 4)
            norm_pe(pe, 3, 4, 5)
            pe.wait_ge(hT_lo, 48)
            mlp_pe(pe, 1)

            gate_rows(1)
            norm_pe(pe, 4, 5, 6)
            pe.wait_ge(hT_lo, 56)

            def qkv(c):
                if c >= 2:
                    pe.wait_ge(qk_kept, c - 1)
                for h in range(2):
                    unit_x(pe, U_QKV + 2 * c + h, None, hTh, hTl, 4 * h,
                           lambda tt, _: ps[:, chunk_bank(c) + tt], h == 0)

            def qk_transposes(src, first):
                pe.wait_ge(qk_n, 1 + first // 4)
                for f in range(4):
                    if first + f >= 2:
                        pe.wait_ge(qk_T, first + f - 1)
                    for k in (2 * f, 2 * f + 1):
                        for tt in range(TT):
                            at = (k % 2) * SEQ + tt * P
                            last = nc.tensor.transpose(ps[:, 6 + f % 2, at:at + P],
                                                       src[:, tt, k * P:(k + 1) * P], ident)
                    last.then_inc(qk_tr, 1)

            for c in range(4):
                qkv(c)
            qk_transposes(Qs, 0)
            qkv(4)
            qk_transposes(Ks, 4)
            qkv(5)
            pe.wait_ge(row_kept, 4)
            for s in range(AT_HEADS + 3):
                if s < AT_HEADS:
                    h, k, r = s, s // 2, slice(HD * (s % 2), HD * (s % 2) + HD)
                    if h == 0:
                        pe.wait_ge(qk_T, 8)
                    if h >= 2:
                        pe.wait_ge(s_arg, h - 1)
                    b = 4 + h % 2
                    mm(pe, ps[:, b, 0:P], qT2[r, k, 0:P], kT2[r, k, 0:P], True)
                    mm(pe, ps[:, b, P:384], qT2[r, k, P:SEQ], kT2[r, k, :]).then_inc(s_z, 1)
                if 2 <= s < AT_HEADS + 2:
                    h = s - 2
                    pe.wait_ge(s_p, h + 1)
                    if h >= 2:
                        pe.wait_ge(s_pT, h - 1)
                    elif h == 0:
                        pe.wait_ge(qk_kept, 6)
                    p, b = aS[:, h % 3], 2 + h % 2
                    for i in range(3):
                        last = nc.tensor.transpose(ps[:, b, i * P:(i + 1) * P], p[:, i * P:(i + 1) * P], ident)
                    last.then_inc(s_tr, 1)
                if s >= 3:
                    h = s - 3
                    pe.wait_ge(s_pT, h + 1)
                    if h >= 4:
                        pe.wait_ge(hT_lo, 56 + h // 2 - 1)
                    r, b, v = slice(HD * (h % 2), HD * (h % 2) + HD), h // 2 % 2, slice(h * HD, h * HD + HD)
                    mm(pe, ps[r, b, 0:SEQ], Vs[:, 0, v], aT[:, h % 3, 0:SEQ], True)
                    mm(pe, ps[r, b, P:SEQ], Vs[:, 1, v], aT[:, h % 3, SEQ:384]).then_inc(s_o, 1)
            square(U_WO, 7)
            norm_pe(pe, 5, 6, 8)
            pe.wait_ge(hT_lo, 72)
            mlp_pe(pe, 2)

        @block.scalar
        def _(act):
            for name, src in PAR_SRC:
                at, n = PARAMS[name]
                if name == "conv_dw":
                    v = src.rearrange("a t (k p) -> (a t k) p", p=P)
                    for g in range(2):
                        act.dma_start(prow[0:124, 2 + g], v[124 * g:124 * g + 124]).then_inc(par_in, 16)
                else:
                    v = src.rearrange("a (k p) -> (a k) p", p=P)
                    act.dma_start(prow[at % P:at % P + n, at // P], v).then_inc(par_in, 16)
            act.dma_start(wsrow[:], w_spatial[0].rearrange("g t p -> t g p")).then_inc(par_in, 16)
            act.dma_start(inv[:], inv_count).then_inc(misc_in, 16)
            act.dma_start(gm_row[:], row(gm_gain[0])).then_inc(misc_in, 16)
            for g in range(4):
                r = slice(HD * (g % 2), HD * (g % 2) + HD)
                act.dma_start(bsp[r, g // 2], b_spatial[0, g].partition_broadcast(HD)).then_inc(misc_in, 16)
            act.wait_ge(pad_ok, 1)
            for g in range(4):
                r = slice(HD * (g % 2), HD * (g % 2) + HD)
                act.dma_start(wpd[r, g // 2, r], w_pool[0, g]).then_inc(misc_in, 16)
            for i, g in enumerate((attn_q_norm_g_2, attn_k_norm_g_2)):
                for half in range(2):
                    act.dma_start(qk_gain[HD * half:HD * half + HD, i:i + 1],
                                  g.rearrange("a d -> d a")).then_inc(qk_gain_in, 16)

            act.wait_ge(x_in, 16)
            act.wait_ge(par_ok, 1)
            for n in range(RING):
                split_hi(act, n, n)
            norm_act(act, 0, 0, 0, None, lambda k: par("g_mix_pre", k), lambda k: 0.0)
            nc.scalar.activation(cond[:, 8:16], par("c", 0, 8), ACT.Sigmoid).then_inc(cond_sig, 1)

            act_step(act, 0)
            act_step(act, 1)
            nc.scalar.activation(qT[:].rearrange("p k n -> p (k n)"),
                                 pair(0).rearrange("p b n -> p (b n)"), ACT.Copy).then_inc(qkv_kept, 1)
            for u in range(2, 6):
                act_step(act, u)
            nc.scalar.activation(vS[:], pair(4), ACT.Copy).then_inc(qkv_kept, 1)
            act_step(act, 6)
            act_step(act, 7)

            def gelu_parts(i, x):
                nc.scalar.activation(gt[:, 0], x, ACT.Square).then_inc(gelu_act, 1)
                act.wait_ge(gelu_dve, 2 * i + 1)
                nc.scalar.activation(gt[:, 1], gt[:, 0], ACT.Sigmoid, scale=GELU_2C).then_inc(gelu_act, 1)

            act.wait_ge(pad_ok, 1)
            nc.scalar.activation(pp[:, :, 16:16 + SEQ], ps[:, 0].rearrange("p (k n) -> p k n", k=2),
                                 ACT.Copy).then_inc(p_kept, 1)
            gelu_parts(0, ps[:, 1])
            act_step(act, 8)
            act.wait_ge(gelu_dve, 2)
            gelu_parts(1, ps[:, 2])
            nc.scalar.preload_act_table_set("natural_log_exp_and_others")

            def softplus(h):
                act.wait_ge(z_done, h + 1)
                if h < 2:
                    act.wait_ge(pool_in, 1)
                else:
                    act.wait_ge(arg_done, h - 1)
                t = sbt[:, h % 2, 0]
                nc.scalar.activation(t, ps[:, 4 + h % 2, 0:384], ACT.Abs, scale=SCALE).then_inc(abs_done, 1)
                act.wait_ge(abs_done, h + 1)
                link_act(act, nc.scalar.activation(t, t, ACT.Exp, scale=-1.0))
                nc.scalar.activation(t, t, ACT.Ln, bias=1.0).then_inc(soft_done, 1)

            def o_split(k, bank, cols):
                nc.scalar.activation(hidh[:, k], ps[:, bank, cols], ACT.Copy).then_inc(o_hi, 1)

            for s in range(12):
                act_step(act, U_GATE + s)
                if s < SB_HEADS:
                    softplus(s)
                if 1 <= s < SB_HEADS + 1:
                    h = s - 1
                    act.wait_ge(arg_done, h + 1)
                    a = sbt[:, h % 2, 2]
                    nc.scalar.activation(a, a, ACT.Exp).then_inc(a_done, 1)
                if s % 2 and s >= 3 and s < SB_HEADS + 2:
                    k = (s - 3) // 2
                    act.wait_ge(av_done, 2 * k + 2)
                    o_split(k, 7, slice((k % 2) * SEQ, (k % 2 + 1) * SEQ))
                if s % 2:
                    g = s // 2
                    nc.scalar.activation(gate[:, g], pair(chunk_bank(g)), ACT.Copy).then_inc(gate_kept, 1)
            act.wait_ge(o_val, 1)
            for k in range(2):
                nc.scalar.activation(hidh[:, 6 + k], gt[:, 0, k * SEQ:(k + 1) * SEQ], ACT.Copy).then_inc(o_hi, 1)
            act.wait_ge(mix_done, 1)
            for k in range(2):
                nc.scalar.activation(hidh[:, 4 + k], ps[:, 5, k * SEQ:(k + 1) * SEQ], ACT.Copy,
                                     scale=par("pool_scale", k)).then_inc(o_hi, 1)
            act.wait_ge(gate_kept, 6)
            for g in range(6):
                nc.scalar.activation(gate[:, g], gate[:, g], ACT.Sigmoid).then_inc(gate_sig, 1)
            for u in range(U_BR, U_OUT):
                act_step(act, u)
            act.wait_ge(used, U_BR)
            hT_act(act, 1, 1, lambda k: 1.0, lambda k: 0.0)
            for u in range(U_OUT, U_OUT + 4):
                act_step(act, u)
            post_act(act, 0, U_OUT + 4)
            norm_act(act, 1, 2, 2, U_OUT + 4, lambda k: par("g_ff_pre", k), lambda k: 0.0)
            mlp_act(act, 0)
            post_act(act, 1, U_MLP[0] + 32)

            def keep_rows(layer):
                for i, dst in enumerate((row_a, row_b)):
                    act.wait_ge(row_bc, 2 * layer + i + 1)
                    if i:
                        act.wait_ge(x_ver, 4 if layer == 0 else 8)
                    nc.scalar.activation(dst[:], pair(4).rearrange("p b n -> p (b n)"),
                                         ACT.Copy).then_inc(row_kept, 1)

            def mod_norm(norm, fill, b, free, layer, vec):
                act.wait_ge(mod_ok, norm - 1)
                norm_act(act, norm, fill, b, free, lambda k: mod_scale(layer, vec, k),
                         lambda k: mod_shift(layer, vec, k))

            keep_rows(0)
            mod_norm(2, 3, 3, U_CIN, 0, 0)
            for c in range(4):
                for h in range(2):
                    act_step(act, U_CIN + 2 * c + h)
                for i in range(2):
                    if c >= 2:
                        act.wait_ge(u_ok, 2 * (c - 2) + i + 1)
                    nc.scalar.activation(csg[:, c % 2, i], ps[:, chunk_bank(c) + 1, i * SEQ:(i + 1) * SEQ],
                                         ACT.Sigmoid, bias=par("conv_b_in", 8 + 2 * c + i)).then_inc(glu_sig, 1)
            act.wait_ge(cs_xc, 1)
            act.wait_ge(cs_sum, 1)
            nc.scalar.activation(cacc[:].rearrange("p k n -> p (k n)"),
                                 cxc[:].rearrange("p k n -> p (k n)"), ACT.Square).then_inc(cs_sq, 1)
            for k in range(KT):
                act.wait_ge(cs_ln, k + 1)
                nc.scalar.activation(csg[:, k % 2, 0], cxc[:, k], ACT.Sigmoid,
                                     bias=par("conv_ln_b", k)).then_inc(cs_sig, 1)
                act.wait_ge(cs_y, k + 1)
                nc.scalar.activation(hTh[:, k], cxc[:, k], ACT.Copy).then_inc(hT_hi, 1)
            for u in range(U_COUT, U_COUT + 4):
                act_step(act, u)
            mod_norm(3, 4, 5, U_COUT + 4, 0, 3)
            mlp_act(act, 1)

            keep_rows(1)
            mod_norm(4, 5, 6, U_QKV, 1, 0)

            def keep_qkv(c):
                for h in range(2):
                    act_step(act, U_QKV + 2 * c + h)
                dst = (Qs, Ks, Vs)[c // 2]
                if c < 4:
                    if c:
                        act.wait_ge(qk_ss, c)
                    nc.scalar.activation(qsq[:], pair(chunk_bank(c)), ACT.Square).then_inc(qk_sq, 1)
                nc.scalar.activation(dst[:, :, (c % 2) * 512:(c % 2 + 1) * 512], pair(chunk_bank(c)),
                                     ACT.Copy).then_inc(qk_kept, 1)

            def keep_T(dst, i, first):
                for f in range(4):
                    act.wait_ge(qk_tr, first + f + 1)
                    nc.scalar.activation(dst[:, 2 * f:2 * f + 2].rearrange("p k n -> p (k n)"),
                                         ps[:, 6 + f % 2], ACT.Copy,
                                         scale=qk_gain[:, i:i + 1]).then_inc(qk_T, 1)

            for c in range(4):
                keep_qkv(c)
            act.wait_ge(qk_gain_in, 64)
            keep_T(qT2, 0, 0)
            keep_qkv(4)
            keep_T(kT2, 1, 4)
            keep_qkv(5)
            for s in range(AT_HEADS + 4):
                if 1 <= s < AT_HEADS + 1:
                    h = s - 1
                    act.wait_ge(s_max, h + 1)
                    for i, c in enumerate((slice(0, P), slice(P, 384))):
                        m = 320 + 2 * (h % 2) + i
                        last = nc.scalar.activation(aS[:, h % 3, c], aS[:, h % 3, c], ACT.Exp, scale=SCALE,
                                                    bias=stat[:, m:m + 1], accum_out=stat[:, m + 8:m + 9])
                        last.then_inc(s_exp, 1)
                if 2 <= s < AT_HEADS + 2:
                    h = s - 2
                    act.wait_ge(s_tr, h + 1)
                    if h >= 3:
                        act.wait_ge(s_o, h - 2)
                    nc.scalar.activation(aT[:, h % 3], ps[:, 2 + h % 2, 0:384], ACT.Copy).then_inc(s_pT, 1)
                if s >= 4 and s % 2 == 0 and s < AT_HEADS + 4:
                    k = (s - 4) // 2
                    act.wait_ge(s_o, 2 * k + 2)
                    nc.scalar.activation(hTh[:, k], ps[:, k % 2, 0:SEQ], ACT.Copy).then_inc(hT_hi, 1)
            for u in range(U_WO, U_WO + 4):
                act_step(act, u)
            mod_norm(5, 6, 8, U_WO + 4, 1, 3)
            mlp_act(act, 2)

        @block.vector
        def _(dve):
            nc.vector.sem_inc(ada_step, 8)
            nc.vector.sem_inc(ada_kept, 1)
            dve.wait_ge(par_tr, 1)
            dve.wait_ge(cst_in, 16)
            for at, n in ((0, N_MISC), (128, 96), (256, 248)):
                link(dve, nc.vector.tensor_copy(pcol[:, at:at + n], ps[:, 0, at:at + n]))
            for g in range(4):
                link(dve, nc.vector.tensor_tensor(wsT[:, g], ps[:, 1, g * P:(g + 1) * P], keep, ALU.mult))
            dve_inc(par_ok)
            norm_dve(dve, 0, 0, 0, lambda k: par("g_mix_pre", k), None)
            for n in range(RING):
                split_lo(dve, n, n)
            dve.wait_ge(cond_sig, 1)
            link(dve, nc.vector.tensor_tensor(cond[:, 0:8], cond[:, 8:16], par("c", 0, 8), ALU.mult))
            for u in range(4):
                dve_step(dve, u)
            dve.wait_ge(used, 4)
            nc.vector.tensor_copy(kT[:].rearrange("p k n -> p (k n)"),
                                  pair(2).rearrange("p b n -> p (b n)")).then_inc(kT_kept, 1)
            for u in range(4, 8):
                dve_step(dve, u)

            def gelu(i, x, dst):
                dve.wait_ge(gelu_act, 2 * i + 1)
                link(dve, nc.vector.tensor_scalar(gt[:, 0], gt[:, 0], GELU_A, 1.0, ALU.mult, ALU.add))
                nc.vector.tensor_tensor(gt[:, 0], gt[:, 0], x, ALU.mult).then_inc(gelu_dve, 1)
                dve.wait_ge(gelu_act, 2 * i + 2)
                nc.vector.tensor_tensor(dst, gt[:, 1], x, ALU.mult).then_inc(gelu_dve, 1)

            gelu(0, ps[:, 1], gu[:].rearrange("p k n -> p (k n)"))
            dve_step(dve, 8)
            gelu(1, ps[:, 2], gv[:].rearrange("p t n -> p (t n)"))
            dve.wait_ge(gelu_dve, 4)
            dve.wait_ge(misc_in, 16 * N_MISC_DMAS)
            for tt in range(TT):
                link(dve, nc.vector.scalar_tensor_tensor(out=gt[:, 2, 0:SEQ], in0=gv[:, tt], scalar=1.0,
                                                         in1=gv[:, tt], op0=ALU.mult, op1=ALU.mult,
                                                         accum_out=stat[:, tt:tt + 1]))
            rsqrt(dve, N_Y, N_SS, N_V, N_A, SEQ)
            for tt in range(TT):
                link(dve, nc.vector.scalar_tensor_tensor(out=gv[:, tt], in0=gv[:, tt],
                                                         scalar=stat[:, 8 + tt:9 + tt], in1=gm_row[:],
                                                         op0=ALU.mult, op1=ALU.mult))
            dve.wait_ge(p_kept, 1)
            src, total = pp, gt[:, 2].rearrange("p (k n) -> p k n", k=2)
            for g, w in enumerate(WINDOWS):
                dst, at = (pa, pb)[g % 2], w - 1
                link(dve, nc.vector.tensor_tensor(dst[:, :, at:], src[:, :, at:],
                                                  src[:, :, at - w // 2:16 + SEQ - w // 2], ALU.add))
                r = slice(HD * (g % 2), HD * (g % 2) + HD)
                link(dve, nc.vector.tensor_tensor(total[r, g // 2], dst[r, g // 2, 16:],
                                                  inv[r, g // 2], ALU.mult))
                src = dst
            nc.vector.tensor_tensor(pp[:, :, 16:], total, pp[:, :, 16:], ALU.subtract).then_inc(pool_in, 1)
            dve_inc(vn_ok)

            def diagonals(t):
                return t.rearrange("p (b n) -> p b n", b=3)[:, 0:3:2, :]

            def log_not(h):
                z = ps[:, 4 + h % 2, 0:384]
                t1, t2, t3 = (sbt[:, h % 2, i] for i in range(3))
                dve.wait_ge(abs_done, h + 1)
                if h >= 2:
                    dve.wait_ge(av_done, h - 1)
                link(dve, nc.vector.tensor_scalar(t2, z, SCALE, 0.0, ALU.mult, ALU.max))
                dve.wait_ge(soft_done, h + 1)
                link(dve, nc.vector.scalar_tensor_tensor(out=t2, in0=t2, scalar=-1.0, in1=t1,
                                                         op0=ALU.mult, op1=ALU.subtract))
                m2 = m01.unsqueeze(1).broadcast_to([P, 2, P])
                n2 = neg.unsqueeze(1).broadcast_to([P, 2, P])
                link(dve, nc.vector.tensor_tensor(diagonals(t2), diagonals(t2), m2, ALU.mult))
                dve_inc(lnot_done)
                link(dve, nc.vector.scalar_tensor_tensor(out=t3, in0=z, scalar=SCALE, in1=t2,
                                                         op0=ALU.mult, op1=ALU.add))
                link(dve, nc.vector.tensor_tensor(diagonals(t3), diagonals(t3), n2, ALU.add))

            for s in range(12):
                dve_step(dve, U_GATE + s)
                if 1 <= s < SB_HEADS + 1:
                    h = s - 1
                    dve.wait_ge(sfx_done, h + 1)
                    t3 = sbt[:, h % 2, 2]
                    nc.vector.tensor_tensor(t3, t3, ps[:, 6, 0:384], ALU.add).then_inc(arg_done, 1)
                if s < SB_HEADS:
                    log_not(s)
                if s % 2 and s >= 3 and s < SB_HEADS + 2:
                    k = (s - 3) // 2
                    dve.wait_ge(o_hi, k + 1)
                    nc.vector.tensor_tensor(hidl[:, k], ps[:, 7, (k % 2) * SEQ:(k % 2 + 1) * SEQ],
                                            hidh[:, k].bitcast(F32), ALU.subtract).then_inc(o_lo, 1)
                if s == 9:
                    dve.wait_ge(mix_done, 2)
                    for i in range(2):
                        o = gt[:, 0, i * SEQ:(i + 1) * SEQ].rearrange("p (t n) -> p t n", t=TT)
                        m = ps[:, 6, i * SEQ:(i + 1) * SEQ].rearrange("p (t n) -> p t n", t=TT)
                        link(dve, nc.vector.tensor_tensor(o, m, bsp[:, i:i + 1].broadcast_to([P, TT, P]),
                                                          ALU.add))
                    nc.vector.tensor_tensor(gt[:, 0], gt[:, 0], gu[:].rearrange("p k n -> p (k n)"),
                                            ALU.mult).then_inc(o_val, 1)
            for k in range(2):
                dve.wait_ge(o_hi, 4 + k + 1)
                nc.vector.tensor_tensor(hidl[:, 6 + k], gt[:, 0, k * SEQ:(k + 1) * SEQ],
                                        hidh[:, 6 + k].bitcast(F32), ALU.subtract).then_inc(o_lo, 1)
            for k in range(2):
                dve.wait_ge(o_hi, 8)
                nc.vector.scalar_tensor_tensor(out=hidl[:, 4 + k], in0=ps[:, 5, k * SEQ:(k + 1) * SEQ],
                                               scalar=par("pool_scale", k), in1=hidh[:, 4 + k].bitcast(F32),
                                               op0=ALU.mult, op1=ALU.subtract).then_inc(o_lo, 1)
            for c in range(2):
                dve_step(dve, U_BR + c)
                dve.wait_ge(used, U_BR + c + 1)
                dve.wait_ge(gate_sig, c + 1)
                link(dve, nc.vector.tensor_tensor(gate[:, c], gate[:, c], pair(2 * c), ALU.mult))
                dve_inc(br_done)
            for b in (1, 2):
                dve_step(dve, U_BR + b + 1)
                dve.wait_ge(used, U_BR + b + 2)
                dve.wait_ge(gate_sig, 6)
                for c in range(2):
                    g = gate[:, 2 * b + c]
                    link(dve, nc.vector.tensor_tensor(g, g, pair((4, 0)[b - 1] + 2 * c), ALU.mult))
                    ins = nc.vector.tensor_tensor(gate[:, c], gate[:, c], g, ALU.add)
                    if b == 1:
                        link(dve, ins)
                    else:
                        ins.then_inc(merged, 1)
            hT_dve(dve, 1, 1, None, None)
            for u in range(U_OUT, U_OUT + 4):
                dve_step(dve, u)
            dve.wait_ge(row_a_in, 16)
            post_dve(dve, 0, row_a)
            norm_dve(dve, 1, 2, 2, lambda k: par("g_ff_pre", k), None)
            mlp_dve(dve, 0)
            dve.wait_ge(row_b_in, 16)
            post_dve(dve, 1, row_b)

            def mod_norm(norm, fill, b, layer, vec):
                sc = (layer * 6 + vec + 1) * 8
                g = par("mix_g" if vec == 0 else "mlp_g", 8 * layer, 8)
                link(dve, nc.vector.scalar_tensor_tensor(out=modT[:, sc:sc + 8], in0=modT[:, sc:sc + 8],
                                                         scalar=1.0, in1=g, op0=ALU.add, op1=ALU.mult))
                dve_inc(mod_ok)
                norm_dve(dve, norm, fill, b, lambda k: mod_scale(layer, vec, k),
                         lambda k: mod_shift(layer, vec, k))

            mod_norm(2, 3, 3, 0, 0)
            dve.wait_ge(tr_done, 16)
            link(dve, nc.vector.memset(u_pad[:, :, 0:PAD], 0.0))
            for c in range(4):
                for h in range(2):
                    dve_step(dve, U_CIN + 2 * c + h)
                for i in range(2):
                    dve.wait_ge(glu_sig, 2 * c + i + 1)
                    ins = nc.vector.scalar_tensor_tensor(
                        out=u_pad[:, 2 * c + i, PAD:], in0=ps[:, chunk_bank(c), i * SEQ:(i + 1) * SEQ],
                        scalar=par("conv_b_in", 2 * c + i), in1=csg[:, c % 2, i], op0=ALU.add, op1=ALU.mult)
                    ins.then_inc(u_ok, 1)
                dve.wait_ge(u_ok, 2 * c + 2)
                for t in range(TAPS):
                    for i in range(2):
                        k = 2 * c + i
                        w = par("conv_dw", t * KT + k)
                        src = u_pad[:, k, t:t + SEQ]
                        if t == 0:
                            ins = nc.vector.tensor_scalar(cacc[:, k], src, w, par("conv_dw_b", k),
                                                          ALU.mult, ALU.add)
                        else:
                            dve.wait_ge(conv_tap, 62 * c + 2 * t - 1 + i)
                            ins = nc.vector.scalar_tensor_tensor(out=cacc[:, k], in0=src, scalar=w,
                                                                 in1=cacc[:, k], op0=ALU.mult, op1=ALU.add)
                        ins.then_inc(conv_tap, 1)
            dve.wait_ge(conv_tap, 62 * 4)
            dve_inc(conv_ok)
            dve.wait_ge(cs_sum, 1)
            mean, y, var, a = cmr[:, 0], cmr[:, 1], cmv[:, 0], cmv[:, 1]
            link(dve, nc.vector.tensor_scalar(mean, ps[:, 4, 0:SEQ], 1.0 / D, None, ALU.mult))
            nc.vector.tensor_tensor(cxc[:], cacc[:], mean.unsqueeze(1).broadcast_to([P, KT, SEQ]),
                                    ALU.subtract).then_inc(cs_xc, 1)
            dve.wait_ge(cs_sum, 2)
            rsqrt(dve, y, ps[:, 5, 0:SEQ], var, a, D)
            dve.wait_ge(cs_xc, 1)
            for k in range(KT):
                nc.vector.scalar_tensor_tensor(out=cxc[:, k], in0=cxc[:, k], scalar=par("conv_ln_g", k),
                                               in1=y, op0=ALU.mult, op1=ALU.mult).then_inc(cs_ln, 1)
                if k:
                    conv_out_part(dve, k - 1)
            conv_out_part(dve, KT - 1)
            for u in range(U_COUT, U_COUT + 4):
                dve_step(dve, u)
            dve.wait_ge(pool_x, 1)
            dve.wait_ge(row_kept, 2)
            gated_dve(dve, U_COUT + 4, row_a)
            mod_norm(3, 4, 5, 0, 3)
            mlp_dve(dve, 1)
            gated_dve(dve, U_MLP[1] + 32, row_b)

            mod_norm(4, 5, 6, 1, 0)
            for c in range(6):
                for h in range(2):
                    dve_step(dve, U_QKV + 2 * c + h)
                if c < 4:
                    dve.wait_ge(qk_sq, c + 1)
                    nc.vector.tensor_reduce(stat[:, 64 + 16 * c:80 + 16 * c].rearrange("p (t h) -> p t h", t=TT),
                                            qsq[:].rearrange("p t (h d) -> p t h d", d=HD), AX.X,
                                            ALU.add).then_inc(qk_ss, 1)
                if c in (1, 3):
                    dve.wait_ge(qk_ss, c + 1)
                    dve.wait_ge(qk_kept, c + 1)
                    at = 32 * (c // 2)
                    cut = [slice(base + at, base + at + 32) for base in (128, 64, 256, 192)]
                    rsqrt(dve, *(stat[:, q] for q in cut), HD)
                    src = (Qs, Ks)[c // 2]
                    for cc in range(2):
                        for tt in range(TT):
                            v = src[:, tt, cc * 512:(cc + 1) * 512].rearrange("p (h d) -> p h d", d=HD)
                            m = 128 + at + 16 * cc + 8 * tt
                            y = stat[:, m:m + 8].unsqueeze(2).broadcast_to([P, 8, HD])
                            link(dve, nc.vector.tensor_tensor(v, v, y, ALU.mult))
                    dve_inc(qk_n)
            for s in range(AT_HEADS + 4):
                if s < AT_HEADS:
                    h = s
                    dve.wait_ge(s_z, h + 1)
                    if h >= 3:
                        dve.wait_ge(s_tr, h - 2)
                    if h == 0:
                        dve.wait_ge(qk_ss, 4)
                    slope = float(np.float32(2.0 ** (-8.0 * (h + 1) / AT_HEADS))) / SCALE
                    a = aS[:, h % 3]
                    ins = nc.vector.scalar_tensor_tensor(out=a, in0=dist, scalar=slope,
                                                         in1=ps[:, 4 + h % 2, 0:384], op0=ALU.mult,
                                                         op1=ALU.add)
                    ins.then_inc(s_arg, 1)
                    dve.wait_ge(s_arg, h + 1)
                    m = 320 + 2 * (h % 2)
                    for i, c in enumerate((slice(0, P), slice(P, 384))):
                        link(dve, nc.vector.tensor_reduce(stat[:, m + 16 + i:m + 17 + i], a[:, c], AX.X, ALU.max))
                    nc.vector.tensor_scalar(stat[:, m:m + 2], stat[:, m + 16:m + 18], -SCALE, None,
                                            ALU.mult).then_inc(s_max, 1)
                if 1 <= s < AT_HEADS + 1:
                    h = s - 1
                    a, m = aS[:, h % 3], 328 + 2 * (h % 2)
                    dve.wait_ge(s_exp, 2 * h + 2)
                    link(dve, nc.vector.reciprocal(stat[:, m + 16:m + 18], stat[:, m:m + 2]))
                    for i, c in enumerate((slice(0, P), slice(P, 384))):
                        link(dve, nc.vector.tensor_scalar(a[:, c], a[:, c], stat[:, m + 16 + i:m + 17 + i],
                                                          None, ALU.mult))
                    dve_inc(s_p)
                if s >= 4 and s % 2 == 0:
                    k = (s - 4) // 2
                    dve.wait_ge(hT_hi, 56 + k + 1)
                    nc.vector.tensor_tensor(hTl[:, k], ps[:, k % 2, 0:SEQ], hTh[:, k].bitcast(F32),
                                            ALU.subtract).then_inc(hT_lo, 1)
            for u in range(U_WO, U_WO + 4):
                dve_step(dve, u)
            gated_dve(dve, U_WO + 4, row_a)
            mod_norm(5, 6, 8, 1, 3)
            mlp_dve(dve, 2)
            gated_dve(dve, U_MLP[2] + 32, row_b)

        @block.gpsimd
        def _(pool):
            nc.gpsimd.memset(zero_r[:].bitcast(F32), 0.0)
            nc.gpsimd.memset(pp[:, :, 0:16], 0.0)
            link_pool(pool, nc.gpsimd.memset(wpd[:], 0.0))
            nc.gpsimd.sem_inc(pad_ok, 1)
            pool.wait_ge(o_lo, 8)
            pool.dma_start(row_a[:], row(g_mix_post[0])).then_inc(row_a_in, 16)
            pool.dma_start(row_b[:], row(g_ff_post[0])).then_inc(row_b_in, 16)
            pool.dma_start(row_c[:], row(conv_b_out_2[0])).then_inc(row_c_in, 16)
            mlp_pool(pool, 0)
            pool.wait_ge(row_kept, 1)
            pool.wait_ge(row_c_in, 16)
            pool.wait_ge(xn_act, 3)
            pool.wait_ge(xn_dve, 3)
            link_pool(pool, nc.gpsimd.tensor_tensor(row_c[:], row_c[:], row_a[:], ALU.mult))
            for tt in range(TT):
                link_pool(pool, nc.gpsimd.tensor_tensor(X[:, tt], X[:, tt], row_c[:], ALU.add))
            nc.gpsimd.sem_inc(pool_x, 1)
            mlp_pool(pool, 1)
            mlp_pool(pool, 2)


_INS = ["x", "w_in", "w_pool", "pool_scale", "gm_gain", "w_spatial", "b_spatial", "w_br_sb", "w_br_pool",
        "w_br_gm", "w_out", "g_mix_pre", "g_mix_post", "g_ff_pre", "g_ff_post", "w_ff_in", "w_ff_out",
        "c_2", "ada_w_2", "ada_b_2", "mix_norm_g_2", "mlp_norm_g_2", "conv_w_in_2", "conv_b_in_2",
        "conv_dw_2", "conv_dw_b_2", "conv_ln_g_2", "conv_ln_b_2", "conv_w_out_2", "conv_b_out_2",
        "attn_w_qkv_2", "attn_q_norm_g_2", "attn_k_norm_g_2", "attn_w_o_2", "mlp_w1_2", "mlp_w2_2"]


def kernel(**inputs):
    import concourse.bacc as bacc
    from concourse.bass_utils import run_bass_kernel_spmd

    nc = bacc.Bacc("TRN2", target_bir_lowering=False, num_devices=1)
    arrays, args = {}, []
    shapes = shape_constants()
    for name in _INS + ["consts", "inv_count"]:
        a = shapes[name == "inv_count"] if name in ("consts", "inv_count") else inputs[name]
        a = np.ascontiguousarray(a)
        arrays[f"in_{name}"] = a
        args.append(nc.dram_tensor(f"in_{name}", a.shape, mybir.dt.from_np(a.dtype),
                                   kind="ExternalInput").ap())
    args.append(nc.dram_tensor("out_x", (1, SEQ, D), F32, kind="ExternalOutput").ap())
    build_kernel(nc, *args)
    r = run_bass_kernel_spmd(nc, [arrays], core_ids=[0])
    return r.results[0]["out_x"]
```

```python
from contextlib import ExitStack

import numpy as np

import concourse.bass as bass
from concourse import mybir

ALU = mybir.AluOpType
ACT = mybir.ActivationFunctionType
AX = mybir.AxisListType
F32 = mybir.dt.float32
F32R = mybir.dt.float32r
I32 = mybir.dt.int32

P = 128
SEQ = 256
TT = SEQ // P
D = 1024
KT = D // P
UNIT = 2048
RING = 4
EPS = 1e-6
RSQRT_MAGIC = 1597463007.0
GELU_2C = 2.0 * float(np.sqrt(2.0 / np.pi))
GELU_A = 0.044715
HD = 64
SB_HEADS = 8
AT_HEADS = 16
TAPS = 31
PAD = TAPS - 1
SCALE = HD ** -0.5
NEG = -1e30
FAR = -3e37
WINDOWS = (2, 4, 8, 16)

U_Q, U_K, U_V, U_PU, U_GV, U_GATE = 0, 2, 4, 6, 8, 9
U_BR = 21
U_OUT = 25
U_MLP = (29, 73, 121)
U_CIN, U_COUT = 61, 69
U_QKV, U_WO = 105, 117
N_UNITS = 153

C_ID, C_ONE, C_TRI, C_M01, C_KEEP, C_NEG, C_DIST, C_END = 0, 128, 256, 384, 512, 640, 768, 1152

PARAMS = {}
_at = 0
for _name, _n in (("g_mix_pre", 8), ("g_ff_pre", 8), ("mix_g", 16), ("mlp_g", 16), ("conv_b_in", 16),
                  ("conv_dw_b", 8), ("conv_ln_g", 8), ("conv_ln_b", 8), ("pool_scale", 2), ("c", 8)):
    PARAMS[_name] = (_at, _n)
    _at += _n
N_MISC = _at
PARAMS["ada_b"] = (128, 96)
PARAMS["conv_dw"] = (256, TAPS * KT)
N_PCOL = 256 + TAPS * KT


def shape_constants():
    c = np.zeros((P, C_END), np.float32)
    i = np.arange(P)
    c[:, C_ID:C_ID + P] = np.eye(P)
    c[:, C_ONE:C_ONE + P] = 1.0
    c[:, C_TRI:C_TRI + P] = i[:, None] > i[None, :]
    c[:, C_M01:C_M01 + P] = i[:, None] < i[None, :]
    c[:, C_KEEP:C_KEEP + P] = i[:, None] <= i[None, :]
    c[:, C_NEG:C_NEG + P] = np.where(i[:, None] < i[None, :], 0.0, NEG)
    near = np.where(i[None, :] <= i[:, None], i[None, :] - i[:, None], FAR)
    c[:, C_DIST:C_DIST + P] = near
    c[:, C_DIST + P:C_DIST + 2 * P] = i[None, :] - i[:, None] - P
    c[:, C_DIST + 2 * P:] = near
    inv = np.zeros((P, 2, SEQ), np.float32)
    t = np.arange(SEQ) + 1.0
    for g, w in enumerate(WINDOWS):
        inv[HD * (g % 2):HD * (g % 2) + HD, g // 2] = 1.0 / np.minimum(t, float(w))
    return c, inv.reshape(P, 2 * SEQ)


def build_kernel(nc, x, w_in, w_pool, pool_scale, gm_gain, w_spatial, b_spatial, w_br_sb, w_br_pool,
                 w_br_gm, w_out, g_mix_pre, g_mix_post, g_ff_pre, g_ff_post, w_ff_in, w_ff_out,
                 c_2, ada_w_2, ada_b_2, mix_norm_g_2, mlp_norm_g_2, conv_w_in_2, conv_b_in_2,
                 conv_dw_2, conv_dw_b_2, conv_ln_g_2, conv_ln_b_2, conv_w_out_2, conv_b_out_2,
                 attn_w_qkv_2, attn_q_norm_g_2, attn_k_norm_g_2, attn_w_o_2, mlp_w1_2, mlp_w2_2,
                 consts, inv_count, out):
    ctx = ExitStack()
    with ctx:
        size = [(nc.sbuf_base + 63) // 64 * 64]

        def nbytes(shape):
            return 4 * int(np.prod(shape[1:]))

        def place(name, shape, dt=F32):
            at = size[0]
            size[0] += (nbytes(shape) + 31) // 32 * 32
            return nc.alloc_sbuf_tensor_at(name, shape, dt, offset=at)

        def area(name, n):
            start = size[0]
            size[0] += n

            def at(tile, offset, shape, dt=F32):
                assert offset + nbytes(shape) <= n, (name, tile)
                return nc.alloc_sbuf_tensor_at(tile, shape, dt, offset=start + offset)

            return at

        raw = place("raw", [P, RING, UNIT])
        hi = place("hi", [P, RING, UNIT], F32R)
        lo = place("lo", [P, RING, UNIT], F32R)
        X = place("X", [P, TT, D])
        hTh = place("hTh", [P, KT, SEQ], F32R)
        hTl = place("hTl", [P, KT, SEQ], F32R)
        hid_area = area("hid", 16384)
        cst = place("cst", [P, C_END])
        pcol = place("pcol", [P, N_PCOL])
        modT = place("modT", [P, 96])
        cond = place("cond", [P, 16])
        stat = place("stat", [P, 352])
        zero_r = place("zero_r", [P, P], F32R)
        qk_gain = place("qk_gain", [P, 2])
        ada_area = area("ada", 16384)
        row_area = area("rows", 12288)
        acc_area = area("acc", 2048)
        big = area("big", 33792)

        assert size[0] <= nc.sbuf_usable_end
        hidh = hid_area("hidh", 0, [P, 8, SEQ], F32R)
        hidl = hid_area("hidl", 8192, [P, 8, SEQ], F32R)
        ada_raw = ada_area("ada_raw", 0, [P, 2, 4, 512])
        ada_acc = acc_area("ada_acc", 0, [P, 512])
        row_a = row_area("row_a", 0, [P, D])
        row_b = row_area("row_b", 4096, [P, D])
        row_c = row_area("row_c", 8192, [P, D])
        diag_n = big("diag_n", 0, [P, TT, P])
        junk_act = big("junk_act", 1024, [P, TT, 2, 512])
        junk_dve = big("junk_dve", 9216, [P, 512])
        y_tmp = big("y_tmp", 12288, [P, D])
        relu = big("relu", 16384, [P, 4 * SEQ])
        sqr = big("sqr", 20480, [P, 4 * SEQ])
        lo_tmp = big("lo_tmp", 24576, [P, 2, 2, SEQ])
        prow = big("prow", 16384, [P, 4, P])
        wsrow = big("wsrow", 18432, [P, 4, P])
        gate = big("gate", 0, [P, 6, TT, 512])
        qT = big("qT", 24576, [P, 4, SEQ])
        kT = big("kT", 28672, [P, 4, SEQ])
        gm_row = big("gm_row", 20480, [P, SEQ])
        vS = ada_area("vS", 0, [P, TT, 512])
        sbt = ada_area("sbt", 4096, [P, 2, 3, 384])
        gt = ada_area("gt", 4096, [P, 3, 512])
        gv = ada_area("gv", 13312, [P, TT, SEQ])
        wpd = big("wpd", 21504, [P, 2, P])
        wsT = row_area("wsT", 0, [P, 4, P])
        pp = row_area("pp", 2048, [P, 2, 16 + SEQ])
        pa = row_area("pa", 4224, [P, 2, 16 + SEQ])
        pb = row_area("pb", 6400, [P, 2, 16 + SEQ])
        gu = row_area("gu", 8576, [P, 2, SEQ])
        bsp = row_area("bsp", 10624, [P, 2, P])
        inv = big("inv", 22528, [P, 2, SEQ])
        u_pad = big("u_pad", 0, [P, KT, PAD + SEQ])
        cacc = big("cacc", 9152, [P, KT, SEQ])
        cxc = big("cxc", 17344, [P, KT, SEQ])
        csg = big("csg", 25536, [P, 2, 2, SEQ])
        cmr = big("cmr", 29632, [P, 2, SEQ])
        cmv = acc_area("cmv", 0, [P, 2, SEQ])
        Qs = big("Qs", 0, [P, TT, D])
        Ks = big("Ks", 8192, [P, TT, D])
        Vs = big("Vs", 16384, [P, TT, D])
        aS = hid_area("aS", 0, [P, 3, 2, 384])
        aT = hid_area("aT", 9216, [P, 2, 2, 384])
        qT2 = ada_area("qT2", 0, [P, KT, SEQ])
        kT2 = ada_area("kT2", 8192, [P, KT, SEQ])

        ps = ctx.enter_context(nc.psum_tensor("ps", [P, 8, 512], F32))

        ident = cst[:, C_ID:C_ID + P]
        ones = cst[:, C_ONE:C_ONE + P]
        tri = cst[:, C_TRI:C_TRI + P]
        m01 = cst[:, C_M01:C_M01 + P]
        keep = cst[:, C_KEEP:C_KEEP + P]
        neg = cst[:, C_NEG:C_NEG + P]
        dist = cst[:, C_DIST:C_DIST + 3 * P]

        def par(name, j=0, n=1):
            at = PARAMS[name][0] + j
            return pcol[:, at:at + n]

        def sem(name):
            return ctx.enter_context(nc.semaphore(name))

        raw_landed = [sem(f"raw_landed{i}") for i in range(RING)]
        hi_made = sem("hi_made")
        lo_made = sem("lo_made")
        used = sem("used")
        ada_landed = [sem(f"ada_landed{i}") for i in range(2)]
        ada_step = sem("ada_step")
        ada_cols = sem("ada_cols")
        ada_kept = sem("ada_kept")
        x_in = sem("x_in")
        cst_in = sem("cst_in")
        par_in = sem("par_in")
        misc_in = sem("misc_in")
        row_a_in = sem("row_a_in")
        row_b_in = sem("row_b_in")
        row_c_in = sem("row_c_in")
        qk_gain_in = sem("qk_gain_in")
        out_sem = sem("out_sem")
        dve_chain = sem("dve_chain")
        act_chain = sem("act_chain")
        pool_chain = sem("pool_chain")
        par_tr = sem("par_tr")
        par_ok = sem("par_ok")
        cond_sig = sem("cond_sig")
        mod_ok = sem("mod_ok")
        x_ver = sem("x_ver")
        x_half = sem("x_half")
        tile0_done = sem("tile0_done")
        ss_act = sem("ss_act")
        diag_ok = sem("diag_ok")
        hT_full = sem("hT_full")
        tr_done = sem("tr_done")
        hT_hi = sem("hT_hi")
        hT_lo = sem("hT_lo")
        relu_done = sem("relu_done")
        sq_done = sem("sq_done")
        hid_hi = sem("hid_hi")
        hid_lo = sem("hid_lo")
        row_bc = sem("row_bc")
        row_kept = sem("row_kept")
        qkv_kept = sem("qkv_kept")
        kT_kept = sem("kT_kept")
        p_kept = sem("p_kept")
        gelu_act = sem("gelu_act")
        gelu_dve = sem("gelu_dve")
        gate_kept = sem("gate_kept")
        gate_sig = sem("gate_sig")
        pool_in = sem("pool_in")
        vn_ok = sem("vn_ok")
        mix_done = sem("mix_done")
        z_done = sem("z_done")
        abs_done = sem("abs_done")
        soft_done = sem("soft_done")
        lnot_done = sem("lnot_done")
        sfx_done = sem("sfx_done")
        arg_done = sem("arg_done")
        a_done = sem("a_done")
        av_done = sem("av_done")
        o_val = sem("o_val")
        o_hi = sem("o_hi")
        o_lo = sem("o_lo")
        br_done = sem("br_done")
        merged = sem("merged")
        pad_ok = sem("pad_ok")
        glu_sig = sem("glu_sig")
        u_ok = sem("u_ok")
        conv_ok = sem("conv_ok")
        cs_sum = sem("cs_sum")
        cs_sq = sem("cs_sq")
        cs_xc = sem("cs_xc")
        cs_ln = sem("cs_ln")
        cs_sig = sem("cs_sig")
        cs_y = sem("cs_y")
        qk_kept = sem("qk_kept")
        qk_sq = sem("qk_sq")
        qk_ss = sem("qk_ss")
        qk_n = sem("qk_n")
        qk_tr = sem("qk_tr")
        qk_T = sem("qk_T")
        s_z = sem("s_z")
        s_arg = sem("s_arg")
        s_max = sem("s_max")
        s_exp = sem("s_exp")
        s_p = sem("s_p")
        s_tr = sem("s_tr")
        s_pT = sem("s_pT")
        s_o = sem("s_o")
        ss_post = sem("ss_post")
        consts_ok = sem("consts_ok")
        pool_x = sem("pool_x")


        def split_hi(act, n, slot):
            act.wait_ge(raw_landed[slot], n_landed(n, slot))
            nc.scalar.activation(hi[:, slot], raw[:, slot], ACT.Copy).then_inc(hi_made, 1)

        def n_landed(n, slot):
            return (n - slot) * (16 // RING) + 16

        def split_lo(dve, n, slot, turn=False):
            dve.wait_ge(hi_made, n + 1)
            if turn:
                dve.wait_ge(lo_made, n)
            nc.vector.tensor_tensor(lo[:, slot], raw[:, slot], hi[:, slot].bitcast(F32),
                                    ALU.subtract).then_inc(lo_made, 1)

        def pool_step(pool, u):
            n, slot = u + RING, u % RING
            pool.wait_ge(hi_made, n + 1)
            pool.wait_ge(lo_made, n)
            nc.gpsimd.tensor_tensor(lo[:, slot], raw[:, slot], hi[:, slot].bitcast(F32),
                                    ALU.subtract).then_inc(lo_made, 1)

        def act_step(act, u, i=None, j=None):
            act.wait_ge(used, u + 1)
            if not isinstance(u, int) or u + RING < N_UNITS:
                split_hi(act, u + RING, slot_of(u, j))

        def dve_step(dve, u, j=None, turn=False):
            if not isinstance(u, int) or u + RING < N_UNITS:
                split_lo(dve, u + RING, slot_of(u, j), turn)

        def slot_of(u, j):
            return (u if j is None else j) % RING

        def load(sp, n, src, j=None):
            slot = slot_of(n, j)
            if not isinstance(n, int) or n >= RING:
                sp.wait_ge(lo_made, n - (RING - 1))
            dst = raw[:, slot].rearrange("p (k n) -> p k n", k=src.shape[1])
            sp.dma_start(dst, src).then_inc(raw_landed[slot], 16)

        def rows3(w):
            return w.rearrange("(k p) n -> p k n", p=P)

        def unit_w(pe, u, j, act_h, act_l, k0, bank, first, nk=4):
            slot = slot_of(u, j)
            pe.wait_ge(lo_made, u + 1)
            wh = hi[:, slot].rearrange("p (k n) -> p k n", k=nk)
            wl = lo[:, slot].rearrange("p (k n) -> p k n", k=nk)
            for ct in range(UNIT // nk // P):
                o = ps[:, bank + ct // 2, (ct % 2) * SEQ:(ct % 2 + 1) * SEQ]
                c = slice(ct * P, (ct + 1) * P)
                for k in range(nk):
                    mm(pe, o, wh[:, k, c], act_h[:, k0 + k], first and k == 0 and ct % 2 == 0)
                    mm(pe, o, wh[:, k, c], act_l[:, k0 + k])
                    last = mm(pe, o, wl[:, k, c], act_h[:, k0 + k])
            last.then_inc(used, 1)

        def mm(pe, o, lhs, rhs, start=False):
            return nc.tensor.matmul(o, lhs, rhs, start=start, stop=False, skip_group_check=True)

        def unit_x(pe, u, j, act_h, act_l, k0, outs, first, nk=4, cols=512, final=False):
            slot = slot_of(u, j)
            pe.wait_ge(lo_made, u + 1)
            wh = hi[:, slot].rearrange("p (k n) -> p k n", k=nk)
            wl = lo[:, slot].rearrange("p (k n) -> p k n", k=nk)
            parts = UNIT // nk // cols
            for tt in range(TT):
                t = slice(tt * P, (tt + 1) * P)
                for c in range(parts):
                    o = outs(tt, c)
                    n = slice(c * cols, (c + 1) * cols)
                    for k in range(nk):
                        mm(pe, o, act_h[:, k0 + k, t], wh[:, k, n], first and k == 0)
                        mm(pe, o, act_l[:, k0 + k, t], wh[:, k, n])
                        last = mm(pe, o, act_h[:, k0 + k, t], wl[:, k, n])
                if final and tt == 0:
                    last.then_inc(tile0_done, 1)
            last.then_inc(used, 1)

        def transposes(pe, src, ready, diag=None):
            pe.wait_ge(*ready)
            for k in range(KT):
                for tt in range(TT):
                    o = tr_bank(k)[:, tt * P:(tt + 1) * P]
                    if diag is None:
                        last = nc.tensor.transpose(o, src(tt, k), ident)
                    else:
                        last = nc.tensor.matmul(o, src(tt, k), diag[:, tt], start=True, stop=True)
                if k % 2:
                    last.then_inc(tr_done, 1)

        def tr_bank(k):
            return ps[:, 4 + k // 2, (k % 2) * SEQ:(k % 2 + 1) * SEQ]

        def hT_act(act, fill, b, scale, bias, mod=None):
            for k in range(KT):
                act.wait_ge(tr_done, 4 * fill + k // 2 + 1)
                if mod is not None and k % 2:
                    if k > 3:
                        act.wait_ge(hT_lo, 8 * b + k - 3)
                    nc.scalar.activation(lo_tmp[:, 1, k // 2 % 2], tr_bank(k), ACT.Identity, bias=bias(k),
                                         scale=scale(k)).then_inc(hT_full, 1)
                nc.scalar.activation(hTh[:, k], tr_bank(k), ACT.Identity, bias=bias(k),
                                     scale=scale(k)).then_inc(hT_hi, 1)

        def hT_dve(dve, fill, b, scale, bias, mod=None):
            for k in range(KT):
                if k % 2 == 0:
                    dve.wait_ge(hT_hi, 8 * b + k + 2)
                if scale is None:
                    nc.vector.tensor_tensor(hTl[:, k], tr_bank(k), hTh[:, k].bitcast(F32),
                                            ALU.subtract).then_inc(hT_lo, 1)
                elif bias is None:
                    nc.vector.scalar_tensor_tensor(out=hTl[:, k], in0=tr_bank(k), scalar=scale(k),
                                                   in1=hTh[:, k].bitcast(F32), op0=ALU.mult,
                                                   op1=ALU.subtract).then_inc(hT_lo, 1)
                else:
                    if k % 2:
                        dve.wait_ge(hT_full, 4 * mod + k // 2 + 1)
                    else:
                        link(dve, nc.vector.tensor_scalar(lo_tmp[:, 0, k // 2 % 2], tr_bank(k), scale(k), bias(k),
                                                          ALU.mult, ALU.add))
                    tmp = lo_tmp[:, k % 2, k // 2 % 2]
                    nc.vector.tensor_tensor(hTl[:, k], tmp, hTh[:, k].bitcast(F32),
                                            ALU.subtract).then_inc(hT_lo, 1)

        links = {"dve": 0, "act": 0, "pool": 0}

        def link(dve, ins):
            links["dve"] += 1
            ins.then_inc(dve_chain, 1)
            dve.wait_ge(dve_chain, links["dve"])

        def link_act(act, ins):
            links["act"] += 1
            ins.then_inc(act_chain, 1)
            act.wait_ge(act_chain, links["act"])

        def link_pool(pool, ins):
            links["pool"] += 1
            ins.then_inc(pool_chain, 1)
            pool.wait_ge(pool_chain, links["pool"])

        def rsqrt(dve, y, ss, v, a, n, ss2=None):
            if ss2 is None:
                link(dve, nc.vector.tensor_scalar(a, ss, 1.0 / n, EPS, ALU.mult, ALU.add))
            else:
                link(dve, nc.vector.scalar_tensor_tensor(out=a, in0=ss, scalar=EPS, in1=ss2, op0=ALU.add,
                                                         op1=ALU.add))
            nc.vector.tensor_scalar(y.bitcast(I32), a.bitcast(I32), 1, None,
                                    ALU.logical_shift_right).then_inc(dve_chain, 1)
            links["dve"] += 1
            link(dve, nc.vector.tensor_scalar(v, a, -0.5, None, ALU.mult))
            link(dve, nc.vector.tensor_scalar(y.bitcast(I32), y.bitcast(I32), -1.0, RSQRT_MAGIC,
                                              ALU.mult, ALU.add))
            for _ in range(3):
                link(dve, nc.vector.tensor_tensor(a, y, y, ALU.mult))
                link(dve, nc.vector.tensor_tensor(a, a, v, ALU.mult))
                link(dve, nc.vector.scalar_tensor_tensor(out=y, in0=a, scalar=1.5, in1=y, op0=ALU.add,
                                                         op1=ALU.mult))

        N_SS, N_Y, N_A, N_V = stat[:, 0:2], stat[:, 8:10], stat[:, 16:18], stat[:, 24:26]

        def halves(t, tt):
            return t[:, tt, 0:512], t[:, tt, 512:D]

        def ss_col(post, c, tt=0, n=1):
            at = 4 * post + 2 * c + tt
            return stat[:, at:at + n]

        def rstd_col(post, tt=0, n=1):
            at = 8 + 2 * post + tt
            return stat[:, at:at + n]

        def rstd(dve, post, tt=0, n=1):
            at = 2 * post + tt
            rsqrt(dve, rstd_col(post, tt, n), ss_col(post, 0, tt, n), stat[:, 24 + at:24 + at + n],
                  stat[:, 16 + at:16 + at + n], D, ss_col(post, 1, tt, n))

        def norm_act(act, norm, fill, b, free, scale, bias, mod=None):
            def square_x(tt, c):
                nc.scalar.activation(junk_act[:, tt, c], halves(X, tt)[c], ACT.Square,
                                     scale=D ** -0.5, accum_out=ss_col(0, c, tt)).then_inc(ss_act, 1)

            if norm == 0:
                act.wait_ge(x_in, 16)
            elif norm > 2:
                act.wait_ge(x_half, 2 * (norm - 2))
                square_x(0, 0)
                square_x(1, 0)
                act.wait_ge(x_ver, 2 * norm - 1)
                square_x(0, 1)
            if norm <= 2:
                if norm:
                    act.wait_ge(x_ver, 2 * norm - 1)
                square_x(0, 0)
                square_x(0, 1)
                if norm:
                    act.wait_ge(x_ver, 2 * norm)
                square_x(1, 0)
            if free:
                act_step(act, free - 2)
                act_step(act, free - 1)
            hT_act(act, fill, b, scale, bias, mod)

        def diagonals_dve(dve):
            rstd(dve, 0, 0, TT)
            i2, y2 = ident.unsqueeze(1).broadcast_to([P, TT, P]), rstd_col(0, 0, TT).unsqueeze(2)
            nc.vector.tensor_tensor(diag_n[:], i2, y2.broadcast_to([P, TT, P]), ALU.mult).then_inc(diag_ok, 1)

        def square_last(dve):
            x = halves(X, 1)[1]
            link(dve, nc.vector.scalar_tensor_tensor(out=junk_dve[:], in0=x, scalar=1.0 / D, in1=x, op0=ALU.mult,
                                                     op1=ALU.mult, accum_out=ss_col(0, 1, 1)))

        def norm_dve(dve, norm):
            if norm == 0:
                dve.wait_ge(x_in, 16)
            else:
                dve.wait_ge(x_ver, 2 * norm)
            square_last(dve)
            dve.wait_ge(ss_act, 3 * norm + 3)
            diagonals_dve(dve)

        def dve_inc(s, n=1):
            nc.vector.sem_inc(s, n)

        def norm_pe(pe, norm):
            transposes(pe, lambda tt, k: X[:, tt, k * P:(k + 1) * P],
                       (diag_ok, norm + 1), diag_n)

        def y_bank(tt, c):
            return ps[:, 2 * tt + c]

        def y_half(tt, c):
            return halves((y_tmp, sqr)[tt][:].unsqueeze(1), 0)[c]

        def y_ready(eng, which, last, tt, c):
            if c == 0:
                eng.wait_ge(used, last)
            elif tt == 0:
                eng.wait_ge(tile0_done, which + 1)
            else:
                eng.wait_ge(used, last + 1)

        QUARTERS = ((0, 0), (1, 0), (0, 1), (1, 1))

        def post_act(act, which, last):
            for tt, c in QUARTERS:
                y_ready(act, which, last, tt, c)
                nc.scalar.activation(junk_act[:, tt, c], y_bank(tt, c), ACT.Square,
                                     scale=D ** -0.5, accum_out=ss_col(1, c, tt)).then_inc(ss_post, 1)

        def post_dve(dve, which, last, row):
            for q, (tt, c) in enumerate(QUARTERS):
                dve.wait_ge(ss_post, 4 * which + q + 1)
                y_ready(dve, which, last, tt, c)
                link(dve, nc.vector.tensor_tensor(y_half(tt, c), y_bank(tt, c), row[:, 512 * c:512 * c + 512],
                                                  ALU.mult))
                if c:
                    rstd(dve, 1, tt)
                    nc.vector.scalar_tensor_tensor(out=X[:, tt], in0=(y_tmp, sqr)[tt][:],
                                                   scalar=rstd_col(1, tt), in1=X[:, tt], op0=ALU.mult,
                                                   op1=ALU.add).then_inc(x_ver, 1)

        def gated_dve(dve, which, last, row, norm=True):
            for tt, c in QUARTERS:
                y_ready(dve, which, last, tt, c)
                y, x = y_half(tt, c), halves(X, tt)[c]
                link(dve, nc.vector.tensor_tensor(y, y_bank(tt, c), row[:, 512 * c:512 * c + 512], ALU.mult))
                ins = nc.vector.tensor_tensor(x, x, y, ALU.add)
                if c == 0:
                    ins.then_inc(x_half, 1)
                    dve.wait_ge(x_half, 2 * (which - 2) + tt + 1)
                    continue
                ins.then_inc(x_ver, 1)
            if norm:
                norm_dve(dve, which + 1)

        def gate_row(pe, layer, i):
            pe.wait_ge(ada_kept, (10, 18, 18, 24)[2 * layer + i] + 1)
            for k in range(KT):
                m = layer * 48 + (2, 5)[i] * 8 + k
                last = nc.tensor.matmul(ps[:, 6 + k // 4, (k % 4) * P:(k % 4 + 1) * P],
                                        modT[:, m:m + 1].broadcast_to([P, P]), ident,
                                        start=True, stop=True)
            last.then_inc(row_bc, 1)

        def keep_row(act, layer, i):
            act.wait_ge(row_bc, 2 * layer + i + 1)
            nc.scalar.activation((row_a, row_b)[i][:], pair(6).rearrange("p b n -> p (b n)"),
                                 ACT.Copy).then_inc(row_kept, 1)

        def hid(t, c):
            return t[:, 4 * (c % 2):4 * (c % 2) + 4]

        def mlp_pe(pe, m):
            u0 = U_MLP[m]
            pe.wait_ge(hT_lo, 8 * (2, 5, 8)[m] + 4)
            unit_w(pe, u0, None, hTh, hTl, 0, 4, True)
            pe.wait_ge(hT_lo, 8 * (2, 5, 8)[m] + 8)
            unit_w(pe, u0 + 1, None, hTh, hTl, 4, 4, False)
            for b in range(4):
                nc.tensor.matmul(ps[:, b, 0:2], zero_r[:], zero_r[:, 0:2], start=True, stop=False,
                                 skip_group_check=True)
            ada_sum(pe, ADA_HEAD[m][0])

            def first(c, u, j, chunk):
                pe.wait_ge(relu_done, chunk)
                unit_w(pe, u, j, hTh, hTl, 0, 4, True)
                unit_w(pe, u + 1, j + 1, hTh, hTl, 4, 4, False)

            def second(par_, u, j, chunk, after=(None, None), final=False):
                pe.wait_ge(hid_lo, chunk)
                for h in range(2):
                    unit_x(pe, u + h, j + h, hid(hidh, par_), hid(hidl, par_), 0,
                           lambda tt, c, h=h: y_bank(tt, h), False, final=final and h == 1)
                    if after[h] is not None:
                        after[h]()

            with nc.tensor.Fori(0, 3, 1) as i:
                n, s = 8 * i + (u0 + 2), u0 + 2
                first(1, n, s, 2 * i + (8 * m + 1))
                second(0, n + 2, s + 2, 2 * i + (8 * m + 1))
                if m < 2:
                    ada_sum(pe, ada_loop(m, i)[0][0])
                first(2, n + 4, s + 4, 2 * i + (8 * m + 2))
                second(1, n + 6, s + 6, 2 * i + (8 * m + 2))
                if m < 2:
                    ada_sum(pe, ada_loop(m, i)[1][0])
            n = u0 + 26
            first(7, n, n, 8 * m + 7)
            second(0, n + 2, n + 2, 8 * m + 7,
                   (lambda: ada_sum(pe, ADA_TAIL[m][0]), (lambda: gate_row(pe, m - 1, 1)) if m else None))
            second(1, n + 4, n + 4, 8 * m + 8, final=True)

        def mlp_act(act, m):
            u0 = U_MLP[m]

            def relu_of(chunk):
                nc.scalar.activation(relu[:], ps[:, 4:6].rearrange("p b n -> p (b n)"),
                                     ACT.Relu).then_inc(relu_done, 1)

            def hi_of(par_, chunk):
                act.wait_ge(sq_done, chunk + 1)
                nc.scalar.activation(hid(hidh, par_).rearrange("p k n -> p (k n)"), sqr[:],
                                     ACT.Copy).then_inc(hid_hi, 1)

            act_step(act, u0)
            act.wait_ge(used, u0 + 2)
            relu_of(8 * m)
            act_step(act, u0 + 1)
            hi_of(0, 8 * m)

            def body(u, s, js, chunk):
                for j in js:
                    if j % 4 == 1 and j < len(js) - 1:
                        act.wait_ge(used, u + (j + 1))
                        relu_of(chunk + j // 4)
                    act_step(act, u + j, j=s + j)
                    if j % 4 == 1 and j < len(js) - 1:
                        hi_of(1 - j // 4, chunk + j // 4)

            with nc.scalar.Fori(0, 3, 1) as i:
                body(8 * i + (u0 + 2), u0 + 2, range(8), 2 * i + (8 * m + 1))
            body(u0 + 26, u0 + 26, range(4) if m < 2 else range(3), 8 * m + 7)
            if m:
                keep_row(act, m - 1, 1)

        def mlp_pool(pool, m):
            def square(chunk, free):
                pool.wait_ge(relu_done, chunk + 1)
                if free:
                    pool.wait_ge(hid_lo, chunk)
                nc.gpsimd.tensor_tensor(sqr[:], relu[:], relu[:], ALU.mult).then_inc(sq_done, 1)

            square(8 * m, m > 0)
            with nc.gpsimd.Fori(1, 8, 1) as c:
                square(c + 8 * m, True)

        ADA_IN = [(0, 0, 6), (1, 0, 7)]
        ADA_QKV = [(18 + q, 1, 6 + q) for q in range(4)]
        ADA_HEAD = ((2, 0, 8), (10, 0, 10), (22, 1, 10))
        ADA_TAIL = ((9, 0, 9), (17, 0, 11), (23, 1, 11))

        def ada_loop(m, i):
            return [(2 * i + (8 * m + 3 + q), m, 2 * i + q) for q in range(2)]

        def ada_load(sp, chunk, h):
            number, layer, c = chunk
            sp.wait_ge(ada_step, number * 8 + (4 * h + 4))
            src = rows3(ada_w_2[layer])[:, 4 * h:4 * h + 4, bass.ds(c * 512, 512)]
            sp.dma_start(ada_raw[:, h], src).then_inc(ada_landed[h], 16)

        def ada_sum(pe, number):
            pe.wait_ge(ada_step, number * 8 + 16)
            pe.wait_ge(ada_kept, number + 1)
            for q in range(4):
                last = nc.tensor.matmul(ps[:, 6, q:q + 1], ada_acc[:, q * P:(q + 1) * P],
                                        ones[:, 0:1], start=True, stop=True)
            last.then_inc(ada_cols, 1)

        def ada_unit(dve, number, h):
            dve.wait_ge(ada_landed[h], number * 16 + 16)
            for k in range(4):
                step = number * 8 + (8 + 4 * h + k)
                w, s = ada_raw[:, h, k], cond[:, 4 * h + k:4 * h + k + 1]
                if h == 0 and k == 0:
                    ins = nc.vector.tensor_scalar(ada_acc[:], w, s, None, ALU.mult)
                else:
                    dve.wait_ge(ada_step, step)
                    ins = nc.vector.scalar_tensor_tensor(out=ada_acc[:], in0=w, scalar=s, in1=ada_acc[:],
                                                         op0=ALU.mult, op1=ALU.add)
                ins.then_inc(ada_step, 1)

        def late_steps(dve, last, chunk):
            for h in range(2):
                if chunk is not None:
                    ada_unit(dve, chunk[0], h)
                dve_step(dve, last - 1 + h)

        def ada_keep(dve, chunk):
            number, layer, c = chunk
            dve.wait_ge(ada_cols, number + 1)
            at = bass.ds(c * 4 + 48 * layer, 4)
            nc.vector.tensor_tensor(modT[:, at], ps[:, 6, 0:4], ada_bT[:, at], ALU.add).then_inc(ada_kept, 1)

        def mlp_dve(dve, m):
            u0 = U_MLP[m]

            def lo_of(par_, chunk):
                dve.wait_ge(hid_hi, chunk + 1)
                nc.vector.tensor_tensor(hid(hidl, par_).rearrange("p k n -> p (k n)"), sqr[:],
                                        hid(hidh, par_).rearrange("p k n -> p (k n)").bitcast(F32),
                                        ALU.subtract).then_inc(hid_lo, 1)

            dve_step(dve, u0)
            dve_step(dve, u0 + 1)
            ada_keep(dve, ADA_HEAD[m])
            lo_of(0, 8 * m)

            def body(u, s, js, chunk, ada):
                for j in js:
                    if ada is not None and j % 2 == 0:
                        ada_unit(dve, ada[j // 4][0], j // 2 % 2)
                    dve_step(dve, u + j, j=s + j)
                    if j % 4 == 1:
                        lo_of(1 - j // 4, chunk + j // 4)
                    if ada is not None and j in (3, 7):
                        ada_keep(dve, ada[j // 7])

            with nc.vector.Fori(0, 3, 1) as i:
                body(8 * i + (u0 + 2), u0 + 2, range(8), 2 * i + (8 * m + 1),
                     ada_loop(m, i) if m < 2 else None)
            for j in range(4 if m < 2 else 3):
                if j < 2:
                    ada_unit(dve, ADA_TAIL[m][0], j)
                dve_step(dve, u0 + 26 + j)
                if j == 1:
                    lo_of(1, 8 * m + 7)
                if j == 2:
                    ada_keep(dve, ADA_TAIL[m])

        def mlp_sp(sp, m, w1, w2, ada_free):
            u0 = U_MLP[m]
            v1, v2 = rows3(w1), rows3(w2)

            def first(n, j, c, h):
                load(sp, n, v1[:, 4 * h:4 * h + 4, bass.ds(c * 512, 512)], j)

            def second(n, j, c, h):
                load(sp, n, v2[:, bass.ds(c * 4, 4), h * 512:h * 512 + 512], j)

            for h in range(2):
                first(u0 + h, u0 + h, 0, h)
            for h in range(2):
                first(u0 + 2 + h, u0 + 2 + h, 1, h)
            sp.wait_ge(*ada_free)
            for h in range(2):
                ada_load(sp, ADA_HEAD[m], h)
            for h in range(2):
                second(u0 + 4 + h, u0 + 4 + h, 0, h)
            with nc.sync.Fori(0, 3, 1) as i:
                n, s = 8 * i + (u0 + 6), u0 + 6
                for j in range(8):
                    c = 2 * i + (2, 1, 3, 2)[j // 2]
                    (first, second)[j // 2 % 2](n + j, s + j, c, j % 2)
                    if m < 2 and j % 2 == 0:
                        ada_load(sp, ada_loop(m, i)[j // 4], j // 2 % 2)
            for h in range(2):
                second(u0 + 30 + h, u0 + 30 + h, 7, h)
                ada_load(sp, ADA_TAIL[m], h)

        ada_bT = par("ada_b", 0, 96)
        conv_tap = sem("conv_tap")
        qsq = big("qsq", 24576, [P, TT, 512])

        PAIRS = AT_HEADS // 2
        query_tiles = (slice(0, P), slice(P, 384))
        softmax_rows = [(i, c) for c in query_tiles for i in range(2)]

        def s_col(pair_, j, n):
            at = 320 + 16 * (pair_ % 2) + j
            return stat[:, at:at + n]

        def mod_shift(layer, vec, k):
            return modT[:, (layer * 6 + vec) * 8 + k:(layer * 6 + vec) * 8 + k + 1]

        def mod_scale(layer, vec, k):
            return mod_shift(layer, vec + 1, k)

        PAR_SRC = (("g_mix_pre", g_mix_pre), ("g_ff_pre", g_ff_pre), ("mix_g", mix_norm_g_2),
                   ("mlp_g", mlp_norm_g_2), ("conv_b_in", conv_b_in_2), ("conv_dw_b", conv_dw_b_2),
                   ("conv_ln_g", conv_ln_g_2), ("conv_ln_b", conv_ln_b_2), ("pool_scale", pool_scale),
                   ("c", c_2), ("ada_b", ada_b_2), ("conv_dw", conv_dw_2))
        N_PAR_DMAS = len(PAR_SRC) + 2
        N_MISC_DMAS = 10

        def conv_out_part(dve, k):
            dve.wait_ge(cs_sig, k + 1)
            nc.vector.scalar_tensor_tensor(out=cxc[:, k], in0=cxc[:, k], scalar=par("conv_ln_b", k),
                                           in1=csg[:, k % 2, 0], op0=ALU.add, op1=ALU.mult).then_inc(cs_y, 1)
            dve.wait_ge(hT_hi, 32 + k + 1)
            nc.vector.tensor_tensor(hTl[:, k], cxc[:, k], hTh[:, k].bitcast(F32),
                                    ALU.subtract).then_inc(hT_lo, 1)

        def chunk_bank(g):
            return 2 * (g % 2)

        def pair(bank):
            return ps[:, bank:bank + 2]

        def row(v, n=D):
            return v.partition_broadcast(P)

        block = ctx.enter_context(nc.Block())

        @block.sync
        def _(sp):
            sp.dma_start(X[:], x.rearrange("a (t p) d -> p (a t) d", p=P)).then_inc(x_in, 16)
            sp.dma_start(cst[:], consts).then_inc(cst_in, 16)
            win = rows3(w_in[0])
            for c in range(4):
                for h in range(2):
                    load(sp, 2 * c + h, win[:, 4 * h:4 * h + 4, 512 * c:512 * c + 512])
                    if c == 1:
                        ada_load(sp, ADA_IN[0], h)
                    elif c == 2:
                        ada_load(sp, ADA_IN[1], h)
            load(sp, U_GV, win[:, :, 2048:2304])
            for c in range(6):
                for h in range(2):
                    n = 2304 + 512 * c
                    load(sp, U_GATE + 2 * c + h, win[:, 4 * h:4 * h + 4, n:n + 512])
            for c in range(2):
                load(sp, U_BR + c, rows3(w_br_sb[0])[:, :, 512 * c:512 * c + 512])
            load(sp, U_BR + 2, rows3(w_br_pool[0]))
            load(sp, U_BR + 3, rows3(w_br_gm[0]))

            def square(first, w):
                for c in range(2):
                    for h in range(2):
                        load(sp, first + 2 * c + h, rows3(w)[:, 4 * h:4 * h + 4, 512 * c:512 * c + 512])

            square(U_OUT, w_out[0])
            mlp_sp(sp, 0, w_ff_in[0], w_ff_out[0], (o_lo, 8))
            for c in range(4):
                for h in range(2):
                    load(sp, U_CIN + 2 * c + h,
                         rows3(conv_w_in_2[0])[:, :, D * h + SEQ * c:D * h + SEQ * c + SEQ])
            square(U_COUT, conv_w_out_2[0])
            mlp_sp(sp, 1, mlp_w1_2[0], mlp_w2_2[0], (conv_ok, 1))
            for c in range(6):
                for h in range(2):
                    load(sp, U_QKV + 2 * c + h,
                         rows3(attn_w_qkv_2[0])[:, 4 * h:4 * h + 4, 512 * c:512 * c + 512])
                    if 2 <= c:
                        ada_load(sp, ADA_QKV[c - 2], h)
            square(U_WO, attn_w_o_2[0])
            mlp_sp(sp, 2, mlp_w1_2[1], mlp_w2_2[1], (s_z, AT_HEADS))
            for tt in range(TT):
                sp.wait_ge(x_ver, 2 * 5 + tt + 1)
                sp.dma_start(out[0, tt * P:(tt + 1) * P, :], X[:, tt]).then_inc(out_sem, 16)
            sp.wait_ge(out_sem, 32)

        @block.tensor
        def _(pe):
            pe.wait_ge(par_in, 16 * N_PAR_DMAS)
            pe.wait_ge(cst_in, 16)
            for g, (at, n) in enumerate(((0, N_MISC), (128, 96), (256, 124), (380, 124))):
                nc.tensor.transpose(ps[:, 0, at:at + n], prow[0:n, g], ident[0:n, 0:n])
            for g in range(4):
                last = nc.tensor.transpose(ps[:, 1, g * P:(g + 1) * P], wsrow[:, g], ident)
            last.then_inc(par_tr, 1)
            norm_pe(pe, 0)

            for c, bank in ((0, 0), (1, 2)):
                if c == 0:
                    pe.wait_ge(hT_lo, 4)
                unit_w(pe, 2 * c, None, hTh, hTl, 0, bank, True)
                if c == 0:
                    pe.wait_ge(hT_lo, 8)
                else:
                    ada_sum(pe, 0)
                unit_w(pe, 2 * c + 1, None, hTh, hTl, 4, bank, False)
            for h in range(2):
                unit_x(pe, U_V + h, None, hTh, hTl, 4 * h, lambda tt, c: ps[:, 4 + tt], h == 0)
            ada_sum(pe, 1)
            pe.wait_ge(qkv_kept, 1)
            unit_w(pe, U_PU, None, hTh, hTl, 0, 0, True)
            unit_w(pe, U_PU + 1, None, hTh, hTl, 4, 0, False)
            pe.wait_ge(kT_kept, 1)
            unit_x(pe, U_GV, None, hTh, hTl, 0, lambda tt, c: ps[:, 2, tt * SEQ:(tt + 1) * SEQ],
                   True, nk=8, cols=SEQ)

            def scores(h):
                if h == 0:
                    pe.wait_ge(qkv_kept, 2)
                if h >= 2:
                    pe.wait_ge(arg_done, h - 1)
                r = slice(HD * (h % 2), HD * (h % 2) + HD)
                k = h // 2
                nc.tensor.matmul(ps[:, 4 + h % 2, 0:SEQ], kT[r, k, 0:P], qT[r, k, :], start=True,
                                 stop=False, skip_group_check=True)
                nc.tensor.matmul(ps[:, 4 + h % 2, SEQ:384], kT[r, k, P:SEQ], qT[r, k, P:SEQ],
                                 start=False, stop=False, skip_group_check=True).then_inc(z_done, 1)

            def suffix(h):
                pe.wait_ge(lnot_done, h + 1)
                if h >= 1:
                    pe.wait_ge(arg_done, h)
                t = sbt[:, h % 2, 1]
                mm(pe, ps[:, 6, 0:SEQ], tri, t[:, 0:SEQ], True)
                mm(pe, ps[:, 6, P:SEQ], ones, t[:, SEQ:384])
                mm(pe, ps[:, 6, SEQ:384], tri, t[:, SEQ:384]).then_inc(sfx_done, 1)

            def values(h):
                pe.wait_ge(a_done, h + 1)
                if h >= 2 and h % 2 == 0:
                    pe.wait_ge(o_lo, h // 2)
                a = sbt[:, h % 2, 2]
                r, at = slice(HD * (h % 2), HD * (h % 2) + HD), (h // 2 % 2) * SEQ
                v = slice(h * HD, h * HD + HD)
                mm(pe, ps[r, 7, at:at + SEQ], vS[:, 0, v], a[:, 0:SEQ], True)
                mm(pe, ps[r, 7, at + P:at + SEQ], vS[:, 1, v], a[:, SEQ:384]).then_inc(av_done, 1)

            for s in range(12):
                g = s // 2
                bank = chunk_bank(g)
                if s == 0:
                    pe.wait_ge(p_kept, 1)
                    pe.wait_ge(gelu_dve, 2)
                elif s == 2:
                    pe.wait_ge(gelu_dve, 4)
                elif s % 2 == 0:
                    pe.wait_ge(gate_kept, g - 1)
                unit_x(pe, U_GATE + s, None, hTh, hTl, 4 * (s % 2), lambda tt, c: ps[:, bank + tt],
                       s % 2 == 0)
                if s < SB_HEADS:
                    scores(s)
                if 1 <= s < SB_HEADS + 1:
                    suffix(s - 1)
                if 2 <= s < SB_HEADS + 2:
                    values(s - 2)
                if s == 9:
                    pe.wait_ge(pool_in, 1)
                    pe.wait_ge(misc_in, 16 * N_MISC_DMAS)
                    pe.wait_ge(arg_done, SB_HEADS)
                    for i in range(2):
                        last = mm(pe, ps[:, 5, i * SEQ:(i + 1) * SEQ], wpd[:, i], pp[:, i, 16:16 + SEQ], True)
                    last.then_inc(mix_done, 1)
                    pe.wait_ge(vn_ok, 1)
                    for g4 in range(4):
                        r = slice(HD * (g4 % 2), HD * (g4 % 2) + HD)
                        for tt in range(TT):
                            at = (g4 // 2) * SEQ + tt * P
                            last = mm(pe, ps[r, 6, at:at + P], gv[:, tt, g4 * HD:(g4 + 1) * HD],
                                      wsT[:, g4], True)
                    last.then_inc(mix_done, 1)

            pe.wait_ge(gate_kept, 6)
            pe.wait_ge(o_lo, 6)
            for c in range(2):
                unit_x(pe, U_BR + c, None, hidh, hidl, 0, lambda tt, _, c=c: ps[:, 2 * c + tt], True)
            pe.wait_ge(o_lo, 8)
            unit_x(pe, U_BR + 2, None, hidh, hidl, 4, lambda tt, c: ps[:, 4 + 2 * c + tt], True, nk=2)
            pe.wait_ge(br_done, 2)
            unit_x(pe, U_BR + 3, None, hidh, hidl, 6, lambda tt, c: ps[:, 2 * c + tt], True, nk=2)
            transposes(pe, lambda tt, k: gate[:, k // 4, tt, (k % 4) * P:(k % 4 + 1) * P],
                       (merged, 2))

            def square(first, b, whole=False):
                for c in range(2):
                    for h in range(2):
                        if c == 0:
                            pe.wait_ge(hT_lo, 8 * b + (8 if whole else 4 * h + 4))
                        unit_x(pe, first + 2 * c + h, None, hTh, hTl, 4 * h,
                               lambda tt, _, c=c: y_bank(tt, c), h == 0, final=c == 1 and h == 1)

            square(U_OUT, 1)
            norm_pe(pe, 1)
            mlp_pe(pe, 0)

            norm_pe(pe, 2)
            pe.wait_ge(hT_lo, 32)
            for c in range(4):
                if c >= 2:
                    pe.wait_ge(u_ok, 2 * (c - 1))
                for h in range(2):
                    unit_w(pe, U_CIN + 2 * c + h, None, hTh, hTl, 0, chunk_bank(c) + h, True, nk=8)
                if c == 0:
                    gate_row(pe, 0, 0)
            pe.wait_ge(conv_ok, 1)
            pe.wait_ge(row_kept, 1)
            for k in range(KT):
                last = mm(pe, ps[:, 4, 0:SEQ], ones, cacc[:, k], k == 0)
            last.then_inc(cs_sum, 1)
            pe.wait_ge(cs_sq, 1)
            for k in range(KT):
                last = mm(pe, ps[:, 5, 0:SEQ], ones, cacc[:, k], k == 0)
            last.then_inc(cs_sum, 1)
            square(U_COUT, 4)
            norm_pe(pe, 3)
            mlp_pe(pe, 1)

            norm_pe(pe, 4)

            def qkv(c, between=lambda: None):
                if c >= 2:
                    pe.wait_ge(qk_kept, c - 1)
                for h in range(2):
                    if c == 0:
                        pe.wait_ge(hT_lo, 48 + 4 * h + 4)
                    unit_x(pe, U_QKV + 2 * c + h, None, hTh, hTl, 4 * h,
                           lambda tt, _: ps[:, chunk_bank(c) + tt], h == 0)
                    if h == 0:
                        between()

            def qk_transposes(src, first):
                pe.wait_ge(qk_n, 1 + first // 4)
                for f in range(4):
                    if first + f >= 2:
                        pe.wait_ge(qk_T, first + f - 1)
                    for k in (2 * f, 2 * f + 1):
                        for tt in range(TT):
                            at = (k % 2) * SEQ + tt * P
                            last = nc.tensor.transpose(ps[:, 6 + f % 2, at:at + P],
                                                       src[:, tt, k * P:(k + 1) * P], ident)
                    last.then_inc(qk_tr, 1)

            def first_unit_done():
                ada_sum(pe, ADA_QKV[0][0])
                pe.wait_ge(ada_kept, 18 + 2)
                gate_row(pe, 1, 0)

            def between_4():
                ada_sum(pe, ADA_QKV[3][0])
                pe.wait_ge(ada_kept, 22 + 1)
                qk_transposes(Qs, 0)

            qkv(0)
            qkv(1, first_unit_done)
            pe.wait_ge(row_kept, 3)
            qkv(2, lambda: ada_sum(pe, ADA_QKV[1][0]))
            qkv(3, lambda: ada_sum(pe, ADA_QKV[2][0]))
            qkv(4, between_4)
            qk_transposes(Ks, 4)
            qkv(5)
            for s in range(PAIRS + 3):
                if s < PAIRS:
                    if s == 0:
                        pe.wait_ge(qk_T, 8)
                    if s >= 2:
                        pe.wait_ge(s_arg, 2 * (s - 1))
                    for i in range(2):
                        b, r = 4 + 2 * (s % 2) + i, slice(HD * i, HD * i + HD)
                        mm(pe, ps[:, b, 0:P], qT2[r, s, 0:P], kT2[r, s, 0:P], True)
                        mm(pe, ps[:, b, P:384], qT2[r, s, P:SEQ], kT2[r, s, :]).then_inc(s_z, 1)
                if 2 <= s < PAIRS + 2:
                    k = s - 2
                    pe.wait_ge(s_p, 2 * k + 2)
                    if k == 0:
                        pe.wait_ge(qk_kept, 6)
                    else:
                        pe.wait_ge(s_pT, k)
                    for i in range(2):
                        for q in range(3):
                            c = slice(q * P, (q + 1) * P)
                            last = nc.tensor.transpose(ps[:, 2 + i, c], aS[:, k % 3, i, c], ident)
                    last.then_inc(s_tr, 1)
                if s >= 3:
                    k = s - 3
                    pe.wait_ge(s_pT, k + 1)
                    if k >= 2:
                        pe.wait_ge(hT_lo, 56 + k - 1)
                    for i in range(2):
                        r, v = slice(HD * i, HD * i + HD), slice((2 * k + i) * HD, (2 * k + i + 1) * HD)
                        mm(pe, ps[r, k % 2, 0:SEQ], Vs[:, 0, v], aT[:, k % 2, i, 0:SEQ], True)
                        last = mm(pe, ps[r, k % 2, P:SEQ], Vs[:, 1, v], aT[:, k % 2, i, SEQ:384])
                    last.then_inc(s_o, 1)
            square(U_WO, 7, True)
            norm_pe(pe, 5)
            mlp_pe(pe, 2)

        @block.scalar
        def _(act):
            for name, src in PAR_SRC:
                at, n = PARAMS[name]
                if name == "conv_dw":
                    v = src.rearrange("a t (k p) -> (a t k) p", p=P)
                    for g in range(2):
                        act.dma_start(prow[0:124, 2 + g], v[124 * g:124 * g + 124]).then_inc(par_in, 16)
                else:
                    v = src.rearrange("a (k p) -> (a k) p", p=P)
                    act.dma_start(prow[at % P:at % P + n, at // P], v).then_inc(par_in, 16)
            act.dma_start(wsrow[:], w_spatial[0].rearrange("g t p -> t g p")).then_inc(par_in, 16)
            act.dma_start(inv[:], inv_count).then_inc(misc_in, 16)
            act.dma_start(gm_row[:], row(gm_gain[0])).then_inc(misc_in, 16)
            for g in range(4):
                r = slice(HD * (g % 2), HD * (g % 2) + HD)
                act.dma_start(bsp[r, g // 2], b_spatial[0, g].partition_broadcast(HD)).then_inc(misc_in, 16)
            act.wait_ge(pad_ok, 1)
            for g in range(4):
                r = slice(HD * (g % 2), HD * (g % 2) + HD)
                act.dma_start(wpd[r, g // 2, r], w_pool[0, g]).then_inc(misc_in, 16)
            for i, g in enumerate((attn_q_norm_g_2, attn_k_norm_g_2)):
                for half in range(2):
                    act.dma_start(qk_gain[HD * half:HD * half + HD, i:i + 1],
                                  g.rearrange("a d -> d a")).then_inc(qk_gain_in, 16)

            act.wait_ge(x_in, 16)
            act.wait_ge(par_ok, 1)
            for n in range(RING):
                split_hi(act, n, n)
            norm_act(act, 0, 0, 0, None, lambda k: par("g_mix_pre", k), lambda k: 0.0)
            nc.scalar.activation(cond[:, 8:16], par("c", 0, 8), ACT.Sigmoid).then_inc(cond_sig, 1)

            act_step(act, 0)
            act_step(act, 1)
            nc.scalar.activation(qT[:].rearrange("p k n -> p (k n)"),
                                 pair(0).rearrange("p b n -> p (b n)"), ACT.Copy).then_inc(qkv_kept, 1)
            for u in range(2, 6):
                act_step(act, u)
            act.wait_ge(ada_step, 8 + 8 * 2)
            nc.scalar.activation(vS[:], pair(4), ACT.Copy).then_inc(qkv_kept, 1)
            act_step(act, 6)
            act_step(act, 7)

            def gelu_parts(i, x):
                nc.scalar.activation(gt[:, 0], x, ACT.Square).then_inc(gelu_act, 1)
                act.wait_ge(gelu_dve, 2 * i + 1)
                nc.scalar.activation(gt[:, 1], gt[:, 0], ACT.Sigmoid, scale=GELU_2C).then_inc(gelu_act, 1)

            act.wait_ge(pad_ok, 1)
            nc.scalar.activation(pp[:, :, 16:16 + SEQ], ps[:, 0].rearrange("p (k n) -> p k n", k=2),
                                 ACT.Copy).then_inc(p_kept, 1)
            gelu_parts(0, ps[:, 1])
            act_step(act, 8)
            act.wait_ge(gelu_dve, 2)
            gelu_parts(1, ps[:, 2])
            nc.scalar.preload_act_table_set("natural_log_exp_and_others")

            def softplus(h):
                act.wait_ge(z_done, h + 1)
                if h < 2:
                    act.wait_ge(pool_in, 1)
                else:
                    act.wait_ge(arg_done, h - 1)
                t = sbt[:, h % 2, 0]
                nc.scalar.activation(t, ps[:, 4 + h % 2, 0:384], ACT.Abs, scale=SCALE).then_inc(abs_done, 1)
                act.wait_ge(abs_done, h + 1)
                link_act(act, nc.scalar.activation(t, t, ACT.Exp, scale=-1.0))
                nc.scalar.activation(t, t, ACT.Ln, bias=1.0).then_inc(soft_done, 1)

            def o_split(k, bank, cols):
                nc.scalar.activation(hidh[:, k], ps[:, bank, cols], ACT.Copy).then_inc(o_hi, 1)

            for s in range(12):
                act_step(act, U_GATE + s)
                if s < SB_HEADS:
                    softplus(s)
                if 1 <= s < SB_HEADS + 1:
                    h = s - 1
                    act.wait_ge(arg_done, h + 1)
                    a = sbt[:, h % 2, 2]
                    nc.scalar.activation(a, a, ACT.Exp).then_inc(a_done, 1)
                if s % 2 and s >= 3 and s < SB_HEADS + 2:
                    k = (s - 3) // 2
                    act.wait_ge(av_done, 2 * k + 2)
                    o_split(k, 7, slice((k % 2) * SEQ, (k % 2 + 1) * SEQ))
                if s % 2:
                    g = s // 2
                    nc.scalar.activation(gate[:, g], pair(chunk_bank(g)), ACT.Copy).then_inc(gate_kept, 1)
            act.wait_ge(o_val, 1)
            for k in range(2):
                nc.scalar.activation(hidh[:, 6 + k], gt[:, 0, k * SEQ:(k + 1) * SEQ], ACT.Copy).then_inc(o_hi, 1)
            act.wait_ge(mix_done, 1)
            for k in range(2):
                nc.scalar.activation(hidh[:, 4 + k], ps[:, 5, k * SEQ:(k + 1) * SEQ], ACT.Copy,
                                     scale=par("pool_scale", k)).then_inc(o_hi, 1)
            act.wait_ge(gate_kept, 6)
            for g in range(6):
                nc.scalar.activation(gate[:, g], gate[:, g], ACT.Sigmoid).then_inc(gate_sig, 1)
            for u in range(U_BR, U_OUT):
                act_step(act, u)
            act.wait_ge(used, U_BR)
            hT_act(act, 1, 1, lambda k: 1.0, lambda k: 0.0)
            for u in range(U_OUT, U_OUT + 2):
                act_step(act, u)
            post_act(act, 0, U_OUT + 3)
            norm_act(act, 1, 2, 2, U_OUT + 4, lambda k: par("g_ff_pre", k), lambda k: 0.0)
            mlp_act(act, 0)
            post_act(act, 1, U_MLP[0] + 31)

            def mod_norm(norm, fill, b, free, layer, vec):
                act.wait_ge(mod_ok, norm - 1)
                norm_act(act, norm, fill, b, free, lambda k: mod_scale(layer, vec, k),
                         lambda k: mod_shift(layer, vec, k), mod=norm - 2)

            mod_norm(2, 3, 3, U_CIN, 0, 0)
            for c in range(4):
                for h in range(2):
                    act_step(act, U_CIN + 2 * c + h)
                for i in range(2):
                    if c >= 2:
                        act.wait_ge(u_ok, 2 * (c - 2) + i + 1)
                    nc.scalar.activation(csg[:, c % 2, i], ps[:, chunk_bank(c) + 1, i * SEQ:(i + 1) * SEQ],
                                         ACT.Sigmoid, bias=par("conv_b_in", 8 + 2 * c + i)).then_inc(glu_sig, 1)
                if c == 0:
                    keep_row(act, 0, 0)
            act.wait_ge(cs_xc, 1)
            act.wait_ge(cs_sum, 1)
            nc.scalar.activation(cacc[:].rearrange("p k n -> p (k n)"),
                                 cxc[:].rearrange("p k n -> p (k n)"), ACT.Square).then_inc(cs_sq, 1)
            for k in range(KT):
                act.wait_ge(cs_ln, k + 1)
                nc.scalar.activation(csg[:, k % 2, 0], cxc[:, k], ACT.Sigmoid,
                                     bias=par("conv_ln_b", k)).then_inc(cs_sig, 1)
                act.wait_ge(cs_y, k + 1)
                nc.scalar.activation(hTh[:, k], cxc[:, k], ACT.Copy).then_inc(hT_hi, 1)
            for u in range(U_COUT, U_COUT + 2):
                act_step(act, u)
            mod_norm(3, 4, 5, U_COUT + 4, 0, 3)
            mlp_act(act, 1)

            mod_norm(4, 5, 6, U_QKV, 1, 0)

            def keep_qkv(c, between=lambda: None):
                act_step(act, U_QKV + 2 * c)
                between()
                act_step(act, U_QKV + 2 * c + 1)
                dst = (Qs, Ks, Vs)[c // 2]
                if c < 4:
                    if c:
                        act.wait_ge(qk_ss, c)
                    nc.scalar.activation(qsq[:], pair(chunk_bank(c)), ACT.Square).then_inc(qk_sq, 1)
                nc.scalar.activation(dst[:, :, (c % 2) * 512:(c % 2 + 1) * 512], pair(chunk_bank(c)),
                                     ACT.Copy).then_inc(qk_kept, 1)

            def keep_T(dst, i, first):
                for f in range(4):
                    act.wait_ge(qk_tr, first + f + 1)
                    nc.scalar.activation(dst[:, 2 * f:2 * f + 2].rearrange("p k n -> p (k n)"),
                                         ps[:, 6 + f % 2], ACT.Copy,
                                         scale=qk_gain[:, i:i + 1]).then_inc(qk_T, 1)

            keep_qkv(0)
            keep_qkv(1, lambda: keep_row(act, 1, 0))
            keep_qkv(2)
            keep_qkv(3)
            act.wait_ge(qk_gain_in, 64)
            keep_qkv(4, lambda: keep_T(qT2, 0, 0))
            keep_T(kT2, 1, 4)
            keep_qkv(5)
            for s in range(1, PAIRS + 4):
                if s < PAIRS + 1:
                    k = s - 1
                    act.wait_ge(s_max, k + 1)
                    for j, (i, c) in enumerate(softmax_rows):
                        a = aS[:, k % 3, i, c]
                        nc.scalar.activation(a, a, ACT.Exp, scale=SCALE, bias=s_col(k, 4 + j, 1),
                                             accum_out=s_col(k, 8 + j, 1)).then_inc(s_exp, 1)
                if 2 <= s < PAIRS + 2:
                    k = s - 2
                    act.wait_ge(s_tr, k + 1)
                    if k >= 2:
                        act.wait_ge(s_o, k - 1)
                    nc.scalar.activation(aT[:, k % 2], ps[:, 2:4, 0:384], ACT.Copy).then_inc(s_pT, 1)
                if s >= 4:
                    k = s - 4
                    act.wait_ge(s_o, k + 1)
                    nc.scalar.activation(hTh[:, k], ps[:, k % 2, 0:SEQ], ACT.Copy).then_inc(hT_hi, 1)
            for u in range(U_WO, U_WO + 2):
                act_step(act, u)
            mod_norm(5, 6, 8, U_WO + 4, 1, 3)
            mlp_act(act, 2)

        @block.vector
        def _(dve):
            nc.vector.sem_inc(ada_step, 8)
            nc.vector.sem_inc(ada_kept, 1)
            dve.wait_ge(par_tr, 1)
            dve.wait_ge(cst_in, 16)
            for at, n in ((0, N_MISC), (128, 96), (256, 248)):
                link(dve, nc.vector.tensor_copy(pcol[:, at:at + n], ps[:, 0, at:at + n]))
            for g in range(4):
                link(dve, nc.vector.tensor_tensor(wsT[:, g], ps[:, 1, g * P:(g + 1) * P], keep, ALU.mult))
            dve_inc(par_ok)
            norm_dve(dve, 0)
            hT_dve(dve, 0, 0, lambda k: par("g_mix_pre", k), None)
            for n in range(RING):
                split_lo(dve, n, n)
            dve.wait_ge(cond_sig, 1)
            link(dve, nc.vector.tensor_tensor(cond[:, 0:8], cond[:, 8:16], par("c", 0, 8), ALU.mult))
            for u in range(8):
                if u < 4:
                    ada_unit(dve, u // 2, u % 2)
                dve_step(dve, u)
                if u == 1:
                    ada_keep(dve, ADA_IN[0])
                if u == 3:
                    dve.wait_ge(used, 4)
                    nc.vector.tensor_copy(kT[:].rearrange("p k n -> p (k n)"),
                                          pair(2).rearrange("p b n -> p (b n)")).then_inc(kT_kept, 1)
            ada_keep(dve, ADA_IN[1])

            def gelu(i, x, dst):
                dve.wait_ge(gelu_act, 2 * i + 1)
                link(dve, nc.vector.tensor_scalar(gt[:, 0], gt[:, 0], GELU_A, 1.0, ALU.mult, ALU.add))
                nc.vector.tensor_tensor(gt[:, 0], gt[:, 0], x, ALU.mult).then_inc(gelu_dve, 1)
                dve.wait_ge(gelu_act, 2 * i + 2)
                nc.vector.tensor_tensor(dst, gt[:, 1], x, ALU.mult).then_inc(gelu_dve, 1)

            gelu(0, ps[:, 1], gu[:].rearrange("p k n -> p (k n)"))
            dve_step(dve, 8)
            gelu(1, ps[:, 2], gv[:].rearrange("p t n -> p (t n)"))
            dve.wait_ge(gelu_dve, 4)
            dve.wait_ge(misc_in, 16 * N_MISC_DMAS)
            for tt in range(TT):
                link(dve, nc.vector.scalar_tensor_tensor(out=gt[:, 2, 0:SEQ], in0=gv[:, tt], scalar=1.0,
                                                         in1=gv[:, tt], op0=ALU.mult, op1=ALU.mult,
                                                         accum_out=stat[:, tt:tt + 1]))
            rsqrt(dve, N_Y, N_SS, N_V, N_A, SEQ)
            for tt in range(TT):
                link(dve, nc.vector.scalar_tensor_tensor(out=gv[:, tt], in0=gv[:, tt],
                                                         scalar=stat[:, 8 + tt:9 + tt], in1=gm_row[:],
                                                         op0=ALU.mult, op1=ALU.mult))
            dve.wait_ge(p_kept, 1)
            src, total = pp, gt[:, 2].rearrange("p (k n) -> p k n", k=2)
            for g, w in enumerate(WINDOWS):
                dst, at = (pa, pb)[g % 2], w - 1
                link(dve, nc.vector.tensor_tensor(dst[:, :, at:], src[:, :, at:],
                                                  src[:, :, at - w // 2:16 + SEQ - w // 2], ALU.add))
                r = slice(HD * (g % 2), HD * (g % 2) + HD)
                link(dve, nc.vector.tensor_tensor(total[r, g // 2], dst[r, g // 2, 16:],
                                                  inv[r, g // 2], ALU.mult))
                src = dst
            nc.vector.tensor_tensor(pp[:, :, 16:], total, pp[:, :, 16:], ALU.subtract).then_inc(pool_in, 1)
            dve_inc(vn_ok)

            def diagonals(t):
                return t.rearrange("p (b n) -> p b n", b=3)[:, 0:3:2, :]

            def log_not(h):
                z = ps[:, 4 + h % 2, 0:384]
                t1, t2, t3 = (sbt[:, h % 2, i] for i in range(3))
                dve.wait_ge(abs_done, h + 1)
                if h >= 2:
                    dve.wait_ge(av_done, h - 1)
                link(dve, nc.vector.tensor_scalar(t2, z, SCALE, 0.0, ALU.mult, ALU.max))
                dve.wait_ge(soft_done, h + 1)
                link(dve, nc.vector.scalar_tensor_tensor(out=t2, in0=t2, scalar=-1.0, in1=t1,
                                                         op0=ALU.mult, op1=ALU.subtract))
                m2 = m01.unsqueeze(1).broadcast_to([P, 2, P])
                n2 = neg.unsqueeze(1).broadcast_to([P, 2, P])
                link(dve, nc.vector.tensor_tensor(diagonals(t2), diagonals(t2), m2, ALU.mult))
                dve_inc(lnot_done)
                link(dve, nc.vector.scalar_tensor_tensor(out=t3, in0=z, scalar=SCALE, in1=t2,
                                                         op0=ALU.mult, op1=ALU.add))
                link(dve, nc.vector.tensor_tensor(diagonals(t3), diagonals(t3), n2, ALU.add))

            for s in range(12):
                dve_step(dve, U_GATE + s)
                if 1 <= s < SB_HEADS + 1:
                    h = s - 1
                    dve.wait_ge(sfx_done, h + 1)
                    t3 = sbt[:, h % 2, 2]
                    nc.vector.tensor_tensor(t3, t3, ps[:, 6, 0:384], ALU.add).then_inc(arg_done, 1)
                if s < SB_HEADS:
                    log_not(s)
                if s % 2 and s >= 3 and s < SB_HEADS + 2:
                    k = (s - 3) // 2
                    dve.wait_ge(o_hi, k + 1)
                    nc.vector.tensor_tensor(hidl[:, k], ps[:, 7, (k % 2) * SEQ:(k % 2 + 1) * SEQ],
                                            hidh[:, k].bitcast(F32), ALU.subtract).then_inc(o_lo, 1)
                if s == 9:
                    dve.wait_ge(mix_done, 2)
                    for i in range(2):
                        o = gt[:, 0, i * SEQ:(i + 1) * SEQ].rearrange("p (t n) -> p t n", t=TT)
                        m = ps[:, 6, i * SEQ:(i + 1) * SEQ].rearrange("p (t n) -> p t n", t=TT)
                        link(dve, nc.vector.tensor_tensor(o, m, bsp[:, i:i + 1].broadcast_to([P, TT, P]),
                                                          ALU.add))
                    nc.vector.tensor_tensor(gt[:, 0], gt[:, 0], gu[:].rearrange("p k n -> p (k n)"),
                                            ALU.mult).then_inc(o_val, 1)
            for k in range(2):
                dve.wait_ge(o_hi, 4 + k + 1)
                nc.vector.tensor_tensor(hidl[:, 6 + k], gt[:, 0, k * SEQ:(k + 1) * SEQ],
                                        hidh[:, 6 + k].bitcast(F32), ALU.subtract).then_inc(o_lo, 1)
            for k in range(2):
                dve.wait_ge(o_hi, 8)
                nc.vector.scalar_tensor_tensor(out=hidl[:, 4 + k], in0=ps[:, 5, k * SEQ:(k + 1) * SEQ],
                                               scalar=par("pool_scale", k), in1=hidh[:, 4 + k].bitcast(F32),
                                               op0=ALU.mult, op1=ALU.subtract).then_inc(o_lo, 1)
            for c in range(2):
                dve_step(dve, U_BR + c)
                dve.wait_ge(used, U_BR + c + 1)
                dve.wait_ge(gate_sig, c + 1)
                link(dve, nc.vector.tensor_tensor(gate[:, c], gate[:, c], pair(2 * c), ALU.mult))
                dve_inc(br_done)
            for b in (1, 2):
                dve_step(dve, U_BR + b + 1)
                dve.wait_ge(used, U_BR + b + 2)
                dve.wait_ge(gate_sig, 6)
                for c in range(2):
                    g = gate[:, 2 * b + c]
                    link(dve, nc.vector.tensor_tensor(g, g, pair((4, 0)[b - 1] + 2 * c), ALU.mult))
                    ins = nc.vector.tensor_tensor(gate[:, c], gate[:, c], g, ALU.add)
                    if b == 1:
                        link(dve, ins)
                    else:
                        ins.then_inc(merged, 1)
            hT_dve(dve, 1, 1, None, None)
            for u in range(U_OUT, U_OUT + 2):
                dve_step(dve, u)
            dve.wait_ge(row_a_in, 16)
            post_dve(dve, 0, U_OUT + 3, row_a)
            norm_dve(dve, 1)
            hT_dve(dve, 2, 2, lambda k: par("g_ff_pre", k), None)
            late_steps(dve, U_OUT + 3, ADA_HEAD[0])
            mlp_dve(dve, 0)
            dve.wait_ge(row_b_in, 16)

            def mod_scales(layer, vec):
                sc = (layer * 6 + vec + 1) * 8
                g = par("mix_g" if vec == 0 else "mlp_g", 8 * layer, 8)
                link(dve, nc.vector.scalar_tensor_tensor(out=modT[:, sc:sc + 8], in0=modT[:, sc:sc + 8],
                                                         scalar=1.0, in1=g, op0=ALU.add, op1=ALU.mult))
                dve_inc(mod_ok)

            def mod_hT(fill, b, layer, vec, last, chunk=None):
                hT_dve(dve, fill, b, lambda k: mod_scale(layer, vec, k),
                       lambda k: mod_shift(layer, vec, k), mod=fill - 3)
                late_steps(dve, last, chunk)

            mod_scales(0, 0)
            post_dve(dve, 1, U_MLP[0] + 31, row_b)
            norm_dve(dve, 2)
            mod_hT(3, 3, 0, 0, U_MLP[0] + 31)
            dve.wait_ge(tr_done, 16)
            link(dve, nc.vector.memset(u_pad[:, :, 0:PAD], 0.0))
            for c in range(4):
                for i in range(2):
                    dve.wait_ge(glu_sig, 2 * c + i + 1)
                    ins = nc.vector.scalar_tensor_tensor(
                        out=u_pad[:, 2 * c + i, PAD:], in0=ps[:, chunk_bank(c), i * SEQ:(i + 1) * SEQ],
                        scalar=par("conv_b_in", 2 * c + i), in1=csg[:, c % 2, i], op0=ALU.add, op1=ALU.mult)
                    ins.then_inc(u_ok, 1)
                dve.wait_ge(u_ok, 2 * c + 2)
                for t in range(TAPS):
                    for i in range(2):
                        k = 2 * c + i
                        w = par("conv_dw", t * KT + k)
                        src = u_pad[:, k, t:t + SEQ]
                        if t == 0:
                            ins = nc.vector.tensor_scalar(cacc[:, k], src, w, par("conv_dw_b", k),
                                                          ALU.mult, ALU.add)
                        else:
                            dve.wait_ge(conv_tap, 62 * c + 2 * t - 1 + i)
                            ins = nc.vector.scalar_tensor_tensor(out=cacc[:, k], in0=src, scalar=w,
                                                                 in1=cacc[:, k], op0=ALU.mult, op1=ALU.add)
                        ins.then_inc(conv_tap, 1)
            dve.wait_ge(conv_tap, 62 * 4)
            dve_inc(conv_ok)
            dve.wait_ge(cs_sum, 1)
            mean, y, var, a = cmr[:, 0], cmr[:, 1], cmv[:, 0], cmv[:, 1]
            link(dve, nc.vector.tensor_scalar(mean, ps[:, 4, 0:SEQ], 1.0 / D, None, ALU.mult))
            nc.vector.tensor_tensor(cxc[:], cacc[:], mean.unsqueeze(1).broadcast_to([P, KT, SEQ]),
                                    ALU.subtract).then_inc(cs_xc, 1)
            dve.wait_ge(cs_sum, 2)
            rsqrt(dve, y, ps[:, 5, 0:SEQ], var, a, D)
            dve.wait_ge(cs_xc, 1)
            for k in range(KT):
                nc.vector.scalar_tensor_tensor(out=cxc[:, k], in0=cxc[:, k], scalar=par("conv_ln_g", k),
                                               in1=y, op0=ALU.mult, op1=ALU.mult).then_inc(cs_ln, 1)
                if k:
                    conv_out_part(dve, k - 1)
            conv_out_part(dve, KT - 1)
            for u in range(U_COUT, U_COUT + 2):
                dve_step(dve, u, turn=u == U_COUT)
            dve.wait_ge(pool_x, 1)
            dve.wait_ge(row_kept, 1)
            mod_scales(0, 3)
            gated_dve(dve, 2, U_COUT + 3, row_a)
            mod_hT(4, 5, 0, 3, U_COUT + 3, ADA_HEAD[1])
            mlp_dve(dve, 1)
            mod_scales(1, 0)
            dve.wait_ge(row_kept, 2)
            gated_dve(dve, 3, U_MLP[1] + 31, row_b)
            mod_hT(5, 6, 1, 0, U_MLP[1] + 31)
            for c in range(6):
                dve_step(dve, U_QKV + 2 * c, turn=c > 0)
                if 1 <= c < 5:
                    ada_keep(dve, ADA_QKV[c - 1])
                if c < 4:
                    for h in range(2):
                        ada_unit(dve, ADA_QKV[c][0], h)
                if c < 4:
                    dve.wait_ge(qk_sq, c + 1)
                    nc.vector.tensor_reduce(stat[:, 64 + 16 * c:80 + 16 * c].rearrange("p (t h) -> p t h", t=TT),
                                            qsq[:].rearrange("p t (h d) -> p t h d", d=HD), AX.X,
                                            ALU.add).then_inc(qk_ss, 1)
                if c in (1, 3):
                    dve.wait_ge(qk_ss, c + 1)
                    dve.wait_ge(qk_kept, c + 1)
                    at = 32 * (c // 2)
                    cut = [slice(base + at, base + at + 32) for base in (128, 64, 256, 192)]
                    rsqrt(dve, *(stat[:, q] for q in cut), HD)
                    src = (Qs, Ks)[c // 2]
                    for cc in range(2):
                        for tt in range(TT):
                            v = src[:, tt, cc * 512:(cc + 1) * 512].rearrange("p (h d) -> p h d", d=HD)
                            m = 128 + at + 16 * cc + 8 * tt
                            y = stat[:, m:m + 8].unsqueeze(2).broadcast_to([P, 8, HD])
                            link(dve, nc.vector.tensor_tensor(v, v, y, ALU.mult))
                    dve_inc(qk_n)
            for s in range(PAIRS + 4):
                if s < PAIRS:
                    if s >= 3:
                        dve.wait_ge(s_tr, s - 2)
                    for i in range(2):
                        dve.wait_ge(s_z, 2 * s + i + 1)
                        slope = float(np.float32(2.0 ** (-8.0 * (2 * s + i + 1) / AT_HEADS))) / SCALE
                        nc.vector.scalar_tensor_tensor(out=aS[:, s % 3, i], in0=dist, scalar=slope,
                                                       in1=ps[:, 4 + 2 * (s % 2) + i, 0:384],
                                                       op0=ALU.mult, op1=ALU.add).then_inc(s_arg, 1)
                    dve.wait_ge(s_arg, 2 * s + 2)
                    for j, c in enumerate(query_tiles):
                        ins = nc.vector.tensor_reduce(s_col(s, 2 * j, 2), aS[:, s % 3, :, c], AX.X, ALU.max)
                        link(dve, ins)
                    nc.vector.tensor_scalar(s_col(s, 4, 4), s_col(s, 0, 4), -SCALE, None,
                                            ALU.mult).then_inc(s_max, 1)
                if 1 <= s < PAIRS + 1:
                    k = s - 1
                    dve.wait_ge(s_exp, 4 * k + 4)
                    link(dve, nc.vector.reciprocal(s_col(k, 12, 4), s_col(k, 8, 4)))
                    for j, c in enumerate(query_tiles):
                        a = aS[:, k % 3, :, c]
                        y = s_col(k, 12 + 2 * j, 2).unsqueeze(2).broadcast_to([P, 2, c.stop - c.start])
                        ins = nc.vector.tensor_tensor(a, a, y, ALU.mult)
                        ins.then_inc(s_p, 1)
                if s >= 4:
                    k = s - 4
                    dve.wait_ge(hT_hi, 56 + k + 1)
                    nc.vector.tensor_tensor(hTl[:, k], ps[:, k % 2, 0:SEQ], hTh[:, k].bitcast(F32),
                                            ALU.subtract).then_inc(hT_lo, 1)
            for u in range(U_WO, U_WO + 2):
                dve_step(dve, u, turn=u == U_WO)
            mod_scales(1, 3)
            dve.wait_ge(row_kept, 3)
            gated_dve(dve, 4, U_WO + 3, row_a)
            mod_hT(6, 8, 1, 3, U_WO + 3, ADA_HEAD[2])
            mlp_dve(dve, 2)
            dve.wait_ge(row_kept, 4)
            gated_dve(dve, 5, U_MLP[2] + 31, row_b, norm=False)

        @block.gpsimd
        def _(pool):
            nc.gpsimd.memset(zero_r[:].bitcast(F32), 0.0)
            nc.gpsimd.memset(pp[:, :, 0:16], 0.0)
            link_pool(pool, nc.gpsimd.memset(wpd[:], 0.0))
            nc.gpsimd.sem_inc(pad_ok, 1)
            pool.wait_ge(o_lo, 8)
            pool.dma_start(row_a[:], row(g_mix_post[0])).then_inc(row_a_in, 16)
            pool.dma_start(row_b[:], row(g_ff_post[0])).then_inc(row_b_in, 16)
            pool.dma_start(row_c[:], row(conv_b_out_2[0])).then_inc(row_c_in, 16)
            mlp_pool(pool, 0)
            for u in range(U_CIN, U_CIN + 8):
                pool_step(pool, u)
            pool.wait_ge(row_kept, 1)
            pool.wait_ge(row_c_in, 16)
            pool.wait_ge(tr_done, 16)
            link_pool(pool, nc.gpsimd.tensor_tensor(row_c[:], row_c[:], row_a[:], ALU.mult))
            for tt in range(TT):
                link_pool(pool, nc.gpsimd.tensor_tensor(X[:, tt], X[:, tt], row_c[:], ALU.add))
            nc.gpsimd.sem_inc(pool_x, 1)
            mlp_pool(pool, 1)
            for c in range(6):
                pool_step(pool, U_QKV + 2 * c + 1)
            mlp_pool(pool, 2)


_INS = ["x", "w_in", "w_pool", "pool_scale", "gm_gain", "w_spatial", "b_spatial", "w_br_sb", "w_br_pool",
        "w_br_gm", "w_out", "g_mix_pre", "g_mix_post", "g_ff_pre", "g_ff_post", "w_ff_in", "w_ff_out",
        "c_2", "ada_w_2", "ada_b_2", "mix_norm_g_2", "mlp_norm_g_2", "conv_w_in_2", "conv_b_in_2",
        "conv_dw_2", "conv_dw_b_2", "conv_ln_g_2", "conv_ln_b_2", "conv_w_out_2", "conv_b_out_2",
        "attn_w_qkv_2", "attn_q_norm_g_2", "attn_k_norm_g_2", "attn_w_o_2", "mlp_w1_2", "mlp_w2_2"]


def kernel(**inputs):
    import concourse.bacc as bacc
    from concourse.bass_utils import run_bass_kernel_spmd

    nc = bacc.Bacc("TRN2", target_bir_lowering=False, num_devices=1)
    arrays, args = {}, []
    shapes = shape_constants()
    for name in _INS + ["consts", "inv_count"]:
        a = shapes[name == "inv_count"] if name in ("consts", "inv_count") else inputs[name]
        a = np.ascontiguousarray(a)
        arrays[f"in_{name}"] = a
        args.append(nc.dram_tensor(f"in_{name}", a.shape, mybir.dt.from_np(a.dtype),
                                   kind="ExternalInput").ap())
    args.append(nc.dram_tensor("out_x", (1, SEQ, D), F32, kind="ExternalOutput").ap())
    build_kernel(nc, *args)
    r = run_bass_kernel_spmd(nc, [arrays], core_ids=[0])
    return r.results[0]["out_x"]
```

```python
from contextlib import ExitStack

import numpy as np

import concourse.bass as bass
from concourse import mybir

ALU = mybir.AluOpType
ACT = mybir.ActivationFunctionType
AX = mybir.AxisListType
F32 = mybir.dt.float32
F32R = mybir.dt.float32r
I32 = mybir.dt.int32

P = 128
SEQ = 256
TT = SEQ // P
D = 1024
KT = D // P
UNIT = 2048
RING = 4
EPS = 1e-6
RSQRT_MAGIC = 1597463007.0
GELU_2C = 2.0 * float(np.sqrt(2.0 / np.pi))
GELU_A = 0.044715
HD = 64
SB_HEADS = 8
AT_HEADS = 16
TAPS = 31
PAD = TAPS - 1
SCALE = HD ** -0.5
NEG = -1e30
FAR = -3e37
WINDOWS = (2, 4, 8, 16)

U_Q, U_K, U_V, U_PU, U_GV, U_GATE = 0, 2, 4, 6, 8, 9
U_BR = 21
U_OUT = 25
U_MLP = (29, 73, 121)
U_CIN, U_COUT = 61, 69
U_QKV, U_WO = 105, 117
N_UNITS = 153

C_ID, C_ONE, C_TRI, C_M01, C_KEEP, C_NEG, C_DIST, C_END = 0, 128, 256, 384, 512, 640, 768, 1152

PARAMS = {}
_at = 0
for _name, _n in (("g_mix_pre", 8), ("g_ff_pre", 8), ("mix_g", 16), ("mlp_g", 16), ("conv_b_in", 16),
                  ("conv_dw_b", 8), ("conv_ln_g", 8), ("conv_ln_b", 8), ("pool_scale", 2), ("c", 8)):
    PARAMS[_name] = (_at, _n)
    _at += _n
N_MISC = _at
PARAMS["ada_b"] = (128, 96)
PARAMS["conv_dw"] = (256, TAPS * KT)
N_PCOL = 256 + TAPS * KT


def shape_constants():
    c = np.zeros((P, C_END), np.float32)
    i = np.arange(P)
    c[:, C_ID:C_ID + P] = np.eye(P)
    c[:, C_ONE:C_ONE + P] = 1.0
    c[:, C_TRI:C_TRI + P] = i[:, None] > i[None, :]
    c[:, C_M01:C_M01 + P] = i[:, None] < i[None, :]
    c[:, C_KEEP:C_KEEP + P] = i[:, None] <= i[None, :]
    c[:, C_NEG:C_NEG + P] = np.where(i[:, None] < i[None, :], 0.0, NEG)
    near = np.where(i[None, :] <= i[:, None], i[None, :] - i[:, None], FAR)
    c[:, C_DIST:C_DIST + P] = near
    c[:, C_DIST + P:C_DIST + 2 * P] = i[None, :] - i[:, None] - P
    c[:, C_DIST + 2 * P:] = near
    inv = np.zeros((P, 2, SEQ), np.float32)
    t = np.arange(SEQ) + 1.0
    for g, w in enumerate(WINDOWS):
        inv[HD * (g % 2):HD * (g % 2) + HD, g // 2] = 1.0 / np.minimum(t, float(w))
    return c, inv.reshape(P, 2 * SEQ)


def build_kernel(nc, x, w_in, w_pool, pool_scale, gm_gain, w_spatial, b_spatial, w_br_sb, w_br_pool,
                 w_br_gm, w_out, g_mix_pre, g_mix_post, g_ff_pre, g_ff_post, w_ff_in, w_ff_out,
                 c_2, ada_w_2, ada_b_2, mix_norm_g_2, mlp_norm_g_2, conv_w_in_2, conv_b_in_2,
                 conv_dw_2, conv_dw_b_2, conv_ln_g_2, conv_ln_b_2, conv_w_out_2, conv_b_out_2,
                 attn_w_qkv_2, attn_q_norm_g_2, attn_k_norm_g_2, attn_w_o_2, mlp_w1_2, mlp_w2_2,
                 consts, inv_count, out):
    ctx = ExitStack()
    with ctx:
        size = [(nc.sbuf_base + 63) // 64 * 64]

        def nbytes(shape):
            return 4 * int(np.prod(shape[1:]))

        def place(name, shape, dt=F32):
            at = size[0]
            size[0] += (nbytes(shape) + 31) // 32 * 32
            return nc.alloc_sbuf_tensor_at(name, shape, dt, offset=at)

        def area(name, n):
            start = size[0]
            size[0] += n

            def at(tile, offset, shape, dt=F32):
                assert offset + nbytes(shape) <= n, (name, tile)
                return nc.alloc_sbuf_tensor_at(tile, shape, dt, offset=start + offset)

            return at

        raw = place("raw", [P, RING, UNIT])
        hi = place("hi", [P, RING, UNIT], F32R)
        lo = place("lo", [P, RING, UNIT], F32R)
        X = place("X", [P, TT, D])
        hTh = place("hTh", [P, KT, SEQ], F32R)
        hTl = place("hTl", [P, KT, SEQ], F32R)
        hid_area = area("hid", 16384)
        cst = place("cst", [P, C_END])
        pcol = place("pcol", [P, N_PCOL])
        modT = place("modT", [P, 96])
        cond = place("cond", [P, 16])
        stat = place("stat", [P, 352])
        zero_r = place("zero_r", [P, P], F32R)
        qk_gain = place("qk_gain", [P, 2])
        ada_area = area("ada", 16384)
        row_area = area("rows", 12288)
        acc_area = area("acc", 2048)
        big = area("big", 33792)

        assert size[0] <= nc.sbuf_usable_end
        hidh = hid_area("hidh", 0, [P, 8, SEQ], F32R)
        hidl = hid_area("hidl", 8192, [P, 8, SEQ], F32R)
        ada_raw = ada_area("ada_raw", 0, [P, 2, 4, 512])
        ada_acc = acc_area("ada_acc", 0, [P, 512])
        pool_mean = acc_area("pool_mean", 0, [P, 2, SEQ])
        row_a = row_area("row_a", 0, [P, D])
        row_b = row_area("row_b", 4096, [P, D])
        row_c = row_area("row_c", 8192, [P, D])
        diag_n = big("diag_n", 0, [P, TT, P])
        junk_act = big("junk_act", 1024, [P, TT, 2, 512])
        junk_dve = big("junk_dve", 9216, [P, 512])
        y_tmp = big("y_tmp", 12288, [P, D])
        relu = big("relu", 16384, [P, 4 * SEQ])
        sqr = big("sqr", 20480, [P, 4 * SEQ])
        lo_tmp = big("lo_tmp", 24576, [P, 2, 2, SEQ])
        prow = big("prow", 16384, [P, 4, P])
        wsrow = big("wsrow", 18432, [P, 4, P])
        gate = big("gate", 0, [P, 6, TT, 512])
        qT = big("qT", 24576, [P, 4, SEQ])
        kT = big("kT", 28672, [P, 4, SEQ])
        gm_row = big("gm_row", 20480, [P, SEQ])
        vS = ada_area("vS", 0, [P, TT, 512])
        sbt = ada_area("sbt", 4096, [P, 2, 3, 384])
        gt = ada_area("gt", 4096, [P, 3, 512])
        gv = ada_area("gv", 13312, [P, TT, SEQ])
        wpd = big("wpd", 21504, [P, 2, P])
        wsT = row_area("wsT", 0, [P, 4, P])
        pp = row_area("pp", 2048, [P, 2, 16 + SEQ])
        pa = row_area("pa", 4224, [P, 2, 16 + SEQ])
        pb = row_area("pb", 6400, [P, 2, 16 + SEQ])
        gu = row_area("gu", 8576, [P, 2, SEQ])
        bsp = row_area("bsp", 10624, [P, 2, P])
        inv = big("inv", 22528, [P, 2, SEQ])
        u_pad = big("u_pad", 0, [P, KT, PAD + SEQ])
        cacc = big("cacc", 9152, [P, KT, SEQ])
        cxc = big("cxc", 17344, [P, KT, SEQ])
        csg = big("csg", 25536, [P, 2, 2, SEQ])
        cmean = big("cmean", 29632, [P, SEQ])
        dw_diag = ada_area("dw_diag", 0, [P, TAPS, P])
        Qs = big("Qs", 0, [P, TT, D])
        Ks = big("Ks", 8192, [P, TT, D])
        Vs = big("Vs", 16384, [P, TT, D])
        aS = hid_area("aS", 0, [P, 3, 2, 384])
        aT = hid_area("aT", 9216, [P, 2, 2, 384])
        qT2 = ada_area("qT2", 0, [P, KT, SEQ])
        kT2 = ada_area("kT2", 8192, [P, KT, SEQ])

        ps = ctx.enter_context(nc.psum_tensor("ps", [P, 8, 512], F32))

        ident = cst[:, C_ID:C_ID + P]
        ones = cst[:, C_ONE:C_ONE + P]
        tri = cst[:, C_TRI:C_TRI + P]
        m01 = cst[:, C_M01:C_M01 + P]
        keep = cst[:, C_KEEP:C_KEEP + P]
        neg = cst[:, C_NEG:C_NEG + P]
        dist = cst[:, C_DIST:C_DIST + 3 * P]

        def par(name, j=0, n=1):
            at = PARAMS[name][0] + j
            return pcol[:, at:at + n]

        def sem(name):
            return ctx.enter_context(nc.semaphore(name))

        raw_landed = [sem(f"raw_landed{i}") for i in range(RING)]
        hi_made = sem("hi_made")
        lo_made = sem("lo_made")
        used = sem("used")
        ada_landed = [sem(f"ada_landed{i}") for i in range(2)]
        ada_step = sem("ada_step")
        ada_cols = sem("ada_cols")
        ada_kept = sem("ada_kept")
        x_in = sem("x_in")
        cst_in = sem("cst_in")
        par_in = [sem("par_in_first"), sem("par_in_rest")]
        misc_in = sem("misc_in")
        row_a_in = sem("row_a_in")
        row_b_in = sem("row_b_in")
        row_c_in = sem("row_c_in")
        qk_gain_in = sem("qk_gain_in")
        out_sem = sem("out_sem")
        dve_chain = sem("dve_chain")
        act_chain = sem("act_chain")
        pool_chain = sem("pool_chain")
        par_tr = sem("par_tr")
        par_ok = sem("par_ok")
        cond_sig = sem("cond_sig")
        mod_ok = sem("mod_ok")
        x_ver = sem("x_ver")
        x_half = sem("x_half")
        tile0_done = sem("tile0_done")
        ss_act = sem("ss_act")
        diag_ok = sem("diag_ok")
        hT_full = sem("hT_full")
        tr_done = sem("tr_done")
        hT_hi = sem("hT_hi")
        hT_lo = sem("hT_lo")
        relu_done = sem("relu_done")
        sq_done = sem("sq_done")
        hid_hi = sem("hid_hi")
        hid_lo = sem("hid_lo")
        row_bc = sem("row_bc")
        row_kept = sem("row_kept")
        qkv_kept = sem("qkv_kept")
        kT_kept = sem("kT_kept")
        p_kept = sem("p_kept")
        gelu_act = sem("gelu_act")
        gelu_dve = sem("gelu_dve")
        gate_kept = sem("gate_kept")
        gate_sig = sem("gate_sig")
        pool_in = sem("pool_in")
        vn_ok = sem("vn_ok")
        mix_done = sem("mix_done")
        z_done = sem("z_done")
        abs_done = sem("abs_done")
        soft_done = sem("soft_done")
        lnot_done = sem("lnot_done")
        sfx_done = sem("sfx_done")
        arg_done = sem("arg_done")
        a_done = sem("a_done")
        av_done = sem("av_done")
        o_val = sem("o_val")
        o_hi = sem("o_hi")
        o_lo = sem("o_lo")
        br_done = sem("br_done")
        product_ok = sem("product_ok")
        two_merged = sem("two_merged")
        merged = sem("merged")
        pad_ok = sem("pad_ok")
        glu_sig = sem("glu_sig")
        u_ok = sem("u_ok")
        conv_tap = sem("conv_tap")
        diag_made = sem("diag_made")
        diag_used = sem("diag_used")
        conv_kept = sem("conv_kept")
        cs_sum = sem("cs_sum")
        cs_rstd = sem("cs_rstd")
        cs_sq = sem("cs_sq")
        cs_xc = sem("cs_xc")
        cs_ln = sem("cs_ln")
        cs_sig = sem("cs_sig")
        cs_y = sem("cs_y")
        qk_kept = sem("qk_kept")
        qk_sq = sem("qk_sq")
        qk_ss = sem("qk_ss")
        qk_n = sem("qk_n")
        qk_tr = sem("qk_tr")
        qk_T = sem("qk_T")
        s_z = sem("s_z")
        s_arg = sem("s_arg")
        s_max = sem("s_max")
        s_exp = sem("s_exp")
        s_p = sem("s_p")
        s_tr = sem("s_tr")
        s_pT = sem("s_pT")
        s_o = sem("s_o")
        ss_post = sem("ss_post")
        consts_ok = sem("consts_ok")
        pool_x = sem("pool_x")


        def split_hi(act, n, slot):
            act.wait_ge(raw_landed[slot], n_landed(n, slot))
            nc.scalar.activation(hi[:, slot], raw[:, slot], ACT.Copy).then_inc(hi_made, 1)

        def n_landed(n, slot):
            return (n - slot) * (16 // RING) + 16

        def split_lo(dve, n, slot, turn=False):
            dve.wait_ge(hi_made, n + 1)
            if turn:
                dve.wait_ge(lo_made, n)
            nc.vector.tensor_tensor(lo[:, slot], raw[:, slot], hi[:, slot].bitcast(F32),
                                    ALU.subtract).then_inc(lo_made, 1)

        def pool_step(pool, u):
            n, slot = u + RING, u % RING
            pool.wait_ge(hi_made, n + 1)
            pool.wait_ge(lo_made, n)
            nc.gpsimd.tensor_tensor(lo[:, slot], raw[:, slot], hi[:, slot].bitcast(F32),
                                    ALU.subtract).then_inc(lo_made, 1)

        def act_step(act, u, i=None, j=None):
            act.wait_ge(used, u + 1)
            if not isinstance(u, int) or u + RING < N_UNITS:
                split_hi(act, u + RING, slot_of(u, j))

        def dve_step(dve, u, j=None, turn=False):
            if not isinstance(u, int) or u + RING < N_UNITS:
                split_lo(dve, u + RING, slot_of(u, j), turn)

        def slot_of(u, j):
            return (u if j is None else j) % RING

        def load(sp, n, src, j=None):
            slot = slot_of(n, j)
            if not isinstance(n, int) or n >= RING:
                sp.wait_ge(lo_made, n - (RING - 1))
            dst = raw[:, slot].rearrange("p (k n) -> p k n", k=src.shape[1])
            sp.dma_start(dst, src).then_inc(raw_landed[slot], 16)

        def rows3(w):
            return w.rearrange("(k p) n -> p k n", p=P)

        def unit_w(pe, u, j, act_h, act_l, k0, bank, first, nk=4, half=None):
            slot = slot_of(u, j)
            pe.wait_ge(lo_made, u + 1)
            wh = hi[:, slot].rearrange("p (k n) -> p k n", k=nk)
            wl = lo[:, slot].rearrange("p (k n) -> p k n", k=nk)
            for k4 in range(0, nk, 4):
                if k4 and half is not None:
                    pe.wait_ge(*half)
                for ct in range(UNIT // nk // P):
                    o = ps[:, bank + ct // 2, (ct % 2) * SEQ:(ct % 2 + 1) * SEQ]
                    c = slice(ct * P, (ct + 1) * P)
                    for k in range(k4, k4 + 4):
                        mm(pe, o, wh[:, k, c], act_h[:, k0 + k], first and k == 0 and ct % 2 == 0)
                        mm(pe, o, wh[:, k, c], act_l[:, k0 + k])
                        last = mm(pe, o, wl[:, k, c], act_h[:, k0 + k])
            last.then_inc(used, 1)

        def mm(pe, o, lhs, rhs, start=False):
            return nc.tensor.matmul(o, lhs, rhs, start=start, stop=False, skip_group_check=True)

        def unit_x(pe, u, j, act_h, act_l, k0, outs, first, nk=4, cols=512, final=False):
            slot = slot_of(u, j)
            pe.wait_ge(lo_made, u + 1)
            wh = hi[:, slot].rearrange("p (k n) -> p k n", k=nk)
            wl = lo[:, slot].rearrange("p (k n) -> p k n", k=nk)
            parts = UNIT // nk // cols
            for tt in range(TT):
                t = slice(tt * P, (tt + 1) * P)
                for c in range(parts):
                    o = outs(tt, c)
                    n = slice(c * cols, (c + 1) * cols)
                    for k in range(nk):
                        mm(pe, o, act_h[:, k0 + k, t], wh[:, k, n], first and k == 0)
                        mm(pe, o, act_l[:, k0 + k, t], wh[:, k, n])
                        last = mm(pe, o, act_h[:, k0 + k, t], wl[:, k, n])
                if final and tt == 0:
                    last.then_inc(tile0_done, 1)
            last.then_inc(used, 1)

        def transposes(pe, src, ready, diag=None):
            for k in range(KT):
                if k % 4 == 0:
                    pe.wait_ge(*ready[k // 4])
                for tt in range(TT):
                    o = tr_bank(k)[:, tt * P:(tt + 1) * P]
                    if diag is None:
                        last = nc.tensor.transpose(o, src(tt, k), ident)
                    else:
                        last = nc.tensor.matmul(o, src(tt, k), diag[:, tt], start=True, stop=True)
                if k % 2:
                    last.then_inc(tr_done, 1)

        def tr_bank(k):
            return ps[:, 4 + k // 2, (k % 2) * SEQ:(k % 2 + 1) * SEQ]

        def hT_act(act, fill, b, scale, bias, mod=None):
            for k in range(KT):
                act.wait_ge(tr_done, 4 * fill + k // 2 + 1)
                if mod is not None and k % 2:
                    if k > 3:
                        act.wait_ge(hT_lo, 8 * b + k - 3)
                    nc.scalar.activation(lo_tmp[:, 1, k // 2 % 2], tr_bank(k), ACT.Identity, bias=bias(k),
                                         scale=scale(k)).then_inc(hT_full, 1)
                nc.scalar.activation(hTh[:, k], tr_bank(k), ACT.Identity, bias=bias(k),
                                     scale=scale(k)).then_inc(hT_hi, 1)

        def hT_dve(dve, fill, b, scale, bias, mod=None):
            for k in range(KT):
                if k % 2 == 0:
                    dve.wait_ge(hT_hi, 8 * b + k + 2)
                if scale is None:
                    nc.vector.tensor_tensor(hTl[:, k], tr_bank(k), hTh[:, k].bitcast(F32),
                                            ALU.subtract).then_inc(hT_lo, 1)
                elif bias is None:
                    nc.vector.scalar_tensor_tensor(out=hTl[:, k], in0=tr_bank(k), scalar=scale(k),
                                                   in1=hTh[:, k].bitcast(F32), op0=ALU.mult,
                                                   op1=ALU.subtract).then_inc(hT_lo, 1)
                else:
                    if k % 2:
                        dve.wait_ge(hT_full, 4 * mod + k // 2 + 1)
                    else:
                        link(dve, nc.vector.tensor_scalar(lo_tmp[:, 0, k // 2 % 2], tr_bank(k), scale(k), bias(k),
                                                          ALU.mult, ALU.add))
                    tmp = lo_tmp[:, k % 2, k // 2 % 2]
                    nc.vector.tensor_tensor(hTl[:, k], tmp, hTh[:, k].bitcast(F32),
                                            ALU.subtract).then_inc(hT_lo, 1)

        links = {"dve": 0, "act": 0, "pool": 0}

        def link(dve, ins):
            links["dve"] += 1
            ins.then_inc(dve_chain, 1)
            dve.wait_ge(dve_chain, links["dve"])

        def link_act(act, ins):
            links["act"] += 1
            ins.then_inc(act_chain, 1)
            act.wait_ge(act_chain, links["act"])

        def link_pool(pool, ins):
            links["pool"] += 1
            ins.then_inc(pool_chain, 1)
            pool.wait_ge(pool_chain, links["pool"])

        def rsqrt(dve, y, ss, v, a, n, ss2=None):
            if ss2 is None:
                link(dve, nc.vector.tensor_scalar(a, ss, 1.0 / n, EPS, ALU.mult, ALU.add))
            else:
                link(dve, nc.vector.scalar_tensor_tensor(out=a, in0=ss, scalar=EPS, in1=ss2, op0=ALU.add,
                                                         op1=ALU.add))
            nc.vector.tensor_scalar(y.bitcast(I32), a.bitcast(I32), 1, None,
                                    ALU.logical_shift_right).then_inc(dve_chain, 1)
            links["dve"] += 1
            link(dve, nc.vector.tensor_scalar(v, a, -0.5, None, ALU.mult))
            link(dve, nc.vector.tensor_scalar(y.bitcast(I32), y.bitcast(I32), -1.0, RSQRT_MAGIC,
                                              ALU.mult, ALU.add))
            for _ in range(3):
                link(dve, nc.vector.tensor_tensor(a, y, y, ALU.mult))
                link(dve, nc.vector.tensor_tensor(a, a, v, ALU.mult))
                link(dve, nc.vector.scalar_tensor_tensor(out=y, in0=a, scalar=1.5, in1=y, op0=ALU.add,
                                                         op1=ALU.mult))

        N_SS, N_Y, N_A, N_V = stat[:, 0:2], stat[:, 8:10], stat[:, 16:18], stat[:, 24:26]

        def halves(t, tt):
            return t[:, tt, 0:512], t[:, tt, 512:D]

        def ss_col(post, c, tt=0, n=1):
            at = 4 * post + 2 * c + tt
            return stat[:, at:at + n]

        def rstd_col(post, tt=0, n=1):
            at = 8 + 2 * post + tt
            return stat[:, at:at + n]

        def rstd(dve, post, tt=0, n=1):
            at = 2 * post + tt
            rsqrt(dve, rstd_col(post, tt, n), ss_col(post, 0, tt, n), stat[:, 24 + at:24 + at + n],
                  stat[:, 16 + at:16 + at + n], D, ss_col(post, 1, tt, n))

        def norm_act(act, norm, fill, b, free, scale, bias, mod=None, before=None):
            def square_x(tt, c):
                nc.scalar.activation(junk_act[:, tt, c], halves(X, tt)[c], ACT.Square,
                                     scale=D ** -0.5, accum_out=ss_col(0, c, tt)).then_inc(ss_act, 1)

            if norm == 0:
                act.wait_ge(x_in, 16)
            elif norm > 2:
                act.wait_ge(x_half, 2 * (norm - 2))
                square_x(0, 0)
                square_x(1, 0)
                act.wait_ge(x_ver, 2 * norm - 1)
                square_x(0, 1)
            if norm <= 2:
                if norm:
                    act.wait_ge(x_ver, 2 * norm - 1)
                square_x(0, 0)
                square_x(0, 1)
                if norm:
                    act.wait_ge(x_ver, 2 * norm)
                square_x(1, 0)
            if free:
                act_step(act, free - 2)
                act_step(act, free - 1)
            if before is not None:
                before()
            hT_act(act, fill, b, scale, bias, mod)

        def diagonals_dve(dve):
            i2, y2 = ident.unsqueeze(1).broadcast_to([P, TT, P]), rstd_col(0, 0, TT).unsqueeze(2)
            nc.vector.tensor_tensor(diag_n[:], i2, y2.broadcast_to([P, TT, P]), ALU.mult).then_inc(diag_ok, 1)

        def square_last(dve):
            x = halves(X, 1)[1]
            link(dve, nc.vector.scalar_tensor_tensor(out=junk_dve[:], in0=x, scalar=1.0 / D, in1=x, op0=ALU.mult,
                                                     op1=ALU.mult, accum_out=ss_col(0, 1, 1)))

        def norm_dve(dve, norm):
            if norm == 0:
                dve.wait_ge(x_in, 16)
            else:
                dve.wait_ge(x_ver, 2 * norm)
            square_last(dve)
            dve.wait_ge(ss_act, 3 * norm + 3)
            rstd(dve, 0, 0, TT)
            diagonals_dve(dve)

        def dve_inc(s, n=1):
            nc.vector.sem_inc(s, n)

        def stay_warm(n):
            for _ in range(n):
                nc.tensor.matmul(ps[:, 7, 0:P], ones, ident, start=True, stop=True)

        def norm_pe(pe, norm):
            if norm == 4:
                pe.wait_ge(row_kept, 2)
            stay_warm((10, 42, 44, 20, 20, 20)[norm])
            transposes(pe, lambda tt, k: X[:, tt, k * P:(k + 1) * P],
                       [(diag_ok, norm + 1 + (norm > 2))] * 2, diag_n)

        def y_bank(tt, c):
            return ps[:, 2 * tt + c]

        def y_half(tt, c):
            return halves((y_tmp, sqr)[tt][:].unsqueeze(1), 0)[c]

        def y_ready(eng, which, last, tt, c):
            if c == 0:
                eng.wait_ge(used, last)
            elif tt == 0:
                eng.wait_ge(tile0_done, which + 1)
            else:
                eng.wait_ge(used, last + 1)

        QUARTERS = ((0, 0), (1, 0), (0, 1), (1, 1))

        def post_act(act, which, last):
            for tt, c in QUARTERS:
                y_ready(act, which, last, tt, c)
                nc.scalar.activation(junk_act[:, tt, c], y_bank(tt, c), ACT.Square,
                                     scale=D ** -0.5, accum_out=ss_col(1, c, tt)).then_inc(ss_post, 1)

        def post_dve(dve, which, last, row):
            for q, (tt, c) in enumerate(QUARTERS):
                dve.wait_ge(ss_post, 4 * which + q + 1)
                y_ready(dve, which, last, tt, c)
                link(dve, nc.vector.tensor_tensor(y_half(tt, c), y_bank(tt, c), row[:, 512 * c:512 * c + 512],
                                                  ALU.mult))
                if c:
                    rstd(dve, 1, tt)
                    nc.vector.scalar_tensor_tensor(out=X[:, tt], in0=(y_tmp, sqr)[tt][:],
                                                   scalar=rstd_col(1, tt), in1=X[:, tt], op0=ALU.mult,
                                                   op1=ALU.add).then_inc(x_ver, 1)

        def gated_dve(dve, which, last, row, norm=True):
            for tt, c in QUARTERS:
                y_ready(dve, which, last, tt, c)
                y, x = y_half(tt, c), halves(X, tt)[c]
                link(dve, nc.vector.tensor_tensor(y, y_bank(tt, c), row[:, 512 * c:512 * c + 512], ALU.mult))
                ins = nc.vector.tensor_tensor(x, x, y, ALU.add)
                if c == 0:
                    ins.then_inc(x_half, 1)
                    dve.wait_ge(x_half, 2 * (which - 2) + tt + 1)
                    continue
                ins.then_inc(x_ver, 1)
            if norm:
                norm_dve(dve, which + 1)

        def gate_row(pe, layer, i):
            pe.wait_ge(ada_kept, (10, 18, 18, 24)[2 * layer + i] + 1)
            for k in range(KT):
                m = layer * 48 + (2, 5)[i] * 8 + k
                last = nc.tensor.matmul(ps[:, 6 + k // 4, (k % 4) * P:(k % 4 + 1) * P],
                                        modT[:, m:m + 1].broadcast_to([P, P]), ident,
                                        start=True, stop=True)
            last.then_inc(row_bc, 1)

        def keep_row(act, layer, i):
            act.wait_ge(row_bc, 2 * layer + i + 1)
            nc.scalar.activation((row_a, row_b)[i][:], pair(6).rearrange("p b n -> p (b n)"),
                                 ACT.Copy).then_inc(row_kept, 1)

        def hid(t, c):
            return t[:, 4 * (c % 2):4 * (c % 2) + 4]

        def mlp_pe(pe, m):
            u0 = U_MLP[m]
            pe.wait_ge(hT_lo, 8 * (2, 5, 8)[m] + 4)
            unit_w(pe, u0, None, hTh, hTl, 0, 4, True)
            pe.wait_ge(hT_lo, 8 * (2, 5, 8)[m] + 8)
            unit_w(pe, u0 + 1, None, hTh, hTl, 4, 4, False)
            for b in range(4):
                nc.tensor.matmul(ps[:, b, 0:2], zero_r[:], zero_r[:, 0:2], start=True, stop=False,
                                 skip_group_check=True)
            ada_sum(pe, ADA_HEAD[m][0])

            def first(c, u, j, chunk):
                pe.wait_ge(relu_done, chunk)
                unit_w(pe, u, j, hTh, hTl, 0, 4, True)
                unit_w(pe, u + 1, j + 1, hTh, hTl, 4, 4, False)

            def second(par_, u, j, chunk, after=(None, None), final=False):
                pe.wait_ge(hid_lo, chunk)
                for h in range(2):
                    unit_x(pe, u + h, j + h, hid(hidh, par_), hid(hidl, par_), 0,
                           lambda tt, c, h=h: y_bank(tt, h), False, final=final and h == 1)
                    if after[h] is not None:
                        after[h]()

            with nc.tensor.Fori(0, 3, 1) as i:
                n, s = 8 * i + (u0 + 2), u0 + 2
                first(1, n, s, 2 * i + (8 * m + 1))
                second(0, n + 2, s + 2, 2 * i + (8 * m + 1))
                if m < 2:
                    ada_sum(pe, ada_loop(m, i)[0][0])
                first(2, n + 4, s + 4, 2 * i + (8 * m + 2))
                second(1, n + 6, s + 6, 2 * i + (8 * m + 2))
                if m < 2:
                    ada_sum(pe, ada_loop(m, i)[1][0])
            n = u0 + 26
            first(7, n, n, 8 * m + 7)
            second(0, n + 2, n + 2, 8 * m + 7,
                   (lambda: ada_sum(pe, ADA_TAIL[m][0]), (lambda: gate_row(pe, m - 1, 1)) if m else None))
            second(1, n + 4, n + 4, 8 * m + 8, final=True)

        def mlp_act(act, m):
            u0 = U_MLP[m]

            def relu_of(chunk):
                nc.scalar.activation(relu[:], ps[:, 4:6].rearrange("p b n -> p (b n)"),
                                     ACT.Relu).then_inc(relu_done, 1)

            def hi_of(par_, chunk):
                act.wait_ge(sq_done, chunk + 1)
                nc.scalar.activation(hid(hidh, par_).rearrange("p k n -> p (k n)"), sqr[:],
                                     ACT.Copy).then_inc(hid_hi, 1)

            act_step(act, u0)
            act.wait_ge(used, u0 + 2)
            relu_of(8 * m)
            act_step(act, u0 + 1)
            hi_of(0, 8 * m)

            def body(u, s, js, chunk):
                for j in js:
                    if j % 4 == 1 and j < len(js) - 1:
                        act.wait_ge(used, u + (j + 1))
                        relu_of(chunk + j // 4)
                    act_step(act, u + j, j=s + j)
                    if j % 4 == 1 and j < len(js) - 1:
                        hi_of(1 - j // 4, chunk + j // 4)

            with nc.scalar.Fori(0, 3, 1) as i:
                body(8 * i + (u0 + 2), u0 + 2, range(8), 2 * i + (8 * m + 1))
            body(u0 + 26, u0 + 26, range(4) if m < 2 else range(3), 8 * m + 7)
            if m:
                keep_row(act, m - 1, 1)

        def mlp_pool(pool, m):
            def square(chunk, free):
                pool.wait_ge(relu_done, chunk + 1)
                if free:
                    pool.wait_ge(hid_lo, chunk)
                nc.gpsimd.tensor_tensor(sqr[:], relu[:], relu[:], ALU.mult).then_inc(sq_done, 1)

            square(8 * m, m > 0)
            with nc.gpsimd.Fori(1, 8, 1) as c:
                square(c + 8 * m, True)

        ADA_IN = [(0, 0, 6), (1, 0, 7)]
        ADA_QKV = [(18 + q, 1, 6 + q) for q in range(4)]
        ADA_HEAD = ((2, 0, 8), (10, 0, 10), (22, 1, 10))
        ADA_TAIL = ((9, 0, 9), (17, 0, 11), (23, 1, 11))

        def ada_loop(m, i):
            return [(2 * i + (8 * m + 3 + q), m, 2 * i + q) for q in range(2)]

        def ada_load(sp, chunk, h):
            number, layer, c = chunk
            sp.wait_ge(ada_step, number * 8 + (4 * h + 4))
            src = rows3(ada_w_2[layer])[:, 4 * h:4 * h + 4, bass.ds(c * 512, 512)]
            sp.dma_start(ada_raw[:, h], src).then_inc(ada_landed[h], 16)

        def ada_sum(pe, number):
            pe.wait_ge(ada_step, number * 8 + 16)
            pe.wait_ge(ada_kept, number + 1)
            for q in range(4):
                last = nc.tensor.matmul(ps[:, 6, q:q + 1], ada_acc[:, q * P:(q + 1) * P],
                                        ones[:, 0:1], start=True, stop=True)
            last.then_inc(ada_cols, 1)

        def ada_unit(dve, number, h):
            dve.wait_ge(ada_landed[h], number * 16 + 16)
            for k in range(4):
                step = number * 8 + (8 + 4 * h + k)
                w, s = ada_raw[:, h, k], cond[:, 4 * h + k:4 * h + k + 1]
                if h == 0 and k == 0:
                    ins = nc.vector.tensor_scalar(ada_acc[:], w, s, None, ALU.mult)
                else:
                    dve.wait_ge(ada_step, step)
                    ins = nc.vector.scalar_tensor_tensor(out=ada_acc[:], in0=w, scalar=s, in1=ada_acc[:],
                                                         op0=ALU.mult, op1=ALU.add)
                ins.then_inc(ada_step, 1)

        def late_steps(dve, last, chunk):
            for h in range(2):
                if chunk is not None:
                    ada_unit(dve, chunk[0], h)
                dve_step(dve, last - 1 + h)

        def ada_keep(dve, chunk):
            number, layer, c = chunk
            dve.wait_ge(ada_cols, number + 1)
            at = bass.ds(c * 4 + 48 * layer, 4)
            nc.vector.tensor_tensor(modT[:, at], ps[:, 6, 0:4], ada_bT[:, at], ALU.add).then_inc(ada_kept, 1)

        def mlp_dve(dve, m):
            u0 = U_MLP[m]

            def lo_of(par_, chunk):
                dve.wait_ge(hid_hi, chunk + 1)
                nc.vector.tensor_tensor(hid(hidl, par_).rearrange("p k n -> p (k n)"), sqr[:],
                                        hid(hidh, par_).rearrange("p k n -> p (k n)").bitcast(F32),
                                        ALU.subtract).then_inc(hid_lo, 1)

            dve_step(dve, u0)
            dve_step(dve, u0 + 1)
            ada_keep(dve, ADA_HEAD[m])
            lo_of(0, 8 * m)

            def body(u, s, js, chunk, ada):
                for j in js:
                    if ada is not None and j % 2 == 0:
                        ada_unit(dve, ada[j // 4][0], j // 2 % 2)
                    dve_step(dve, u + j, j=s + j)
                    if j % 4 == 1:
                        lo_of(1 - j // 4, chunk + j // 4)
                    if ada is not None and j in (3, 7):
                        ada_keep(dve, ada[j // 7])

            with nc.vector.Fori(0, 3, 1) as i:
                body(8 * i + (u0 + 2), u0 + 2, range(8), 2 * i + (8 * m + 1),
                     ada_loop(m, i) if m < 2 else None)
            for j in range(4 if m < 2 else 3):
                if j < 2:
                    ada_unit(dve, ADA_TAIL[m][0], j)
                dve_step(dve, u0 + 26 + j)
                if j == 1:
                    lo_of(1, 8 * m + 7)
                if j == 2:
                    ada_keep(dve, ADA_TAIL[m])

        def mlp_sp(sp, m, w1, w2, ada_free):
            u0 = U_MLP[m]
            v1, v2 = rows3(w1), rows3(w2)

            def first(n, j, c, h):
                load(sp, n, v1[:, 4 * h:4 * h + 4, bass.ds(c * 512, 512)], j)

            def second(n, j, c, h):
                load(sp, n, v2[:, bass.ds(c * 4, 4), h * 512:h * 512 + 512], j)

            for h in range(2):
                first(u0 + h, u0 + h, 0, h)
            for h in range(2):
                first(u0 + 2 + h, u0 + 2 + h, 1, h)
            sp.wait_ge(*ada_free)
            for h in range(2):
                ada_load(sp, ADA_HEAD[m], h)
            for h in range(2):
                second(u0 + 4 + h, u0 + 4 + h, 0, h)
            with nc.sync.Fori(0, 3, 1) as i:
                n, s = 8 * i + (u0 + 6), u0 + 6
                for j in range(8):
                    c = 2 * i + (2, 1, 3, 2)[j // 2]
                    (first, second)[j // 2 % 2](n + j, s + j, c, j % 2)
                    if m < 2 and j % 2 == 0:
                        ada_load(sp, ada_loop(m, i)[j // 4], j // 2 % 2)
            for h in range(2):
                second(u0 + 30 + h, u0 + 30 + h, 7, h)
                ada_load(sp, ADA_TAIL[m], h)

        ada_bT = par("ada_b", 0, 96)
        qsq = big("qsq", 24576, [P, TT, 512])

        PAIRS = AT_HEADS // 2
        query_tiles = (slice(0, P), slice(P, 384))
        softmax_rows = [(i, c) for c in query_tiles for i in range(2)]

        def s_col(pair_, j, n):
            at = 320 + 16 * (pair_ % 2) + j
            return stat[:, at:at + n]

        def mod_shift(layer, vec, k):
            return modT[:, (layer * 6 + vec) * 8 + k:(layer * 6 + vec) * 8 + k + 1]

        def mod_scale(layer, vec, k):
            return mod_shift(layer, vec + 1, k)

        PAR_SRC = (("g_mix_pre", g_mix_pre), ("g_ff_pre", g_ff_pre), ("mix_g", mix_norm_g_2),
                   ("mlp_g", mlp_norm_g_2), ("conv_b_in", conv_b_in_2), ("conv_dw_b", conv_dw_b_2),
                   ("conv_ln_g", conv_ln_g_2), ("conv_ln_b", conv_ln_b_2), ("pool_scale", pool_scale),
                   ("c", c_2), ("ada_b", ada_b_2), ("conv_dw", conv_dw_2))
        N_PAR_DMAS = (len(PAR_SRC) - 2, 4)
        N_MISC_DMAS = 10

        CONV_PE = (5, 6, 7)
        CONV_ROUNDS = ((0, 1), (2, 3), (4,))
        GLU_AFTER = {(0, 13): 1, (0, 26): 2, (1, 8): 3}

        PAR_REST = ((0, 96), (96, 124), (220, 124))

        def conv_silu(dve, k):
            dve.wait_ge(cs_sig, k + 1)
            nc.vector.scalar_tensor_tensor(out=cxc[:, k], in0=cxc[:, k], scalar=par("conv_ln_b", k),
                                           in1=csg[:, k % 2, 0], op0=ALU.add, op1=ALU.mult).then_inc(cs_y, 1)

        def conv_lo(dve, k):
            dve.wait_ge(cs_y, k + 1)
            dve.wait_ge(hT_hi, 32 + k + 1)
            nc.vector.tensor_tensor(hTl[:, k], cxc[:, k], hTh[:, k].bitcast(F32),
                                    ALU.subtract).then_inc(hT_lo, 1)

        def chunk_bank(g):
            return 2 * (g % 2)

        def pair(bank):
            return ps[:, bank:bank + 2]

        def row(v, n=D):
            return v.partition_broadcast(P)

        block = ctx.enter_context(nc.Block())

        @block.sync
        def _(sp):
            sp.dma_start(X[:], x.rearrange("a (t p) d -> p (a t) d", p=P)).then_inc(x_in, 16)
            sp.dma_start(cst[:], consts).then_inc(cst_in, 16)
            def parameter_loads():
                sp.dma_start(prow[0:96, 1], ada_b_2.rearrange("a (k p) -> (a k) p", p=P)).then_inc(par_in[1], 16)
                v = conv_dw_2.rearrange("a t (k p) -> (a t k) p", p=P)
                for g in range(2):
                    sp.dma_start(prow[0:124, 2 + g], v[124 * g:124 * g + 124]).then_inc(par_in[1], 16)
                sp.dma_start(wsrow[:], w_spatial[0].rearrange("g t p -> t g p")).then_inc(par_in[1], 16)

            def misc_loads():
                sp.dma_start(inv[:], inv_count).then_inc(misc_in, 16)
                sp.dma_start(gm_row[:], row(gm_gain[0])).then_inc(misc_in, 16)
                sp.wait_ge(pad_ok, 1)
                for g in range(4):
                    r = slice(HD * (g % 2), HD * (g % 2) + HD)
                    sp.dma_start(bsp[r, g // 2], b_spatial[0, g].partition_broadcast(HD)).then_inc(misc_in, 16)
                    sp.dma_start(wpd[r, g // 2, r], w_pool[0, g]).then_inc(misc_in, 16)
                for i, g in enumerate((attn_q_norm_g_2, attn_k_norm_g_2)):
                    for half in range(2):
                        sp.dma_start(qk_gain[HD * half:HD * half + HD, i:i + 1],
                                     g.rearrange("a d -> d a")).then_inc(qk_gain_in, 16)

            win = rows3(w_in[0])
            for c in range(4):
                for h in range(2):
                    load(sp, 2 * c + h, win[:, 4 * h:4 * h + 4, 512 * c:512 * c + 512])
                    if c == 0 and h == 0:
                        sp.wait_ge(par_in[0], 16 * N_PAR_DMAS[0])
                    if 2 * c + h == 3:
                        parameter_loads()
                    elif 2 * c + h >= 5:
                        half = 2 * c + h - 5
                        ada_load(sp, ADA_IN[half // 2], half % 2)
            load(sp, U_GV, win[:, :, 2048:2304])
            ada_load(sp, ADA_IN[1], 1)
            misc_loads()
            for c in range(6):
                for h in range(2):
                    n = 2304 + 512 * c
                    load(sp, U_GATE + 2 * c + h, win[:, 4 * h:4 * h + 4, n:n + 512])
            for c in range(2):
                load(sp, U_BR + c, rows3(w_br_sb[0])[:, :, 512 * c:512 * c + 512])
            load(sp, U_BR + 2, rows3(w_br_pool[0]))
            load(sp, U_BR + 3, rows3(w_br_gm[0]))

            def square(first, w):
                for c in range(2):
                    for h in range(2):
                        load(sp, first + 2 * c + h, rows3(w)[:, 4 * h:4 * h + 4, 512 * c:512 * c + 512])

            square(U_OUT, w_out[0])
            mlp_sp(sp, 0, w_ff_in[0], w_ff_out[0], (o_lo, 8))
            for c in range(4):
                for h in range(2):
                    load(sp, U_CIN + 2 * c + h,
                         rows3(conv_w_in_2[0])[:, :, D * h + SEQ * c:D * h + SEQ * c + SEQ])
            square(U_COUT, conv_w_out_2[0])
            mlp_sp(sp, 1, mlp_w1_2[0], mlp_w2_2[0], (diag_used, TAPS * len(CONV_PE)))
            for c in range(6):
                for h in range(2):
                    load(sp, U_QKV + 2 * c + h,
                         rows3(attn_w_qkv_2[0])[:, 4 * h:4 * h + 4, 512 * c:512 * c + 512])
                    if 2 <= c:
                        ada_load(sp, ADA_QKV[c - 2], h)
            square(U_WO, attn_w_o_2[0])
            mlp_sp(sp, 2, mlp_w1_2[1], mlp_w2_2[1], (s_z, AT_HEADS))
            for tt in range(TT):
                sp.wait_ge(x_ver, 2 * 5 + tt + 1)
                sp.dma_start(out[0, tt * P:(tt + 1) * P, :], X[:, tt]).then_inc(out_sem, 16)
            sp.wait_ge(out_sem, 32)

        @block.tensor
        def _(pe):
            pe.wait_ge(par_in[0], 16 * N_PAR_DMAS[0])
            pe.wait_ge(cst_in, 16)
            nc.tensor.transpose(ps[:, 0, 0:N_MISC], prow[0:N_MISC, 0], ident[0:N_MISC, 0:N_MISC]).then_inc(
                par_tr, 1)
            norm_pe(pe, 0)

            def other_parameters():
                pe.wait_ge(par_in[1], 16 * N_PAR_DMAS[1])
                for g, (at, n) in enumerate(PAR_REST):
                    nc.tensor.transpose(ps[:, 7, at:at + n], prow[0:n, 1 + g], ident[0:n, 0:n])
                for g in range(4):
                    last = nc.tensor.transpose(ps[:, 6, g * P:(g + 1) * P], wsrow[:, g], ident)
                last.then_inc(par_tr, 1)

            for c, bank in ((0, 0), (1, 2)):
                if c == 0:
                    pe.wait_ge(hT_lo, 4)
                unit_w(pe, 2 * c, None, hTh, hTl, 0, bank, True)
                if c == 0:
                    pe.wait_ge(hT_lo, 8)
                    other_parameters()
                unit_w(pe, 2 * c + 1, None, hTh, hTl, 4, bank, False)
            for h in range(2):
                unit_x(pe, U_V + h, None, hTh, hTl, 4 * h, lambda tt, c: ps[:, 4 + tt], h == 0)
                if h == 0:
                    ada_sum(pe, 0)
            pe.wait_ge(qkv_kept, 1)
            unit_w(pe, U_PU, None, hTh, hTl, 0, 0, True)
            unit_w(pe, U_PU + 1, None, hTh, hTl, 4, 0, False)
            ada_sum(pe, 1)
            pe.wait_ge(kT_kept, 1)
            unit_x(pe, U_GV, None, hTh, hTl, 0, lambda tt, c: ps[:, 2, tt * SEQ:(tt + 1) * SEQ],
                   True, nk=8, cols=SEQ)

            def scores(h):
                if h == 0:
                    pe.wait_ge(qkv_kept, 2)
                if h >= 2:
                    pe.wait_ge(arg_done, h - 1)
                r = slice(HD * (h % 2), HD * (h % 2) + HD)
                k = h // 2
                nc.tensor.matmul(ps[:, 4 + h % 2, 0:SEQ], kT[r, k, 0:P], qT[r, k, :], start=True,
                                 stop=False, skip_group_check=True)
                nc.tensor.matmul(ps[:, 4 + h % 2, SEQ:384], kT[r, k, P:SEQ], qT[r, k, P:SEQ],
                                 start=False, stop=False, skip_group_check=True).then_inc(z_done, 1)

            def suffix(h):
                pe.wait_ge(lnot_done, h + 1)
                if h >= 1:
                    pe.wait_ge(arg_done, h)
                t = sbt[:, h % 2, 1]
                mm(pe, ps[:, 6, 0:SEQ], tri, t[:, 0:SEQ], True)
                mm(pe, ps[:, 6, P:SEQ], ones, t[:, SEQ:384])
                mm(pe, ps[:, 6, SEQ:384], tri, t[:, SEQ:384]).then_inc(sfx_done, 1)

            def values(h):
                pe.wait_ge(a_done, h + 1)
                if h >= 2 and h % 2 == 0:
                    pe.wait_ge(o_lo, h // 2)
                a = sbt[:, h % 2, 2]
                r, at = slice(HD * (h % 2), HD * (h % 2) + HD), (h // 2 % 2) * SEQ
                v = slice(h * HD, h * HD + HD)
                mm(pe, ps[r, 7, at:at + SEQ], vS[:, 0, v], a[:, 0:SEQ], True)
                mm(pe, ps[r, 7, at + P:at + SEQ], vS[:, 1, v], a[:, SEQ:384]).then_inc(av_done, 1)

            for s in range(12):
                g = s // 2
                bank = chunk_bank(g)
                if s == 0:
                    pe.wait_ge(p_kept, 1)
                    pe.wait_ge(gelu_dve, 2)
                elif s == 2:
                    pe.wait_ge(gelu_dve, 4)
                elif s % 2 == 0:
                    pe.wait_ge(gate_kept, g - 1)
                unit_x(pe, U_GATE + s, None, hTh, hTl, 4 * (s % 2), lambda tt, c: ps[:, bank + tt],
                       s % 2 == 0)
                if s < SB_HEADS:
                    scores(s)
                if 1 <= s < SB_HEADS + 1:
                    suffix(s - 1)
                if 2 <= s < SB_HEADS + 2:
                    values(s - 2)
                if s == 9:
                    pe.wait_ge(pool_in, 1)
                    pe.wait_ge(misc_in, 16 * N_MISC_DMAS)
                    pe.wait_ge(arg_done, SB_HEADS)
                    for i in range(2):
                        last = mm(pe, ps[:, 5, i * SEQ:(i + 1) * SEQ], wpd[:, i], pp[:, i, 16:16 + SEQ], True)
                    last.then_inc(mix_done, 1)
                    pe.wait_ge(vn_ok, 1)
                    for g4 in range(4):
                        r = slice(HD * (g4 % 2), HD * (g4 % 2) + HD)
                        for tt in range(TT):
                            at = (g4 // 2) * SEQ + tt * P
                            last = mm(pe, ps[r, 6, at:at + P], gv[:, tt, g4 * HD:(g4 + 1) * HD],
                                      wsT[:, g4], True)
                    last.then_inc(mix_done, 1)

            pe.wait_ge(o_lo, 4)
            for c in range(2):
                pe.wait_ge(gate_kept, 5 + c)
                unit_x(pe, U_BR + c, None, hidh, hidl, 0, lambda tt, _, c=c: ps[:, 2 * c + tt], True)
            pe.wait_ge(o_lo, 8)
            unit_x(pe, U_BR + 2, None, hidh, hidl, 4, lambda tt, c: ps[:, 4 + 2 * c + tt], True, nk=2)
            pe.wait_ge(br_done, 2)
            unit_x(pe, U_BR + 3, None, hidh, hidl, 6, lambda tt, c: ps[:, 2 * c + tt], True, nk=2)
            transposes(pe, lambda tt, k: gate[:, k // 4, tt, (k % 4) * P:(k % 4 + 1) * P],
                       [(merged, 1), (merged, 2)])

            def square(first, b, whole=False):
                for c in range(2):
                    for h in range(2):
                        if c == 0:
                            pe.wait_ge(hT_lo, 8 * b + (8 if whole else 4 * h + 4))
                        unit_x(pe, first + 2 * c + h, None, hTh, hTl, 4 * h,
                               lambda tt, _, c=c: y_bank(tt, c), h == 0, final=c == 1 and h == 1)

            square(U_OUT, 1)
            norm_pe(pe, 1)
            mlp_pe(pe, 0)

            norm_pe(pe, 2)
            pe.wait_ge(hT_lo, 28)
            for c in range(4):
                if c >= 2:
                    pe.wait_ge(u_ok, 2 * (c - 1))
                for h in range(2):
                    unit_w(pe, U_CIN + 2 * c + h, None, hTh, hTl, 0, chunk_bank(c) + h, True, nk=8,
                           half=(hT_lo, 32) if c == h == 0 else None)
                if c == 0:
                    gate_row(pe, 0, 0)
            pe.wait_ge(row_kept, 1)
            for i, k in enumerate(CONV_PE):
                pe.wait_ge(u_ok, k + 1)
                for t in range(TAPS):
                    pe.wait_ge(diag_made, TAPS * i + t + 1)
                    mm(pe, ps[:, 4 + i, 0:SEQ], dw_diag[:, t], u_pad[:, k, t:t + SEQ],
                       t == 0).then_inc(diag_used, 1)
            for i, k in enumerate((0, 1, 2, 3, 5, 6, 4, 7)):
                if k in CONV_PE:
                    pe.wait_ge(conv_kept, k - 4)
                elif k == 0:
                    pe.wait_ge(conv_tap, 4 * TAPS)
                elif k == 4:
                    pe.wait_ge(conv_tap, 5 * TAPS + 1)
                last = mm(pe, ps[:, 7, 0:SEQ], ones, cacc[:, k], i == 0)
            last.then_inc(cs_sum, 1)
            for k in range(KT):
                pe.wait_ge(cs_sq, k + 1)
                for tt in range(TT):
                    last = mm(pe, ps[:, 4, tt:tt + 1], cacc[:, k, tt * P:(tt + 1) * P], ones[:, 0:1],
                              k == 0 and tt == 0)
            last.then_inc(cs_sum, 1)
            pe.wait_ge(diag_ok, 3 + 1)
            for tt in range(TT):
                last = nc.tensor.matmul(ps[:, 5, tt * P:(tt + 1) * P], ones, diag_n[:, tt], start=True,
                                        stop=True)
            last.then_inc(cs_rstd, 1)
            stay_warm(18)
            square(U_COUT, 4)
            norm_pe(pe, 3)
            mlp_pe(pe, 1)

            norm_pe(pe, 4)

            def qkv(c, between=lambda: None):
                if c >= 2:
                    pe.wait_ge(qk_kept, c - 1)
                for h in range(2):
                    if c == 0:
                        pe.wait_ge(hT_lo, 48 + 4 * h + 4)
                    unit_x(pe, U_QKV + 2 * c + h, None, hTh, hTl, 4 * h,
                           lambda tt, _: ps[:, chunk_bank(c) + tt], h == 0)
                    if h == 0:
                        between()

            def qk_transposes(src, first):
                pe.wait_ge(qk_n, 1 + first // 4)
                for f in range(4):
                    if first + f >= 2:
                        pe.wait_ge(qk_T, first + f - 1)
                    for k in (2 * f, 2 * f + 1):
                        for tt in range(TT):
                            at = (k % 2) * SEQ + tt * P
                            last = nc.tensor.transpose(ps[:, 6 + f % 2, at:at + P],
                                                       src[:, tt, k * P:(k + 1) * P], ident)
                    last.then_inc(qk_tr, 1)

            def first_unit_done():
                ada_sum(pe, ADA_QKV[0][0])
                pe.wait_ge(ada_kept, 18 + 2)
                gate_row(pe, 1, 0)

            qkv(0)
            qkv(1, first_unit_done)
            pe.wait_ge(row_kept, 3)
            qkv(2, lambda: ada_sum(pe, ADA_QKV[1][0]))
            qkv(3, lambda: ada_sum(pe, ADA_QKV[2][0]))
            qkv(4, lambda: ada_sum(pe, ADA_QKV[3][0]))
            pe.wait_ge(ada_kept, 22 + 1)
            qk_transposes(Qs, 0)
            qkv(5, lambda: qk_transposes(Ks, 4))
            for s in range(PAIRS + 3):
                if s < PAIRS:
                    if s == 0:
                        pe.wait_ge(qk_T, 8)
                    if s >= 2:
                        pe.wait_ge(s_arg, 2 * (s - 1))
                    for i in range(2):
                        b, r = 4 + 2 * (s % 2) + i, slice(HD * i, HD * i + HD)
                        mm(pe, ps[:, b, 0:P], qT2[r, s, 0:P], kT2[r, s, 0:P], True)
                        mm(pe, ps[:, b, P:384], qT2[r, s, P:SEQ], kT2[r, s, :]).then_inc(s_z, 1)
                if 2 <= s < PAIRS + 2:
                    k = s - 2
                    pe.wait_ge(s_p, 2 * k + 2)
                    if k == 0:
                        pe.wait_ge(qk_kept, 6)
                    else:
                        pe.wait_ge(s_pT, k)
                    for i in range(2):
                        for q in range(3):
                            c = slice(q * P, (q + 1) * P)
                            last = nc.tensor.transpose(ps[:, 2 + i, c], aS[:, k % 3, i, c], ident)
                    last.then_inc(s_tr, 1)
                if s >= 3:
                    k = s - 3
                    pe.wait_ge(s_pT, k + 1)
                    if k >= 2:
                        pe.wait_ge(hT_lo, 56 + k - 1)
                    for i in range(2):
                        r, v = slice(HD * i, HD * i + HD), slice((2 * k + i) * HD, (2 * k + i + 1) * HD)
                        mm(pe, ps[r, k % 2, 0:SEQ], Vs[:, 0, v], aT[:, k % 2, i, 0:SEQ], True)
                        last = mm(pe, ps[r, k % 2, P:SEQ], Vs[:, 1, v], aT[:, k % 2, i, SEQ:384])
                    last.then_inc(s_o, 1)
            square(U_WO, 7, True)
            norm_pe(pe, 5)
            mlp_pe(pe, 2)

        @block.scalar
        def _(act):
            for name, src in PAR_SRC:
                at, n = PARAMS[name]
                if at < P:
                    v = src.rearrange("a (k p) -> (a k) p", p=P)
                    act.dma_start(prow[at:at + n, 0], v).then_inc(par_in[0], 16)

            def first_split():
                split_hi(act, 0, 0)
                act.wait_ge(par_ok, 1)

            norm_act(act, 0, 0, 0, None, lambda k: par("g_mix_pre", k), lambda k: 0.0, before=first_split)
            for n in range(1, RING):
                split_hi(act, n, n)
            nc.scalar.activation(cond[:, 8:16], par("c", 0, 8), ACT.Sigmoid).then_inc(cond_sig, 1)

            act_step(act, 0)
            act_step(act, 1)
            nc.scalar.activation(qT[:].rearrange("p k n -> p (k n)"),
                                 pair(0).rearrange("p b n -> p (b n)"), ACT.Copy).then_inc(qkv_kept, 1)
            for u in range(2, 8):
                act_step(act, u)
            act.wait_ge(ada_step, 8 + 8 * 2)
            nc.scalar.activation(vS[:], pair(4), ACT.Copy).then_inc(qkv_kept, 1)

            def gelu_parts(i, x):
                nc.scalar.activation(gt[:, 0], x, ACT.Square).then_inc(gelu_act, 1)
                act.wait_ge(gelu_dve, 2 * i + 1)
                nc.scalar.activation(gt[:, 1], gt[:, 0], ACT.Sigmoid, scale=GELU_2C).then_inc(gelu_act, 1)

            act.wait_ge(pad_ok, 1)
            nc.scalar.activation(pp[:, :, 16:16 + SEQ], ps[:, 0].rearrange("p (k n) -> p k n", k=2),
                                 ACT.Copy).then_inc(p_kept, 1)
            gelu_parts(0, ps[:, 1])
            act_step(act, 8)
            act.wait_ge(gelu_dve, 2)
            gelu_parts(1, ps[:, 2])
            nc.scalar.preload_act_table_set("natural_log_exp_and_others")

            def softplus(h):
                act.wait_ge(z_done, h + 1)
                if h < 2:
                    act.wait_ge(vn_ok, 1)
                else:
                    act.wait_ge(arg_done, h - 1)
                t = sbt[:, h % 2, 0]
                nc.scalar.activation(t, ps[:, 4 + h % 2, 0:384], ACT.Abs, scale=SCALE).then_inc(abs_done, 1)
                act.wait_ge(abs_done, h + 1)
                link_act(act, nc.scalar.activation(t, t, ACT.Exp, scale=-1.0))
                nc.scalar.activation(t, t, ACT.Ln, bias=1.0).then_inc(soft_done, 1)

            def o_split(k, bank, cols):
                nc.scalar.activation(hidh[:, k], ps[:, bank, cols], ACT.Copy).then_inc(o_hi, 1)

            for s in range(12):
                if s == 11:
                    act.wait_ge(used, U_GATE + 12)
                    nc.scalar.activation(gate[:, 5], pair(chunk_bank(5)), ACT.Copy).then_inc(gate_kept, 1)
                act_step(act, U_GATE + s)
                if s < SB_HEADS:
                    softplus(s)
                if 1 <= s < SB_HEADS + 1:
                    h = s - 1
                    act.wait_ge(arg_done, h + 1)
                    a = sbt[:, h % 2, 2]
                    nc.scalar.activation(a, a, ACT.Exp).then_inc(a_done, 1)
                if s % 2 and s >= 3 and s < SB_HEADS + 2:
                    k = (s - 3) // 2
                    act.wait_ge(av_done, 2 * k + 2)
                    o_split(k, 7, slice((k % 2) * SEQ, (k % 2 + 1) * SEQ))
                if s % 2 and s < 11:
                    g = s // 2
                    nc.scalar.activation(gate[:, g], pair(chunk_bank(g)), ACT.Copy).then_inc(gate_kept, 1)
            act.wait_ge(o_val, 1)
            for k in range(2):
                nc.scalar.activation(hidh[:, 6 + k], gt[:, 0, k * SEQ:(k + 1) * SEQ], ACT.Copy).then_inc(o_hi, 1)
            act.wait_ge(mix_done, 1)
            for k in range(2):
                nc.scalar.activation(hidh[:, 4 + k], ps[:, 5, k * SEQ:(k + 1) * SEQ], ACT.Copy,
                                     scale=par("pool_scale", k)).then_inc(o_hi, 1)
            act.wait_ge(gate_kept, 6)
            for g in range(6):
                nc.scalar.activation(gate[:, g], gate[:, g], ACT.Sigmoid).then_inc(gate_sig, 1)
            for u in range(U_BR, U_OUT):
                act_step(act, u)
            act.wait_ge(used, U_BR)
            hT_act(act, 1, 1, lambda k: 1.0, lambda k: 0.0)
            for u in range(U_OUT, U_OUT + 2):
                act_step(act, u)
            post_act(act, 0, U_OUT + 3)
            norm_act(act, 1, 2, 2, U_OUT + 4, lambda k: par("g_ff_pre", k), lambda k: 0.0)
            mlp_act(act, 0)
            post_act(act, 1, U_MLP[0] + 31)

            def mod_norm(norm, fill, b, free, layer, vec):
                act.wait_ge(mod_ok, norm - 1)
                norm_act(act, norm, fill, b, free, lambda k: mod_scale(layer, vec, k),
                         lambda k: mod_shift(layer, vec, k), mod=norm - 2)

            def tap_diagonal(act, i, t):
                at = t * KT + CONV_PE[i]
                nc.scalar.activation(dw_diag[:, t], ident, ACT.Copy,
                                     scale=par("conv_dw", at)).then_inc(diag_made, 1)

            mod_norm(2, 3, 3, U_CIN, 0, 0)
            for c in range(4):
                for h in range(2):
                    act_step(act, U_CIN + 2 * c + h)
                for i in range(2):
                    if c >= 2:
                        act.wait_ge(u_ok, 2 * (c - 2) + i + 1)
                    nc.scalar.activation(csg[:, c % 2, i], ps[:, chunk_bank(c) + 1, i * SEQ:(i + 1) * SEQ],
                                         ACT.Sigmoid, bias=par("conv_b_in", 8 + 2 * c + i)).then_inc(glu_sig, 1)
                if c == 0:
                    keep_row(act, 0, 0)
                    act.wait_ge(ada_step, 8 + 8 * (ADA_TAIL[0][0] + 1))
                    for t in range(TAPS):
                        tap_diagonal(act, 0, t)
            for i in range(len(CONV_PE)):
                if i + 1 < len(CONV_PE):
                    for t in range(TAPS):
                        act.wait_ge(diag_used, TAPS * i + t + 1)
                        tap_diagonal(act, i + 1, t)
                act.wait_ge(diag_used, TAPS * (i + 1))
                k = CONV_PE[i]
                nc.scalar.activation(cacc[:, k], ps[:, 4 + i, 0:SEQ], ACT.Identity,
                                     bias=par("conv_dw_b", k)).then_inc(conv_kept, 1)
            for k in range(KT):
                act.wait_ge(cs_xc, k + 1)
                act.wait_ge(cs_sum, 1)
                nc.scalar.activation(cacc[:, k], cxc[:, k], ACT.Square).then_inc(cs_sq, 1)
            for k in range(KT + 1):
                if k < KT:
                    act.wait_ge(cs_ln, k + 1)
                    nc.scalar.activation(csg[:, k % 2, 0], cxc[:, k], ACT.Sigmoid,
                                         bias=par("conv_ln_b", k)).then_inc(cs_sig, 1)
                if k:
                    act.wait_ge(cs_y, k)
                    nc.scalar.activation(hTh[:, k - 1], cxc[:, k - 1], ACT.Copy).then_inc(hT_hi, 1)
            for u in range(U_COUT, U_COUT + 2):
                act_step(act, u)
            mod_norm(3, 4, 5, U_COUT + 4, 0, 3)
            mlp_act(act, 1)

            mod_norm(4, 5, 6, U_QKV, 1, 0)

            def keep_qkv(c, between=lambda: None):
                act_step(act, U_QKV + 2 * c)
                between()
                act_step(act, U_QKV + 2 * c + 1)
                dst = (Qs, Ks, Vs)[c // 2]
                if c < 4:
                    if c:
                        act.wait_ge(qk_ss, c)
                    nc.scalar.activation(qsq[:], pair(chunk_bank(c)), ACT.Square).then_inc(qk_sq, 1)
                nc.scalar.activation(dst[:, :, (c % 2) * 512:(c % 2 + 1) * 512], pair(chunk_bank(c)),
                                     ACT.Copy).then_inc(qk_kept, 1)

            def keep_T(dst, i, first):
                for f in range(4):
                    act.wait_ge(qk_tr, first + f + 1)
                    nc.scalar.activation(dst[:, 2 * f:2 * f + 2].rearrange("p k n -> p (k n)"),
                                         ps[:, 6 + f % 2], ACT.Copy,
                                         scale=qk_gain[:, i:i + 1]).then_inc(qk_T, 1)

            keep_qkv(0)
            keep_qkv(1, lambda: keep_row(act, 1, 0))
            keep_qkv(2)
            keep_qkv(3)
            act.wait_ge(qk_gain_in, 64)
            keep_qkv(4)
            keep_T(qT2, 0, 0)
            keep_qkv(5, lambda: keep_T(kT2, 1, 4))
            for s in range(1, PAIRS + 4):
                if s < PAIRS + 1:
                    k = s - 1
                    act.wait_ge(s_max, k + 1)
                    for j, (i, c) in enumerate(softmax_rows):
                        a = aS[:, k % 3, i, c]
                        nc.scalar.activation(a, a, ACT.Exp, scale=SCALE, bias=s_col(k, 4 + j, 1),
                                             accum_out=s_col(k, 8 + j, 1)).then_inc(s_exp, 1)
                if 2 <= s < PAIRS + 2:
                    k = s - 2
                    act.wait_ge(s_tr, k + 1)
                    if k >= 2:
                        act.wait_ge(s_o, k - 1)
                    nc.scalar.activation(aT[:, k % 2], ps[:, 2:4, 0:384], ACT.Copy).then_inc(s_pT, 1)
                if s >= 4:
                    k = s - 4
                    act.wait_ge(s_o, k + 1)
                    nc.scalar.activation(hTh[:, k], ps[:, k % 2, 0:SEQ], ACT.Copy).then_inc(hT_hi, 1)
            for u in range(U_WO, U_WO + 2):
                act_step(act, u)
            mod_norm(5, 6, 8, U_WO + 4, 1, 3)
            mlp_act(act, 2)

        @block.vector
        def _(dve):
            nc.vector.sem_inc(ada_step, 8)
            nc.vector.sem_inc(ada_kept, 1)
            dve.wait_ge(cst_in, 16)
            norm_dve(dve, 0)
            dve.wait_ge(par_tr, 1)
            nc.vector.tensor_copy(pcol[:, 0:N_MISC], ps[:, 0, 0:N_MISC]).then_inc(par_ok, 1)
            dve.wait_ge(par_ok, 1)
            split_lo(dve, 0, 0)
            hT_dve(dve, 0, 0, lambda k: par("g_mix_pre", k), None)
            for n in range(1, RING):
                split_lo(dve, n, n)
            dve.wait_ge(cond_sig, 1)
            link(dve, nc.vector.tensor_tensor(cond[:, 0:8], cond[:, 8:16], par("c", 0, 8), ALU.mult))
            for u in range(8):
                if u in (2, 3, 5, 6):
                    ada_unit(dve, *((0, 0), (0, 1), (), (1, 0), (1, 1))[u - 2])
                dve_step(dve, u)
                if u == 0:
                    dve.wait_ge(par_tr, 2)
                    for at, n, to in ((0, 96, 128), (96, 248, 256)):
                        link(dve, nc.vector.tensor_copy(pcol[:, to:to + n], ps[:, 7, at:at + n]))
                    k4 = keep.unsqueeze(1).broadcast_to([P, 4, P])
                    nc.vector.tensor_tensor(wsT[:], ps[:, 6].rearrange("p (g n) -> p g n", g=4), k4,
                                            ALU.mult).then_inc(par_ok, 1)
                if u == 4:
                    ada_keep(dve, ADA_IN[0])
                if u == 3:
                    dve.wait_ge(used, 4)
                    nc.vector.tensor_copy(kT[:].rearrange("p k n -> p (k n)"),
                                          pair(2).rearrange("p b n -> p (b n)")).then_inc(kT_kept, 1)
            ada_keep(dve, ADA_IN[1])

            def gelu(i, x, dst):
                dve.wait_ge(gelu_act, 2 * i + 1)
                link(dve, nc.vector.tensor_scalar(gt[:, 0], gt[:, 0], GELU_A, 1.0, ALU.mult, ALU.add))
                nc.vector.tensor_tensor(gt[:, 0], gt[:, 0], x, ALU.mult).then_inc(gelu_dve, 1)
                dve.wait_ge(gelu_act, 2 * i + 2)
                nc.vector.tensor_tensor(dst, gt[:, 1], x, ALU.mult).then_inc(gelu_dve, 1)

            gelu(0, ps[:, 1], gu[:].rearrange("p k n -> p (k n)"))
            dve_step(dve, 8)
            gelu(1, ps[:, 2], gv[:].rearrange("p t n -> p (t n)"))
            dve.wait_ge(gelu_dve, 4)
            dve.wait_ge(misc_in, 16 * N_MISC_DMAS)
            for tt in range(TT):
                link(dve, nc.vector.scalar_tensor_tensor(out=gt[:, 2, 0:SEQ], in0=gv[:, tt], scalar=1.0,
                                                         in1=gv[:, tt], op0=ALU.mult, op1=ALU.mult,
                                                         accum_out=stat[:, tt:tt + 1]))
            rsqrt(dve, N_Y, N_SS, N_V, N_A, SEQ)
            for tt in range(TT):
                link(dve, nc.vector.scalar_tensor_tensor(out=gv[:, tt], in0=gv[:, tt],
                                                         scalar=stat[:, 8 + tt:9 + tt], in1=gm_row[:],
                                                         op0=ALU.mult, op1=ALU.mult))
            dve_inc(vn_ok)

            def diagonals(t):
                return t.rearrange("p (b n) -> p b n", b=3)[:, 0:3:2, :]

            def log_not(h):
                z = ps[:, 4 + h % 2, 0:384]
                t1, t2, t3 = (sbt[:, h % 2, i] for i in range(3))
                dve.wait_ge(abs_done, h + 1)
                if h >= 2:
                    dve.wait_ge(av_done, h - 1)
                link(dve, nc.vector.tensor_scalar(t2, z, SCALE, 0.0, ALU.mult, ALU.max))
                dve.wait_ge(soft_done, h + 1)
                link(dve, nc.vector.scalar_tensor_tensor(out=t2, in0=t2, scalar=-1.0, in1=t1,
                                                         op0=ALU.mult, op1=ALU.subtract))
                m2 = m01.unsqueeze(1).broadcast_to([P, 2, P])
                n2 = neg.unsqueeze(1).broadcast_to([P, 2, P])
                link(dve, nc.vector.tensor_tensor(diagonals(t2), diagonals(t2), m2, ALU.mult))
                dve_inc(lnot_done)
                link(dve, nc.vector.scalar_tensor_tensor(out=t3, in0=z, scalar=SCALE, in1=t2,
                                                         op0=ALU.mult, op1=ALU.add))
                link(dve, nc.vector.tensor_tensor(diagonals(t3), diagonals(t3), n2, ALU.add))

            for s in range(12):
                dve_step(dve, U_GATE + s)
                if 1 <= s < SB_HEADS + 1:
                    h = s - 1
                    dve.wait_ge(sfx_done, h + 1)
                    t3 = sbt[:, h % 2, 2]
                    nc.vector.tensor_tensor(t3, t3, ps[:, 6, 0:384], ALU.add).then_inc(arg_done, 1)
                if s < SB_HEADS:
                    log_not(s)
                if s % 2 and s >= 3 and s < SB_HEADS + 2:
                    k = (s - 3) // 2
                    dve.wait_ge(o_hi, k + 1)
                    nc.vector.tensor_tensor(hidl[:, k], ps[:, 7, (k % 2) * SEQ:(k % 2 + 1) * SEQ],
                                            hidh[:, k].bitcast(F32), ALU.subtract).then_inc(o_lo, 1)
                if s == 9:
                    dve.wait_ge(mix_done, 2)
                    for i in range(2):
                        o = gt[:, 0, i * SEQ:(i + 1) * SEQ].rearrange("p (t n) -> p t n", t=TT)
                        m = ps[:, 6, i * SEQ:(i + 1) * SEQ].rearrange("p (t n) -> p t n", t=TT)
                        link(dve, nc.vector.tensor_tensor(o, m, bsp[:, i:i + 1].broadcast_to([P, TT, P]),
                                                          ALU.add))
                    nc.vector.tensor_tensor(gt[:, 0], gt[:, 0], gu[:].rearrange("p k n -> p (k n)"),
                                            ALU.mult).then_inc(o_val, 1)
            for k in range(2):
                dve.wait_ge(o_hi, 4 + k + 1)
                nc.vector.tensor_tensor(hidl[:, 6 + k], gt[:, 0, k * SEQ:(k + 1) * SEQ],
                                        hidh[:, 6 + k].bitcast(F32), ALU.subtract).then_inc(o_lo, 1)
            for k in range(2):
                dve.wait_ge(o_hi, 8)
                nc.vector.scalar_tensor_tensor(out=hidl[:, 4 + k], in0=ps[:, 5, k * SEQ:(k + 1) * SEQ],
                                               scalar=par("pool_scale", k), in1=hidh[:, 4 + k].bitcast(F32),
                                               op0=ALU.mult, op1=ALU.subtract).then_inc(o_lo, 1)
            for c in range(2):
                dve.wait_ge(used, U_BR + c + 1)
                dve.wait_ge(gate_sig, c + 1)
                link(dve, nc.vector.tensor_tensor(gate[:, c], gate[:, c], pair(2 * c), ALU.mult))
                dve_inc(br_done)
                dve_step(dve, U_BR + c)
            dve.wait_ge(used, U_BR + 3)
            dve.wait_ge(gate_sig, 6)
            for c in range(2):
                g = gate[:, 2 + c]
                nc.vector.tensor_tensor(g, g, pair(4 + 2 * c), ALU.mult).then_inc(product_ok, 1)
            dve.wait_ge(used, U_BR + 4)
            for c in range(2):
                g = gate[:, 4 + c]
                link(dve, nc.vector.tensor_tensor(g, g, pair(2 * c), ALU.mult))
                dve.wait_ge(two_merged, c + 1)
                nc.vector.tensor_tensor(gate[:, c], gate[:, c], g, ALU.add).then_inc(merged, 1)
            hT_dve(dve, 1, 1, None, None)
            for u in range(U_BR + 2, U_OUT):
                dve_step(dve, u)
            for u in range(U_OUT, U_OUT + 2):
                dve_step(dve, u)
            dve.wait_ge(row_a_in, 16)
            post_dve(dve, 0, U_OUT + 3, row_a)
            norm_dve(dve, 1)
            hT_dve(dve, 2, 2, lambda k: par("g_ff_pre", k), None)
            late_steps(dve, U_OUT + 3, ADA_HEAD[0])
            mlp_dve(dve, 0)
            dve.wait_ge(row_b_in, 16)

            def mod_scales(layer, vec):
                sc = (layer * 6 + vec + 1) * 8
                g = par("mix_g" if vec == 0 else "mlp_g", 8 * layer, 8)
                link(dve, nc.vector.scalar_tensor_tensor(out=modT[:, sc:sc + 8], in0=modT[:, sc:sc + 8],
                                                         scalar=1.0, in1=g, op0=ALU.add, op1=ALU.mult))
                dve_inc(mod_ok)

            def mod_hT(fill, b, layer, vec, last, chunk=None):
                hT_dve(dve, fill, b, lambda k: mod_scale(layer, vec, k),
                       lambda k: mod_shift(layer, vec, k), mod=fill - 3)
                late_steps(dve, last, chunk)

            mod_scales(0, 0)
            post_dve(dve, 1, U_MLP[0] + 31, row_b)
            norm_dve(dve, 2)
            mod_hT(3, 3, 0, 0, U_MLP[0] + 31)
            dve.wait_ge(tr_done, 16)
            link(dve, nc.vector.memset(u_pad[:, :, 0:PAD], 0.0))

            def glu(c):
                for i in range(2):
                    dve.wait_ge(glu_sig, 2 * c + i + 1)
                    nc.vector.scalar_tensor_tensor(
                        out=u_pad[:, 2 * c + i, PAD:], in0=ps[:, chunk_bank(c), i * SEQ:(i + 1) * SEQ],
                        scalar=par("conv_b_in", 2 * c + i), in1=csg[:, c % 2, i], op0=ALU.add,
                        op1=ALU.mult).then_inc(u_ok, 1)

            glu(0)
            taps = 0
            for n, tiles in enumerate(CONV_ROUNDS):
                dve.wait_ge(u_ok, tiles[-1] + 1)
                for t in range(TAPS):
                    for k in tiles:
                        odd = len(tiles) == 1 and t % 2
                        acc = cxc[:, k] if odd else cacc[:, k]
                        w, src = par("conv_dw", t * KT + k), u_pad[:, k, t:t + SEQ]
                        if t == 0:
                            ins = nc.vector.tensor_scalar(acc, src, w, par("conv_dw_b", k), ALU.mult,
                                                          ALU.add)
                        elif odd and t == 1:
                            ins = nc.vector.tensor_scalar(acc, src, w, None, ALU.mult)
                        else:
                            dve.wait_ge(conv_tap, taps - 1)
                            ins = nc.vector.scalar_tensor_tensor(out=acc, in0=src, scalar=w, in1=acc,
                                                                 op0=ALU.mult, op1=ALU.add)
                        ins.then_inc(conv_tap, 1)
                        taps += 1
                    if (n, t) in GLU_AFTER:
                        glu(GLU_AFTER[n, t])
            dve.wait_ge(conv_tap, taps)
            nc.vector.tensor_tensor(cacc[:, 4], cacc[:, 4], cxc[:, 4], ALU.add).then_inc(conv_tap, 1)
            dve.wait_ge(cs_sum, 1)
            link(dve, nc.vector.tensor_scalar(cmean[:], ps[:, 7, 0:SEQ], 1.0 / D, None, ALU.mult))
            for k in range(KT):
                nc.vector.tensor_tensor(cxc[:, k], cacc[:, k], cmean[:], ALU.subtract).then_inc(cs_xc, 1)
            dve.wait_ge(cs_sum, 2)
            rsqrt(dve, rstd_col(0, 0, TT), ps[:, 4, 0:TT], stat[:, 24:26], stat[:, 16:18], D)
            diagonals_dve(dve)
            dve.wait_ge(cs_rstd, 1)
            for k in range(KT + 2):
                if k < KT:
                    nc.vector.scalar_tensor_tensor(out=cxc[:, k], in0=cxc[:, k],
                                                   scalar=par("conv_ln_g", k), in1=ps[:, 5, 0:SEQ],
                                                   op0=ALU.mult, op1=ALU.mult).then_inc(cs_ln, 1)
                if 1 <= k <= KT:
                    conv_silu(dve, k - 1)
                if k >= 2:
                    conv_lo(dve, k - 2)
            for u in range(U_COUT, U_COUT + 2):
                dve_step(dve, u, turn=u == U_COUT)
            dve.wait_ge(pool_x, 1)
            dve.wait_ge(row_kept, 1)
            mod_scales(0, 3)
            gated_dve(dve, 2, U_COUT + 3, row_a)
            mod_hT(4, 5, 0, 3, U_COUT + 3, ADA_HEAD[1])
            mlp_dve(dve, 1)
            mod_scales(1, 0)
            dve.wait_ge(row_kept, 2)
            gated_dve(dve, 3, U_MLP[1] + 31, row_b)
            mod_hT(5, 6, 1, 0, U_MLP[1] + 31)
            for c in range(6):
                if 1 <= c < 5:
                    ada_keep(dve, ADA_QKV[c - 1])
                dve_step(dve, U_QKV + 2 * c, turn=c > 0)
                if c < 4:
                    for h in range(2):
                        ada_unit(dve, ADA_QKV[c][0], h)
                if c < 4:
                    dve.wait_ge(qk_sq, c + 1)
                    nc.vector.tensor_reduce(stat[:, 64 + 16 * c:80 + 16 * c].rearrange("p (t h) -> p t h", t=TT),
                                            qsq[:].rearrange("p t (h d) -> p t h d", d=HD), AX.X,
                                            ALU.add).then_inc(qk_ss, 1)
                if c in (1, 3):
                    dve.wait_ge(qk_ss, c + 1)
                    dve.wait_ge(qk_kept, c + 1)
                    at = 32 * (c // 2)
                    cut = [slice(base + at, base + at + 32) for base in (128, 64, 256, 192)]
                    rsqrt(dve, *(stat[:, q] for q in cut), HD)
                    src = (Qs, Ks)[c // 2]
                    for cc in range(2):
                        for tt in range(TT):
                            v = src[:, tt, cc * 512:(cc + 1) * 512].rearrange("p (h d) -> p h d", d=HD)
                            m = 128 + at + 16 * cc + 8 * tt
                            y = stat[:, m:m + 8].unsqueeze(2).broadcast_to([P, 8, HD])
                            link(dve, nc.vector.tensor_tensor(v, v, y, ALU.mult))
                    dve_inc(qk_n)
            for s in range(PAIRS + 4):
                if s < PAIRS:
                    if s >= 3:
                        dve.wait_ge(s_tr, s - 2)
                    for i in range(2):
                        dve.wait_ge(s_z, 2 * s + i + 1)
                        slope = float(np.float32(2.0 ** (-8.0 * (2 * s + i + 1) / AT_HEADS))) / SCALE
                        nc.vector.scalar_tensor_tensor(out=aS[:, s % 3, i], in0=dist, scalar=slope,
                                                       in1=ps[:, 4 + 2 * (s % 2) + i, 0:384],
                                                       op0=ALU.mult, op1=ALU.add).then_inc(s_arg, 1)
                    dve.wait_ge(s_arg, 2 * s + 2)
                    for j, c in enumerate(query_tiles):
                        ins = nc.vector.tensor_reduce(s_col(s, 2 * j, 2), aS[:, s % 3, :, c], AX.X, ALU.max)
                        link(dve, ins)
                    nc.vector.tensor_scalar(s_col(s, 4, 4), s_col(s, 0, 4), -SCALE, None,
                                            ALU.mult).then_inc(s_max, 1)
                if 1 <= s < PAIRS + 1:
                    k = s - 1
                    dve.wait_ge(s_exp, 4 * k + 4)
                    link(dve, nc.vector.reciprocal(s_col(k, 12, 4), s_col(k, 8, 4)))
                    for j, c in enumerate(query_tiles):
                        a = aS[:, k % 3, :, c]
                        y = s_col(k, 12 + 2 * j, 2).unsqueeze(2).broadcast_to([P, 2, c.stop - c.start])
                        ins = nc.vector.tensor_tensor(a, a, y, ALU.mult)
                        ins.then_inc(s_p, 1)
                if s >= 4:
                    k = s - 4
                    dve.wait_ge(hT_hi, 56 + k + 1)
                    nc.vector.tensor_tensor(hTl[:, k], ps[:, k % 2, 0:SEQ], hTh[:, k].bitcast(F32),
                                            ALU.subtract).then_inc(hT_lo, 1)
            for u in range(U_WO, U_WO + 2):
                dve_step(dve, u, turn=u == U_WO)
            mod_scales(1, 3)
            dve.wait_ge(row_kept, 3)
            gated_dve(dve, 4, U_WO + 3, row_a)
            mod_hT(6, 8, 1, 3, U_WO + 3, ADA_HEAD[2])
            mlp_dve(dve, 2)
            dve.wait_ge(row_kept, 4)
            gated_dve(dve, 5, U_MLP[2] + 31, row_b, norm=False)

        @block.gpsimd
        def _(pool):
            nc.gpsimd.memset(zero_r[:].bitcast(F32), 0.0)
            nc.gpsimd.memset(pp[:, :, 0:16], 0.0)
            link_pool(pool, nc.gpsimd.memset(wpd[:], 0.0))
            nc.gpsimd.sem_inc(pad_ok, 1)
            pool.wait_ge(p_kept, 1)
            pool.wait_ge(misc_in, 16 * N_MISC_DMAS)
            pool.wait_ge(ada_kept, 2 + 1)
            src = pp
            for g, w in enumerate(WINDOWS):
                dst, at = (pa, pb)[g % 2], w - 1
                link_pool(pool, nc.gpsimd.tensor_tensor(dst[:, :, at:], src[:, :, at:],
                                                        src[:, :, at - w // 2:16 + SEQ - w // 2], ALU.add))
                r = slice(HD * (g % 2), HD * (g % 2) + HD)
                link_pool(pool, nc.gpsimd.tensor_tensor(pool_mean[r, g // 2], dst[r, g // 2, 16:],
                                                        inv[r, g // 2], ALU.mult))
                src = dst
            nc.gpsimd.tensor_tensor(pp[:, :, 16:], pool_mean[:], pp[:, :, 16:],
                                    ALU.subtract).then_inc(pool_in, 1)
            for c in range(2):
                pool.wait_ge(product_ok, c + 1)
                nc.gpsimd.tensor_tensor(gate[:, c], gate[:, c], gate[:, 2 + c], ALU.add).then_inc(two_merged, 1)
            pool.wait_ge(o_lo, 8)
            pool.dma_start(row_a[:], row(g_mix_post[0])).then_inc(row_a_in, 16)
            pool.dma_start(row_b[:], row(g_ff_post[0])).then_inc(row_b_in, 16)
            pool.dma_start(row_c[:], row(conv_b_out_2[0])).then_inc(row_c_in, 16)
            mlp_pool(pool, 0)
            for u in range(U_CIN, U_CIN + 8):
                pool_step(pool, u)
            pool.wait_ge(row_kept, 1)
            pool.wait_ge(row_c_in, 16)
            pool.wait_ge(tr_done, 16)
            link_pool(pool, nc.gpsimd.tensor_tensor(row_c[:], row_c[:], row_a[:], ALU.mult))
            for tt in range(TT):
                link_pool(pool, nc.gpsimd.tensor_tensor(X[:, tt], X[:, tt], row_c[:], ALU.add))
            nc.gpsimd.sem_inc(pool_x, 1)
            mlp_pool(pool, 1)
            for c in range(6):
                pool_step(pool, U_QKV + 2 * c + 1)
            mlp_pool(pool, 2)


_INS = ["x", "w_in", "w_pool", "pool_scale", "gm_gain", "w_spatial", "b_spatial", "w_br_sb", "w_br_pool",
        "w_br_gm", "w_out", "g_mix_pre", "g_mix_post", "g_ff_pre", "g_ff_post", "w_ff_in", "w_ff_out",
        "c_2", "ada_w_2", "ada_b_2", "mix_norm_g_2", "mlp_norm_g_2", "conv_w_in_2", "conv_b_in_2",
        "conv_dw_2", "conv_dw_b_2", "conv_ln_g_2", "conv_ln_b_2", "conv_w_out_2", "conv_b_out_2",
        "attn_w_qkv_2", "attn_q_norm_g_2", "attn_k_norm_g_2", "attn_w_o_2", "mlp_w1_2", "mlp_w2_2"]


def kernel(**inputs):
    import concourse.bacc as bacc
    from concourse.bass_utils import run_bass_kernel_spmd

    nc = bacc.Bacc("TRN2", target_bir_lowering=False, num_devices=1)
    arrays, args = {}, []
    shapes = shape_constants()
    for name in _INS + ["consts", "inv_count"]:
        a = shapes[name == "inv_count"] if name in ("consts", "inv_count") else inputs[name]
        a = np.ascontiguousarray(a)
        arrays[f"in_{name}"] = a
        args.append(nc.dram_tensor(f"in_{name}", a.shape, mybir.dt.from_np(a.dtype),
                                   kind="ExternalInput").ap())
    args.append(nc.dram_tensor("out_x", (1, SEQ, D), F32, kind="ExternalOutput").ap())
    build_kernel(nc, *args)
    r = run_bass_kernel_spmd(nc, [arrays], core_ids=[0])
    return r.results[0]["out_x"]
```
